# Optimizing a Trainium2 kernel written in Bass

```python
import jax, jax.numpy as jnp
from jax import lax
import numpy as np

D_MODEL = 1024
BATCH = 1
SEQ = 2048
DEPTH = 2

D_MIX = D_MODEL
DN_HEADS = 4
DN_HEAD_K = 128
DN_HEAD_V = 128
DN_QK = DN_HEADS * DN_HEAD_K
DN_V = DN_HEADS * DN_HEAD_V
DN_CONV_DIM = 2 * DN_QK + DN_V
CONV_K = 5
DN_CHUNK = 64
N_DIR = 2
ATT_HEADS = 8
ATT_KV_HEADS = 2
ATT_HEAD_DIM = 64
ATT_Q = ATT_HEADS * ATT_HEAD_DIM
ATT_KV = ATT_KV_HEADS * ATT_HEAD_DIM
Q_BLOCK = 128
ROPE_THETA = 10000.0
GRID_W = 64
EPS = 1e-6
IN_SIZES = (DN_CONV_DIM, DN_V, N_DIR * DN_HEADS, N_DIR * DN_HEADS, ATT_Q, ATT_KV, ATT_KV, ATT_Q)
IN_COLS = sum(IN_SIZES)

kernel_name = "hybrid_deltanet_gqa_axial_encoder"

def _rmsnorm(x, w):
    x32 = x.astype(jnp.float32)
    y = x32 * lax.rsqrt(jnp.mean(x32 * x32, axis=-1, keepdims=True) + EPS)
    return (y * w.astype(jnp.float32)).astype(x.dtype)

def _l2norm(x):
    return x * lax.rsqrt(jnp.sum(x * x, axis=-1, keepdims=True) + EPS)

def _gated_delta_rule(q, k, v, g, beta):
    B, T, H, Dk = q.shape
    Dv = v.shape[-1]
    C = DN_CHUNK
    N = T // C

    def chunk(t):
        return jnp.moveaxis(t.reshape(B, N, C, H, t.shape[-1]), 3, 2)

    qc, kc, vc = chunk(q), chunk(k), chunk(v)
    gc = jnp.cumsum(jnp.moveaxis(g.reshape(B, N, C, H), 3, 2), axis=-1)
    bc = jnp.moveaxis(beta.reshape(B, N, C, H), 3, 2)[..., None]
    incl = jnp.tril(jnp.ones((C, C), dtype=bool))
    strict = jnp.tril(jnp.ones((C, C), dtype=bool), -1)
    decay = jnp.exp(jnp.where(incl, gc[..., :, None] - gc[..., None, :], -jnp.inf))
    k_beta = kc * bc
    lower = jnp.where(strict, jnp.einsum('bnhid,bnhjd->bnhij', k_beta, kc) * decay, 0.0)
    a_mat = lower + jnp.eye(C, dtype=lower.dtype)
    rhs = jnp.concatenate([vc * bc, k_beta * jnp.exp(gc)[..., None]], axis=-1)
    sol = lax.linalg.triangular_solve(a_mat, rhs, left_side=True, lower=True, unit_diagonal=True)
    u, w = sol[..., :Dv], sol[..., Dv:]
    attn = jnp.einsum('bnhid,bnhjd->bnhij', qc, kc) * decay

    def step(state, inp):
        q_i, k_i, u_i, w_i, g_i, a_i = inp
        v_new = u_i - jnp.einsum('bhcd,bhde->bhce', w_i, state)
        o_i = (jnp.einsum('bhcd,bhde->bhce', q_i * jnp.exp(g_i)[..., None], state)
               + jnp.einsum('bhij,bhje->bhie', a_i, v_new))
        g_last = g_i[..., -1:]
        k_dec = k_i * jnp.exp(g_last - g_i)[..., None]
        state = state * jnp.exp(g_last)[..., None] + jnp.einsum('bhcd,bhce->bhde', k_dec, v_new)
        return state, o_i

    xs = tuple(jnp.moveaxis(t, 1, 0) for t in (qc, kc, u, w, gc, attn))
    s0 = jnp.zeros((B, H, Dk, Dv), dtype=q.dtype)
    _, o = lax.scan(step, s0, xs)
    return o.transpose(1, 0, 3, 2, 4).reshape(B, T, H, Dv)

def _bidir_delta(q, k, v, g, beta):
    def flip(t):
        return jnp.flip(t, axis=1)
    fwd = _gated_delta_rule(q, k, v, g[:, :, 0], beta[:, :, 0])
    bwd = flip(_gated_delta_rule(flip(q), flip(k), flip(v), flip(g[:, :, 1]), flip(beta[:, :, 1])))
    return fwd + bwd

def _deltanet_branch(qkv, z, b, a, conv_w, a_log, dt_bias, norm_w):
    Bsz, T, _ = qkv.shape
    pad = CONV_K // 2
    qkv = jax.nn.silu(lax.conv_general_dilated(
        qkv, conv_w[:, None, :], window_strides=(1,), padding=[(pad, pad)],
        dimension_numbers=('NWC', 'WIO', 'NWC'), feature_group_count=DN_CONV_DIM))
    qkv32 = qkv.astype(jnp.float32)
    q = qkv32[..., :DN_QK].reshape(Bsz, T, DN_HEADS, DN_HEAD_K)
    k = qkv32[..., DN_QK:2 * DN_QK].reshape(Bsz, T, DN_HEADS, DN_HEAD_K)
    v = qkv32[..., 2 * DN_QK:].reshape(Bsz, T, DN_HEADS, DN_HEAD_V)
    q = _l2norm(q) * (DN_HEAD_K ** -0.5)
    k = _l2norm(k)
    beta = jax.nn.sigmoid(b.astype(jnp.float32)).reshape(Bsz, T, N_DIR, DN_HEADS)
    g = -jnp.exp(a_log.astype(jnp.float32)) * jax.nn.softplus(
        a.astype(jnp.float32).reshape(Bsz, T, N_DIR, DN_HEADS) + dt_bias.astype(jnp.float32))
    o = _bidir_delta(q, k, v, g, beta)
    o = _rmsnorm(o, norm_w).reshape(Bsz, T, DN_V)
    return (o * jax.nn.silu(z.astype(jnp.float32))).astype(z.dtype)

def _rope(x, pos):
    d = x.shape[-1]
    inv = ROPE_THETA ** (-jnp.arange(0, d, 2, dtype=jnp.float32) / d)
    ang = pos[:, None] * inv[None, :]
    cos = jnp.concatenate([jnp.cos(ang), jnp.cos(ang)], axis=-1)[:, None, :]
    sin = jnp.concatenate([jnp.sin(ang), jnp.sin(ang)], axis=-1)[:, None, :]
    x32 = x.astype(jnp.float32)
    rot = jnp.concatenate([-x32[..., d // 2:], x32[..., :d // 2]], axis=-1)
    return (x32 * cos + rot * sin).astype(x.dtype)

def _axial_rope(x, row, col):
    h = x.shape[-1] // 2
    return jnp.concatenate([_rope(x[..., :h], row), _rope(x[..., h:], col)], axis=-1)

def _block_attention(q, k, v):
    B, T, Hq, Dh = q.shape
    Hkv = k.shape[2]
    G = Hq // Hkv
    NB = T // Q_BLOCK
    qb = jnp.moveaxis(q.reshape(B, NB, Q_BLOCK, Hkv, G, Dh), 1, 0)
    scale = Dh ** -0.5

    def one_block(q_blk):
        s = jnp.einsum('bqkgd,bskd->bkgqs', q_blk, k).astype(jnp.float32) * scale
        p = jax.nn.softmax(s, axis=-1).astype(v.dtype)
        return jnp.einsum('bkgqs,bskd->bqkgd', p, v)

    o = lax.map(one_block, qb)
    return jnp.moveaxis(o, 0, 1).reshape(B, T, Hq * Dh)

def _attention_branch(q, k, v, z, q_norm_w, k_norm_w, row, col):
    Bsz, T, _ = q.shape
    q = q.reshape(Bsz, T, ATT_HEADS, ATT_HEAD_DIM)
    k = k.reshape(Bsz, T, ATT_KV_HEADS, ATT_HEAD_DIM)
    v = v.reshape(Bsz, T, ATT_KV_HEADS, ATT_HEAD_DIM)
    q = _axial_rope(_rmsnorm(q, q_norm_w), row, col)
    k = _axial_rope(_rmsnorm(k, k_norm_w), row, col)
    o = _block_attention(q, k, v)
    return (o.astype(jnp.float32) * jax.nn.silu(z.astype(jnp.float32))).astype(z.dtype)

def setup_inputs(seed: int = 0) -> dict:
    key = jax.random.key(seed)
    ks = jax.random.split(key, 12)
    f32 = jnp.float32
    x = jax.random.normal(ks[0], (BATCH, SEQ, D_MODEL), f32)
    norm_w = 1.0 + 0.02 * jax.random.normal(ks[1], (DEPTH, D_MODEL), f32)
    w_in = jax.random.normal(ks[2], (DEPTH, D_MODEL, IN_COLS), f32) * D_MODEL ** -0.5
    conv_w = jax.random.normal(ks[3], (DEPTH, CONV_K, DN_CONV_DIM), f32) * CONV_K ** -0.5
    a_log = jnp.log(jax.random.uniform(ks[4], (DEPTH, N_DIR, DN_HEADS), f32, 1.0, 16.0))
    dt = jnp.exp(jax.random.uniform(ks[5], (DEPTH, N_DIR, DN_HEADS), f32, np.log(1e-3), np.log(1e-1)))
    dt_bias = dt + jnp.log(-jnp.expm1(-dt))
    dn_norm_w = 1.0 + 0.02 * jax.random.normal(ks[6], (DEPTH, DN_HEAD_V), f32)
    q_norm_w = 1.0 + 0.02 * jax.random.normal(ks[7], (DEPTH, ATT_HEAD_DIM), f32)
    k_norm_w = 1.0 + 0.02 * jax.random.normal(ks[8], (DEPTH, ATT_HEAD_DIM), f32)
    w_out = jax.random.normal(ks[9], (DEPTH, D_MIX, D_MODEL), f32) * D_MIX ** -0.5
    final_norm_w = 1.0 + 0.02 * jax.random.normal(ks[10], (D_MODEL,), f32)
    return {"x": x, "norm_w": norm_w, "w_in": w_in, "conv_w": conv_w, "a_log": a_log,
            "dt_bias": dt_bias, "dn_norm_w": dn_norm_w, "q_norm_w": q_norm_w, "k_norm_w": k_norm_w,
            "w_out": w_out, "final_norm_w": final_norm_w}

def reference(x, norm_w, w_in, conv_w, a_log, dt_bias, dn_norm_w, q_norm_w, k_norm_w, w_out, final_norm_w):
    T = x.shape[1]
    rows = T // GRID_W
    row = jnp.repeat(jnp.arange(rows, dtype=jnp.float32), GRID_W)
    col = jnp.tile(jnp.arange(GRID_W, dtype=jnp.float32), rows)
    splits = np.cumsum(IN_SIZES)[:-1].tolist()
    for l in range(DEPTH):
        h = _rmsnorm(x, norm_w[l])
        proj = jnp.einsum('btd,dc->btc', h, w_in[l])
        dn_qkv, dn_z, dn_b, dn_a, at_q, at_k, at_v, at_z = jnp.split(proj, splits, axis=-1)
        y_dn = _deltanet_branch(dn_qkv, dn_z, dn_b, dn_a, conv_w[l], a_log[l], dt_bias[l], dn_norm_w[l])
        y_at = _attention_branch(at_q, at_k, at_v, at_z, q_norm_w[l], k_norm_w[l], row, col)
        y = jnp.concatenate([y_dn, y_at], axis=-1)
        x = x + jnp.einsum('btc,cd->btd', y, w_out[l])
    return _rmsnorm(x, final_norm_w)


_drawn_inputs = setup_inputs


def setup_inputs(seed=0):
    import zlib

    import numpy as np

    out = dict(_drawn_inputs(seed))
    spreads = {}
    factors = {'norm_w': 3.069,
     'dn_norm_w': 4.839,
     'q_norm_w': 8.0,
     'k_norm_w': 8.0,
     'final_norm_w': 2.918}
    for name, (base, spread) in spreads.items():
        noise = np.random.default_rng([zlib.crc32(name.encode()), seed]).standard_normal(out[name].shape)
        drawn = base * np.exp(spread * noise) if base else spread * noise
        out[name] = __import__('jax').numpy.asarray(drawn.astype(out[name].dtype))
    for name, factor in factors.items():
        out[name] = (out[name] * factor).astype(out[name].dtype)
    return out
```

```python
from contextlib import ExitStack, contextmanager

import numpy as np

import concourse.bass as bass
from concourse import mybir

P = 128
F32 = mybir.dt.float32
F32R = mybir.dt.float32r
ALU = mybir.AluOpType
ACT = mybir.ActivationFunctionType
AX = mybir.AxisListType

SEQ = 2048
D_MODEL = 1024
DEPTH = 2
KT = D_MODEL // P
NC = SEQ // P
QB = 512
NQ = SEQ // QB
HALF = SEQ // 2
CONV_K = 5
PADW = SEQ + CONV_K - 1
EPS = 1e-6

DN_HEADS = 4
N_DIR = 2
ITEMS = N_DIR * DN_HEADS
ATT_HEADS = 8
KV_HEADS = 2
GROUP = ATT_HEADS // KV_HEADS
DH = 64
SCALE = float(DH) ** -0.5
LEVELS = 7

CONV_TILES = 3 * DN_HEADS
T_V, T_Q, T_K = 0, DN_HEADS, 2 * DN_HEADS
T_AQ = CONV_TILES
T_AK = T_AQ + ATT_HEADS // 2
T_AV = T_AK + 1
T_Z = T_AV + 1
N_TILES = T_Z + 8
WCOLS = KT * P + 8
W_BA = 2 * ITEMS


@contextmanager
def semaphores(nc, names):
    with ExitStack() as stack:
        sems = {n: stack.enter_context(nc.semaphore(n)) for n in names.split()}
        yield sems
        for s in sems.values():
            nc.sync.sem_clear(s)
        nc.all_engine_barrier()


class Buffers:

    def __init__(self, nc, stack, phase):
        self.nc, self.stack, self.phase = nc, stack, phase

    def sbuf(self, name, shape, dtype=F32):
        return self.stack.enter_context(self.nc.sbuf_tensor(f"{self.phase}_sb_{name}", shape, dtype))

    def banks(self):
        return self.stack.enter_context(self.nc.psum_tensor(f"{self.phase}_banks", [P, 8, QB], F32))


def wait_in_loop(sp, s, name, value):
    sp.wait_ge(s[name], value)
    sp.sem_inc(s["passed"], 1)


def load_input(nc, a, c):
    with ExitStack() as stack, semaphores(nc, "x_loaded0 x_loaded1 x_stored0 x_stored1 squared summed passed") as s:
        b = Buffers(nc, stack, "load")
        x = b.sbuf("x", [P, 2, SEQ])
        sq = b.sbuf("sq", [P, 2, SEQ])
        acc = c.sq_acc
        with nc.Block() as block:

            @block.sync
            def _(sp):
                with sp.Fori(0, KT // 2) as i:
                    for u in range(2):
                        wait_in_loop(sp, s, "squared", 2 * i)
                        wait_in_loop(sp, s, f"x_stored{u}", 16 * i)
                        sp.dma_start(x[:, u, :], a.x_in[i * 2 + u]).then_inc(s[f"x_loaded{u}"], 16)
                    for u in range(2):
                        wait_in_loop(sp, s, f"x_loaded{u}", 16 * i + 16)
                        sp.dma_start(a.x_res[i * 2 + u], x[:, u, :]).then_inc(s[f"x_stored{u}"], 16)
                for u in range(2):
                    sp.wait_ge(s[f"x_stored{u}"], KT // 2 * 16)

            @block.scalar
            def _(act):
                with act.Fori(0, KT // 2) as i:
                    for u in range(2):
                        act.wait_ge(s[f"x_loaded{u}"], 16 * i + 16)
                        act.wait_ge(s["summed"], 2 * i + u)
                        nc.scalar.activation(sq[:, u, :], x[:, u, :], ACT.Square).then_inc(s["squared"], 1)

            @block.vector
            def _(dve):
                nc.vector.memset(acc[:], 0.0).then_inc(s["summed"], 1)
                with dve.Fori(0, KT // 2) as i:
                    for u in range(2):
                        dve.wait_ge(s["squared"], 2 * i + u + 1)
                        dve.wait_ge(s["summed"], 2 * i + u + 1)
                        nc.vector.tensor_tensor(acc[:], acc[:], sq[:, u, :], ALU.add).then_inc(s["summed"], 1)


def token_scales(nc, a, c, when):
    with ExitStack() as stack, semaphores(nc, "sums root scale turned copied stored") as s:
        b = Buffers(nc, stack, "scales_" + when)
        table = b.sbuf("table", [P, NC])
        inv = b.sbuf("inv", [P, NC])
        rows = b.sbuf("rows", [NC, P])
        ps = b.banks()
        with nc.Block() as block:

            @block.tensor
            def _(pe):
                for t in range(NC):
                    mm = nc.tensor.matmul(ps[:, 0, t:t + 1], c.sq_acc[:, t * P:(t + 1) * P], c.ones[:, 0:1],
                                          start=True, stop=True)
                mm.then_inc(s["sums"], 1)
                pe.wait_ge(s["scale"], 1)
                nc.tensor.transpose(ps[0:NC, 1, 0:P], inv[:], c.ident[:]).then_inc(s["turned"], 1)

            @block.scalar
            def _(act):
                act.wait_ge(s["sums"], 1)
                nc.scalar.activation(table[:], ps[:, 0, 0:NC], ACT.Sqrt, bias=c.eps[:, 0:1],
                                     scale=1.0 / D_MODEL).then_inc(s["root"], 1)

            @block.vector
            def _(dve):
                dve.wait_ge(s["root"], 1)
                nc.vector.reciprocal(inv[:], table[:]).then_inc(s["scale"], 1)
                dve.wait_ge(s["turned"], 1)
                nc.vector.tensor_copy(rows[:], ps[0:NC, 1, 0:P]).then_inc(s["copied"], 1)

            @block.sync
            def _(sp):
                sp.wait_ge(s["copied"], 1)
                sp.dma_start(a.x_scale.rearrange("(c p) -> c p", p=P), rows[:]).then_inc(s["stored"], 16)
                sp.wait_ge(s["stored"], 16)


def input_projection(nc, a, c, l):
    names = ("x_loaded0 x_loaded1 scale_loaded small_loaded normed h_hi h_lo w_loaded0 w_loaded1 w_hi w_lo "
             "proj_done psum_free passed "
             "conv_step taps_kept conv_done out_ready out_stored0 out_stored1 ba_hi ba_split ba_stored edges "
             "squared stats_done")
    with ExitStack() as stack, semaphores(nc, names) as s:
        b = Buffers(nc, stack, "proj")
        h_hi = b.sbuf("h_hi", [P, KT, SEQ], F32R)
        h_lo = b.sbuf("h_lo", [P, KT, SEQ], F32R)
        pad = b.sbuf("pad", [P, 2, PADW])
        out = b.sbuf("out", [P, 2, SEQ])
        w_raw = b.sbuf("w_raw", [P, 2, WCOLS])
        w_hi = b.sbuf("w_hi", [P, 2, KT, P], F32R)
        w_lo = b.sbuf("w_lo", [P, 2, KT, P], F32R)
        nw = b.sbuf("nw", [P, KT])
        sq = b.sbuf("sq", [P, SEQ])
        taps = b.sbuf("taps", [P, 2, WCOLS - KT * P])
        ba_raw = b.sbuf("ba_raw", [P, KT, W_BA])
        ba_w = b.sbuf("ba_w", [P, KT, 2 * W_BA], F32R)
        ps = b.banks()
        scale = out[:, 1, :]

        with nc.Block() as block:

            @block.sync
            def _(sp):
                sp.dma_start(nw[:], a.norm_w[l]).then_inc(s["small_loaded"], 16)
                sp.dma_start(ba_raw[:], a.w_ba[l]).then_inc(s["small_loaded"], 16)
                sp.dma_start(scale, a.x_scale.partition_broadcast(P)).then_inc(s["scale_loaded"], 16)
                for k in range(KT):
                    if k >= 2:
                        sp.wait_ge(s["h_lo"], k - 1)
                    sp.dma_start(pad[:, k % 2, 0:SEQ], a.x_res[k]).then_inc(s[f"x_loaded{k % 2}"], 16)
                for u in range(2):
                    sp.dma_start(w_raw[:, u, :], a.w_in[l, u]).then_inc(s[f"w_loaded{u}"], 16)
                sp.wait_ge(s["out_ready"], 1)
                sp.dma_start(a.ba, out[0:2 * W_BA, 0, :]).then_inc(s["ba_stored"], 16)
                sp.wait_ge(s["ba_stored"], 16)
                for u in range(2):
                    sp.sem_inc(s[f"out_stored{u}"], 16)
                with sp.Fori(0, N_TILES // 2 - 1) as i:
                    for u in range(2):
                        t = i * 2 + u
                        wait_in_loop(sp, s, "w_lo", t + 1)
                        sp.dma_start(w_raw[:, u, :], a.w_in[l, t + 2]).then_inc(s[f"w_loaded{u}"], 16)
                        wait_in_loop(sp, s, "out_ready", t + 2)
                        sp.dma_start(a.proj[t], out[:, u, :]).then_inc(s[f"out_stored{u}"], 16)
                for u in range(2):
                    t = N_TILES - 2 + u
                    sp.wait_ge(s["out_ready"], t + 2)
                    sp.dma_start(a.proj[t], out[:, u, :]).then_inc(s[f"out_stored{u}"], 16)
                for u in range(2):
                    sp.wait_ge(s[f"out_stored{u}"], 16 * (N_TILES // 2 + 1))

            @block.tensor
            def _(pe):
                pe.wait_ge(s["ba_split"], 2)
                pe.wait_ge(s["h_lo"], KT)
                for n in range(NQ):
                    for k in range(KT):
                        for part, h in enumerate((h_hi, h_lo)):
                            mm = nc.tensor.matmul(ps[0:2 * W_BA, 4 + n, :], ba_w[:, k, :],
                                                  h[:, k, n * QB:(n + 1) * QB],
                                                  start=(k == 0 and part == 0), stop=(k == KT - 1 and part == 1))
                mm.then_inc(s["proj_done"], 2)

                def tile_half(i, u, half):
                    t = i * 2 + u
                    pe.wait_ge(s["w_hi"], t + 1)
                    pe.wait_ge(s["w_lo"], t + 1)
                    pe.wait_ge(s["psum_free"], 2 * t + half + 1)
                    for k in range(KT):
                        for w, h in ((w_hi, h_hi), (w_hi, h_lo), (w_lo, h_hi)):
                            for n in range(2):
                                at = half * HALF + n * QB
                                mm = nc.tensor.matmul(
                                    ps[:, 2 * half + n, :], w[:, u, k, :], h[:, k, at:at + QB],
                                    start=(k == 0 and w is w_hi and h is h_hi), stop=(k == KT - 1 and w is w_lo))
                    mm.then_inc(s["proj_done"], 1)

                def square_sums(i, u):
                    t = i * 2 + u
                    pe.wait_ge(s["squared"], t + 3)
                    for n in range(NC):
                        col = (t - T_Q) * 2 * NC + 2 * n
                        mm = nc.tensor.matmul(ps[:, 4, bass.ds(col, 2)], sq[:, n * P:(n + 1) * P], c.halves[:],
                                              start=True, stop=True)
                    mm.then_inc(s["stats_done"], 1)

                with pe.Fori(0, T_Q // 2 + 1) as i:
                    for u in range(2):
                        for half in range(2):
                            tile_half(i, u, half)
                pe.wait_ge(s["out_ready"], 1)
                with pe.Fori(T_Q // 2 + 1, T_Z // 2 + 1) as i:
                    for u in range(2):
                        tile_half(i, u, 0)
                        square_sums(i - 1, u)
                        tile_half(i, u, 1)
                with pe.Fori(T_Z // 2 + 1, N_TILES // 2) as i:
                    for u in range(2):
                        for half in range(2):
                            tile_half(i, u, half)

            @block.gpsimd
            def _(pool):
                pool.sem_inc(s["squared"], T_Q + 2)
                with pool.Fori(T_Q // 2, T_Z // 2) as i:
                    for u in range(2):
                        t = i * 2 + u
                        pool.wait_ge(s["out_ready"], t + 2)
                        pool.wait_ge(s["stats_done"], t - T_Q)
                        nc.gpsimd.tensor_tensor(sq[:], out[:, u, :], out[:, u, :], ALU.mult).then_inc(s["squared"], 1)

            @block.scalar
            def _(act):
                act.wait_ge(s["small_loaded"], 32)
                nc.scalar.copy(ba_w[:, :, 0:W_BA], ba_raw[:]).then_inc(s["ba_hi"], 1)
                for k in range(KT):
                    act.wait_ge(s["normed"], k + 1)
                    nc.scalar.copy(h_hi[:, k, :], pad[:, k % 2, 0:SEQ]).then_inc(s["h_hi"], 1)

                def split_hi(t, i, u):
                    act.wait_ge(s[f"w_loaded{u}"], 16 * i + 16)
                    act.wait_ge(s["proj_done"], 2 * t)
                    nc.scalar.copy(w_hi[:, u].rearrange("p k m -> p (k m)"), w_raw[:, u, 0:KT * P]).then_inc(s["w_hi"], 1)

                def evacuate(t, u, half, dst, func):
                    act.wait_ge(s["proj_done"], 2 * t + half + 3)
                    src = ps[:, 2 * half:2 * half + 2, :].rearrange("p b n -> p (b n)")
                    return nc.scalar.activation(dst, src, func)

                split_hi(0, 0, 0)
                act.wait_ge(s["proj_done"], 2)
                nc.scalar.copy(out[0:2 * W_BA, 0, :], ps[0:2 * W_BA, 4:8, :].rearrange("p b n -> p (b n)")) \
                    .then_inc(s["out_ready"], 1)
                act.wait_ge(s["out_ready"], 1)
                act.sem_inc(s["psum_free"], 2)
                with act.Fori(0, CONV_TILES // 2) as i:
                    for u in range(2):
                        t = i * 2 + u
                        split_hi(t + 1, i + u, 1 - u)
                        for half in range(2):
                            lo = CONV_K // 2 + half * HALF
                            act.wait_ge(s["conv_done"], t + 1)
                            evacuate(t, u, half, pad[:, u, lo:lo + HALF], ACT.Copy).then_inc(s["psum_free"], 1)
                        act.wait_ge(s["conv_done"], t + 3)
                        nc.scalar.activation(out[:, u, :], out[:, u, :], ACT.Silu).then_inc(s["out_ready"], 1)

                def plain(i, u, func, more, squares=False):
                    t = i * 2 + u
                    if more:
                        split_hi(t + 1, i + u, 1 - u)
                    act.wait_ge(s[f"out_stored{u}"], 16 * i + 16)
                    if squares:
                        act.wait_ge(s["squared"], t + 1)
                    for half in range(2):
                        e = evacuate(t, u, half, out[:, u, half * HALF:(half + 1) * HALF], func)
                        e.then_inc(s["psum_free"], 1)
                    act.wait_ge(s["psum_free"], 2 * t + 4)
                    act.sem_inc(s["out_ready"], 1)

                with act.Fori(T_AQ // 2, T_Z // 2) as i:
                    for u in range(2):
                        plain(i, u, ACT.Copy, True, True)
                for u in range(2):
                    plain(T_Z // 2, u, ACT.Silu, True, True)
                with act.Fori(T_Z // 2 + 1, N_TILES // 2 - 1) as i:
                    for u in range(2):
                        plain(i, u, ACT.Silu, True)
                plain(N_TILES // 2 - 1, 0, ACT.Silu, True)
                plain(N_TILES // 2 - 1, 1, ACT.Silu, False)

            @block.vector
            def _(dve):
                dve.wait_ge(s["scale_loaded"], 16)
                dve.wait_ge(s["small_loaded"], 32)

                def split_h(k):
                    dve.wait_ge(s["h_hi"], k + 1)
                    nc.vector.tensor_tensor(h_lo[:, k, :], pad[:, k % 2, 0:SEQ], h_hi[:, k, :].bitcast(F32),
                                            ALU.subtract).then_inc(s["h_lo"], 1)

                for k in range(KT):
                    dve.wait_ge(s[f"x_loaded{k % 2}"], 16 * (k // 2) + 16)
                    nc.vector.scalar_tensor_tensor(out=pad[:, k % 2, 0:SEQ], in0=pad[:, k % 2, 0:SEQ],
                                                   scalar=nw[:, k:k + 1], in1=scale, op0=ALU.mult,
                                                   op1=ALU.mult).then_inc(s["normed"], 1)
                    if k >= 1:
                        split_h(k - 1)
                    if k == 2:
                        dve.wait_ge(s["ba_hi"], 1)
                        nc.vector.tensor_tensor(ba_w[:, :, W_BA:2 * W_BA], ba_raw[:],
                                                ba_w[:, :, 0:W_BA].bitcast(F32), ALU.subtract).then_inc(s["ba_split"], 2)
                split_h(KT - 1)

                def keep_taps(t, i, u):
                    dve.wait_ge(s[f"w_loaded{u}"], 16 * i + 16)
                    nc.vector.tensor_copy(taps[:, u, :], w_raw[:, u, KT * P:WCOLS]).then_inc(s["taps_kept"], 1)

                def split_w(t, u):
                    dve.wait_ge(s["w_hi"], t + 1)
                    nc.vector.tensor_tensor(w_lo[:, u].rearrange("p k m -> p (k m)"), w_raw[:, u, 0:KT * P],
                                            w_hi[:, u].rearrange("p k m -> p (k m)").bitcast(F32),
                                            ALU.subtract).then_inc(s["w_lo"], 1)

                keep_taps(0, 0, 0)
                split_w(0, 0)
                dve.wait_ge(s["h_lo"], KT)
                nc.vector.memset(pad[:, :, 0:CONV_K // 2], 0.0).then_inc(s["edges"], 1)
                nc.vector.memset(pad[:, :, PADW - CONV_K // 2:PADW], 0.0).then_inc(s["edges"], 1)
                dve.wait_ge(s["edges"], 2)
                dve.sem_inc(s["conv_done"], 2)
                with dve.Fori(0, CONV_TILES // 2) as i:
                    for u in range(2):
                        t = i * 2 + u
                        dve.wait_ge(s["conv_done"], t + 2)
                        keep_taps(t + 1, i + u, 1 - u)
                        split_w(t + 1, 1 - u)
                        dve.wait_ge(s["psum_free"], 2 * t + 4)
                        dve.wait_ge(s["squared"], t + 1)
                        dve.wait_ge(s[f"out_stored{u}"], 16 * i + 16)
                        dve.wait_ge(s["taps_kept"], t + 1)
                        for j in range(CONV_K):
                            if j:
                                dve.wait_ge(s["conv_step"], t * (CONV_K - 1) + j)
                            src = pad[:, u, j:j + SEQ]
                            done = s["conv_step"] if j < CONV_K - 1 else s["conv_done"]
                            if j == 0:
                                nc.vector.tensor_scalar(out[:, u, :], src, taps[:, u, j:j + 1], None, ALU.mult).then_inc(done, 1)
                            else:
                                nc.vector.scalar_tensor_tensor(out=out[:, u, :], in0=src, scalar=taps[:, u, j:j + 1],
                                                               in1=out[:, u, :], op0=ALU.mult, op1=ALU.add).then_inc(done, 1)
                with dve.Fori(CONV_TILES // 2, N_TILES // 2 - 1) as i:
                    for u in range(2):
                        split_w(i * 2 + u + 1, 1 - u)
                split_w(N_TILES - 1, 1)
                dve.wait_ge(s["stats_done"], T_Z - T_Q)
                nc.vector.tensor_copy(c.sums[:].rearrange("p t c h -> p (t c h)"),
                                      ps[:, 4, 0:(T_Z - T_Q) * 2 * NC]).then_inc(s["edges"], 1)
TABLES = 5
T_G, T_NEG, T_BETA, T_BETA_END, T_CHUNK = range(TABLES)
DN_D = P
N_QK = ATT_HEADS // 2 + 1


def scratch(a, dram):
    a.g_rows = dram("g_rows", (NC, ITEMS, P))
    a.qk_rows = dram("qk_rows", (N_QK * 2, SEQ))
    a.att_q = dram("att_q", (ATT_HEADS, P, SEQ))
    a.att_k = dram("att_k", (KV_HEADS, P, SEQ))
    a.att_v = dram("att_v", (P, NC, KV_HEADS, DH))
    a.dn_o = dram("dn_o", (DN_HEADS, P, SEQ))
    a.att_o = dram("att_o", (ATT_HEADS, DH + 1, SEQ))
    a.den_rows = dram("den_rows", (ATT_HEADS, SEQ))
    a.o_rows = dram("o_rows", (DN_HEADS, SEQ))


def token_tables(nc, a, c, l):
    names = ("loaded ba_turned act_step dve_step summed g_copied turned copied stored att_root")
    n_ba = 2 * ITEMS
    with ExitStack() as stack, semaphores(nc, names) as s:
        b = Buffers(nc, stack, "tab")
        ba = b.sbuf("ba", [2 * W_BA, SEQ])
        masks = b.sbuf("masks", [P, N_DIR, P])
        decay = b.sbuf("decay", [P, 2, ITEMS])
        x = b.sbuf("x", [P, NC, n_ba])
        low = b.sbuf("low", [P, NC, n_ba])
        beta = b.sbuf("beta", [P, NC, ITEMS])
        pos = b.sbuf("pos", [P, NC, ITEMS])
        mag = b.sbuf("mag", [P, NC, ITEMS])
        e = b.sbuf("e", [P, NC, ITEMS])
        u = b.sbuf("u", [P, NC, ITEMS])
        ln = b.sbuf("ln", [P, NC, ITEMS])
        inv = b.sbuf("inv", [P, NC, ITEMS])
        g = b.sbuf("g", [P, NC, ITEMS])
        rate = b.sbuf("rate", [P, ITEMS])
        end = b.sbuf("end", [P, NC, ITEMS])
        kk = b.sbuf("kk", [P, DN_HEADS, NC])
        rk2 = b.sbuf("rk2", [P, DN_HEADS, NC])
        att = b.sbuf("att", [P, N_QK, 2, NC])
        att_inv = b.sbuf("att_inv", [P, N_QK * 2 * NC])
        rows = b.sbuf("rows", [P, 3, P])
        ps = b.banks()
        n_att = N_QK * 2 * NC
        with nc.Block() as block:

            @block.sync
            def _(sp):
                sp.dma_start(ba[:], a.ba).then_inc(s["loaded"], 16)
                sp.dma_start(masks[:], a.masks[:, :, LEVELS, :]).then_inc(s["loaded"], 16)
                sp.dma_start(decay[:], a.decay[l].partition_broadcast(P)).then_inc(s["loaded"], 16)
                sp.wait_ge(s["copied"], 1)
                sp.dma_start(a.g_rows.rearrange("c i t -> (c i) t"), rows[:, 0, :]).then_inc(s["stored"], 16)
                sp.wait_ge(s["copied"], 3)
                qk = a.qk_rows.rearrange("r (c p) -> (r c) p", p=P)
                sp.dma_start(qk[0:P], rows[:, 1, :]).then_inc(s["stored"], 16)
                sp.dma_start(qk[P:n_att], rows[0:n_att - P, 2, :]).then_inc(s["stored"], 16)
                sp.wait_ge(s["stored"], 48)

            @block.tensor
            def _(pe):
                pe.wait_ge(s["loaded"], 48)
                for n in range(NC):
                    mm = nc.tensor.transpose(ps[:, 0, n * 2 * W_BA:(n + 1) * 2 * W_BA], ba[:, n * P:(n + 1) * P],
                                             c.ident[0:2 * W_BA, 0:2 * W_BA])
                mm.then_inc(s["ba_turned"], 1)
                pe.wait_ge(s["dve_step"], 11)
                for d in range(N_DIR):
                    h = slice(d * DN_HEADS, (d + 1) * DN_HEADS)
                    nc.tensor.matmul(ps[:, 1 + d, 0:NC * DN_HEADS], masks[:, d, :], g[:, :, h], start=True, stop=True)
                nc.tensor.matmul(ps[:, 3, 0:NC * ITEMS], c.ones[:], g[:].rearrange("p c i -> p (c i)"),
                                 start=True, stop=True).then_inc(s["summed"], 1)
                pe.wait_ge(s["g_copied"], 2)
                nc.tensor.transpose(ps[:, 4, 0:P], e[:].rearrange("p c i -> p (c i)"), c.ident[:]).then_inc(s["turned"], 1)
                pe.wait_ge(s["att_root"], 2)
                nc.tensor.transpose(ps[:, 5, 0:P], att_inv[:, 0:P], c.ident[:])
                nc.tensor.transpose(ps[0:n_att - P, 6, 0:P], att_inv[:, P:n_att], c.ident[:]).then_inc(s["turned"], 1)

            @block.scalar
            def _(act):
                act.wait_ge(s["loaded"], 48)
                nc.scalar.activation(rate[:], decay[:, 0, :], ACT.Exp).then_inc(s["act_step"], 1)
                act.wait_ge(s["dve_step"], 2)
                nc.scalar.activation(beta[:], x[:, :, 0:ITEMS], ACT.Exp, scale=-1.0).then_inc(s["act_step"], 1)
                act.wait_ge(s["dve_step"], 5)
                nc.scalar.activation(e[:], mag[:], ACT.Exp, scale=-1.0).then_inc(s["act_step"], 1)
                act.wait_ge(s["dve_step"], 6)
                nc.scalar.activation(ln[:], u[:], ACT.Ln).then_inc(s["act_step"], 1)
                act.wait_ge(s["g_copied"], 3)
                nc.scalar.activation(c.tok[:, :, T_NEG, :], e[:], ACT.Exp).then_inc(s["act_step"], 1)
                nc.scalar.activation(c.tok[:, :, T_CHUNK, :], mag[:], ACT.Exp).then_inc(s["act_step"], 1)
                nc.scalar.activation(end[:], pos[:], ACT.Exp).then_inc(s["act_step"], 1)
                act.wait_ge(s["dve_step"], 12)
                nc.scalar.activation(c.v_scale[:], kk[:].rearrange("p h c -> p c h"), ACT.Sqrt).then_inc(s["act_step"], 1)
                first = T_AQ - T_Q
                nc.scalar.activation(att[:].rearrange("p t h c -> p t c h"), c.sums[:, first:first + N_QK], ACT.Sqrt,
                                     bias=c.eps[:, 0:1], scale=1.0 / DH).then_inc(s["att_root"], 1)

            @block.vector
            def _(dve):
                step = s["dve_step"]
                dve.wait_ge(s["ba_turned"], 1)
                parts = ps[:, 0, :].rearrange("p (c w) -> p c w", w=2 * W_BA)
                nc.vector.tensor_copy(low[:], parts[:, :, W_BA:2 * W_BA]).then_inc(step, 1)
                dve.wait_ge(step, 1)
                nc.vector.tensor_tensor(x[:], parts[:, :, 0:W_BA], low[:], ALU.add).then_inc(step, 1)
                dve.wait_ge(step, 2)
                bias = decay[:, 1, :].unsqueeze(1).broadcast_to([P, NC, ITEMS])
                nc.vector.tensor_tensor(u[:], x[:, :, ITEMS:n_ba], bias, ALU.add).then_inc(step, 1)
                dve.wait_ge(step, 3)
                nc.vector.tensor_scalar(pos[:], u[:], 0.0, None, ALU.max).then_inc(step, 1)
                nc.vector.scalar_tensor_tensor(out=mag[:], in0=u[:], scalar=-1.0, in1=u[:], op0=ALU.mult,
                                               op1=ALU.max).then_inc(step, 1)
                dve.wait_ge(s["act_step"], 3)
                dve.wait_ge(step, 5)
                nc.vector.tensor_scalar(u[:], e[:], 1.0, None, ALU.add).then_inc(step, 1)
                dve.wait_ge(step, 6)
                nc.vector.scalar_tensor_tensor(out=g[:], in0=u[:], scalar=-1.0, in1=e[:], op0=ALU.add,
                                               op1=ALU.subtract).then_inc(step, 1)
                nc.vector.reciprocal(inv[:], u[:]).then_inc(step, 1)
                dve.wait_ge(step, 8)
                nc.vector.tensor_tensor(g[:], g[:], inv[:], ALU.mult).then_inc(step, 1)
                dve.wait_ge(step, 9)
                dve.wait_ge(s["act_step"], 4)
                nc.vector.tensor_tensor(ln[:], ln[:], g[:], ALU.subtract).then_inc(s["g_copied"], 1)
                dve.wait_ge(s["g_copied"], 1)
                nc.vector.scalar_tensor_tensor(out=ln[:], in0=ln[:], scalar=1.0, in1=pos[:], op0=ALU.mult,
                                               op1=ALU.add).then_inc(step, 1)
                dve.wait_ge(step, 10)
                nc.vector.scalar_tensor_tensor(out=g[:], in0=ln[:], scalar=-1.0,
                                               in1=rate[:].unsqueeze(1).broadcast_to([P, NC, ITEMS]),
                                               op0=ALU.mult, op1=ALU.mult).then_inc(step, 1)
                k0 = T_K - T_Q
                nc.vector.scalar_tensor_tensor(out=kk[:], in0=c.sums[:, k0:k0 + DN_HEADS, :, 0], scalar=EPS,
                                               in1=c.sums[:, k0:k0 + DN_HEADS, :, 1], op0=ALU.add, op1=ALU.add).then_inc(step, 1)
                dve.wait_ge(step, 12)
                nc.vector.reciprocal(rk2[:], kk[:]).then_inc(step, 1)
                nc.vector.scalar_tensor_tensor(out=c.q_eps[:], in0=c.sums[:, 0:DN_HEADS, :, 0], scalar=EPS,
                                               in1=c.sums[:, 0:DN_HEADS, :, 1], op0=ALU.add, op1=ALU.add).then_inc(step, 1)
                dve.wait_ge(step, 14)
                nc.vector.tensor_scalar(c.q_eps[:], c.q_eps[:], EPS * DN_D, None, ALU.mult).then_inc(step, 1)
                nc.vector.tensor_scalar(beta[:], beta[:], 1.0, None, ALU.add).then_inc(step, 1)
                dve.wait_ge(step, 16)
                nc.vector.reciprocal(inv[:], beta[:]).then_inc(step, 1)
                dve.wait_ge(step, 17)
                for d in range(N_DIR):
                    h = slice(d * DN_HEADS, (d + 1) * DN_HEADS)
                    nc.vector.tensor_tensor(c.tok[:, :, T_BETA, h], inv[:, :, h], rk2[:].rearrange("p h c -> p c h"),
                                            ALU.mult).then_inc(step, 1)
                dve.wait_ge(s["summed"], 1)
                for d in range(N_DIR):
                    h = slice(d * DN_HEADS, (d + 1) * DN_HEADS)
                    cum = ps[:, 1 + d, 0:NC * DN_HEADS].rearrange("p (c h) -> p c h", h=DN_HEADS)
                    nc.vector.tensor_copy(e[:, :, h], cum).then_inc(step, 1)
                nc.vector.tensor_copy(mag[:], ps[:, 3, 0:NC * ITEMS].rearrange("p (c i) -> p c i", i=ITEMS)).then_inc(step, 1)
                dve.wait_ge(step, 22)
                nc.vector.tensor_copy(c.tok[:, :, T_G, :], e[:]).then_inc(s["g_copied"], 1)
                nc.vector.tensor_tensor(pos[:], mag[:], e[:], ALU.subtract).then_inc(s["g_copied"], 1)
                dve.wait_ge(s["act_step"], 7)
                nc.vector.tensor_scalar(c.tok[:, :, T_NEG, :], c.tok[:, :, T_NEG, :], -1.0, None, ALU.mult).then_inc(step, 1)
                nc.vector.tensor_tensor(c.tok[:, :, T_BETA_END, :], c.tok[:, :, T_BETA, :], end[:], ALU.mult).then_inc(step, 1)
                dve.wait_ge(s["turned"], 1)
                nc.vector.tensor_copy(rows[:, 0, :], ps[:, 4, 0:P]).then_inc(s["copied"], 1)
                dve.wait_ge(s["att_root"], 1)
                nc.vector.reciprocal(att_inv[:], att[:].rearrange("p t h c -> p (t h c)")).then_inc(s["att_root"], 1)
                dve.wait_ge(s["turned"], 2)
                nc.vector.tensor_copy(rows[:, 1, :], ps[:, 5, 0:P]).then_inc(s["copied"], 1)
                nc.vector.tensor_copy(rows[0:n_att - P, 2, :], ps[0:n_att - P, 6, 0:P]).then_inc(s["copied"], 1)


def attention_inputs(nc, a, c, l):
    names = ("const_loaded x_loaded0 x_loaded1 y_loaded0 y_loaded1 r_loaded0 r_loaded1 v_loaded "
             "cos_done sin_done rotated scaled hi lo stored0 stored1 v_turned v_copied v_stored passed")
    with ExitStack() as stack, semaphores(nc, names) as s:
        b = Buffers(nc, stack, "rot")
        rope = b.sbuf("rope", [P, 2, SEQ])
        w = b.sbuf("w", [P, 4])
        x = b.sbuf("x", [P, 2, SEQ])
        y = b.sbuf("y", [P, 2, SEQ])
        r = b.sbuf("r", [P, 2, SEQ])
        hi = b.sbuf("hi", [P, 2, SEQ], F32R)
        lo = b.sbuf("lo", [P, 2, SEQ], F32R)
        v = b.sbuf("v", [P, SEQ])
        vt = b.sbuf("vt", [P, NC, P])
        ps = b.banks()
        quarter = DH // 4
        with nc.Block() as block:

            @block.sync
            def _(sp):
                sp.dma_start(rope[:], a.rope.rearrange("f p n -> p f n")).then_inc(s["const_loaded"], 16)
                sp.dma_start(w[:], a.qk_norm_w[l]).then_inc(s["const_loaded"], 16)
                sp.dma_start(v[:], a.proj[T_AV]).then_inc(s["v_loaded"], 16)
                for t in range(N_QK):
                    u = t % 2
                    if t >= 2:
                        sp.wait_ge(s["lo"], t - 1)
                    src = a.proj[T_AQ + t]
                    sp.dma_start(x[:, u, :], src).then_inc(s[f"x_loaded{u}"], 16)
                    for q in range(0, P // quarter):
                        sp.dma_start(y[q * quarter:(q + 1) * quarter, u, :],
                                     src[(q ^ 1) * quarter:((q ^ 1) + 1) * quarter]).then_inc(s[f"y_loaded{u}"], 16)
                    for half in range(2):
                        sp.dma_start(r[half * DH:(half + 1) * DH, u, :],
                                     a.qk_rows[2 * t + half].partition_broadcast(DH)).then_inc(s[f"r_loaded{u}"], 16)
                    if t == 1:
                        sp.wait_ge(s["v_copied"], NQ)
                        sp.dma_start(a.att_v.rearrange("p c k d -> p c (k d)"), vt[:]).then_inc(s["v_stored"], 16)
                sp.wait_ge(s["v_stored"], 16)

            @block.gpsimd
            def _(pool):
                for t in range(N_QK):
                    u = t % 2
                    pool.wait_ge(s["sin_done"], t + 1)
                    pool.wait_ge(s["cos_done"], t + 1)
                    nc.gpsimd.tensor_tensor(x[:, u, :], x[:, u, :], y[:, u, :], ALU.add).then_inc(s["rotated"], 1)

            @block.tensor
            def _(pe):
                pe.wait_ge(s["v_loaded"], 16)
                for n in range(NQ):
                    for m in range(NQ):
                        at = (n * NQ + m) * P
                        mm = nc.tensor.transpose(ps[:, n, m * P:(m + 1) * P], v[:, at:at + P], c.ident[:])
                    mm.then_inc(s["v_turned"], 1)

            @block.scalar
            def _(act):
                for n in range(NQ):
                    act.wait_ge(s["v_turned"], n + 1)
                    nc.scalar.copy(vt[:, n * NQ:(n + 1) * NQ, :].rearrange("p c d -> p (c d)"), ps[:, n, :]) \
                        .then_inc(s["v_copied"], 1)
                def store(t):
                    act.wait_ge(s["lo"], t + 1)
                    dst = a.att_q if t < N_QK - 1 else a.att_k
                    for half in range(2):
                        head = (2 * t if t < N_QK - 1 else 0) + half
                        rows = slice(half * DH, (half + 1) * DH)
                        for part, at in ((hi, 0), (lo, DH)):
                            act.dma_start(dst[head, at:at + DH], part[rows, t % 2, :].bitcast(F32)) \
                                .then_inc(s[f"stored{t % 2}"], 16)

                for t in range(N_QK):
                    u = t % 2
                    act.wait_ge(s["scaled"], t + 1)
                    if t >= 2:
                        act.wait_ge(s[f"stored{u}"], 64 * (t // 2))
                    nc.scalar.copy(hi[:, u, :], x[:, u, :]).then_inc(s["hi"], 1)
                    if t:
                        store(t - 1)
                store(N_QK - 1)
                act.wait_ge(s["stored0"], 3 * 64)
                act.wait_ge(s["stored1"], 2 * 64)

            @block.vector
            def _(dve):
                dve.wait_ge(s["const_loaded"], 32)

                def split(t):
                    dve.wait_ge(s["hi"], t + 1)
                    nc.vector.tensor_tensor(lo[:, t % 2, :], x[:, t % 2, :], hi[:, t % 2, :].bitcast(F32),
                                            ALU.subtract).then_inc(s["lo"], 1)

                for t in range(N_QK):
                    u = t % 2
                    col = 0 if t < N_QK - 1 else 2
                    dve.wait_ge(s[f"y_loaded{u}"], 16 * 8 * (t // 2 + 1))
                    nc.vector.scalar_tensor_tensor(out=y[:, u, :], in0=y[:, u, :], scalar=w[:, col + 1:col + 2],
                                                   in1=rope[:, 1, :], op0=ALU.mult, op1=ALU.mult).then_inc(s["sin_done"], 1)
                    dve.wait_ge(s[f"x_loaded{u}"], 16 * (t // 2 + 1))
                    nc.vector.scalar_tensor_tensor(out=x[:, u, :], in0=x[:, u, :], scalar=w[:, col:col + 1],
                                                   in1=rope[:, 0, :], op0=ALU.mult, op1=ALU.mult).then_inc(s["cos_done"], 1)
                    if t:
                        split(t - 1)
                    dve.wait_ge(s["rotated"], t + 1)
                    dve.wait_ge(s[f"r_loaded{u}"], 32 * (t // 2 + 1))
                    nc.vector.tensor_tensor(x[:, u, :], x[:, u, :], r[:, u, :], ALU.mult).then_inc(s["scaled"], 1)
                split(N_QK - 1)


SIDES = range(N_DIR)
HEADS = range(DN_HEADS)


def chunk_of(side, i):
    return i if side == 0 else i * -1 + (NC - 1)


def delta_net(nc, a, c, l):
    per_side = ("k1_loaded k2_loaded qv_loaded scalars1 scalars2 dd dt eg u y0 y0_part t0 x0 masked p_done p_copied "
                "xp_done x_updated xt_done y_copied yf kq_done att kt_done kk vt_done vv qg "
                "ks_done r tr_done vn vd out_done o_added ds_done state vs gram dtm ")
    names = " ".join(f"{n}{side}" for n in per_side.split() for side in SIDES) + " masks_loaded zeroed o_stored passed"
    with ExitStack() as stack, semaphores(nc, names) as s:
        b = Buffers(nc, stack, "dn")
        pair = lambda name: b.sbuf(name, [P, N_DIR, DN_HEADS, P])
        masks = b.sbuf("masks", [P, N_DIR, LEVELS + 1, P])
        k1, row, k2, q, v = (pair(n) for n in ("k1", "row", "k2", "q", "v"))
        dd, eg, dt, u, y_part = (pair(n) for n in ("dd", "eg", "dt", "u", "y_part"))
        x, y, p, yf = (pair(n) for n in ("x", "y", "p", "yf"))
        att, qg, kk, vv = (pair(n) for n in ("att", "qg", "kk", "vv"))
        r, vn, vd, state = (pair(n) for n in ("r", "vn", "vd", "state"))
        um = b.sbuf("um", [P, N_DIR, 2, DN_HEADS, P])
        sc1 = b.sbuf("sc1", [P, N_DIR, TABLES, DN_HEADS])
        sc2 = b.sbuf("sc2", [P, N_DIR, TABLES, DN_HEADS])
        vs = b.sbuf("vs", [P, N_DIR, DN_HEADS])
        o = b.sbuf("out", [P, DN_HEADS, SEQ])
        ps = b.banks()
        bank = lambda n: ps[:, n, :].rearrange("p (h t) -> p h t", h=DN_HEADS)
        inner, outer = (lambda side, n: bank(2 * side + n)), (lambda side, n: bank(4 + 2 * side + n))
        mask = lambda side, lv: masks[:, side, lv, :].unsqueeze(1).broadcast_to([P, DN_HEADS, P])
        ident = c.ident[:].unsqueeze(1).broadcast_to([P, DN_HEADS, P])
        per_head = lambda t: t.unsqueeze(2).broadcast_to([P, DN_HEADS, P])

        with nc.Block() as block:

            @block.sync
            def _(sp):
                sp.dma_start(masks[:], a.masks).then_inc(s["masks_loaded"], 16)

                def channels(first, side, i):
                    at = chunk_of(side, i) * P
                    return a.proj[first:first + DN_HEADS, :, bass.ds(at, P)].rearrange("h p t -> p h t")

                def load_k1(side, i):
                    sp.dma_start(k1[:, side], channels(T_K, side, i)).then_inc(s[f"k1_loaded{side}"], 16)
                    rows = a.g_rows[chunk_of(side, i), side * DN_HEADS:(side + 1) * DN_HEADS]
                    sp.dma_start(row[:, side], rows.partition_broadcast(P)).then_inc(s[f"k1_loaded{side}"], 16)

                def load_k2(side, i):
                    sp.dma_start(k2[:, side], channels(T_K, side, i)).then_inc(s[f"k2_loaded{side}"], 16)

                def load_qv(side, i):
                    sp.dma_start(q[:, side], channels(T_Q, side, i)).then_inc(s[f"qv_loaded{side}"], 16)
                    sp.dma_start(v[:, side], channels(T_V, side, i)).then_inc(s[f"qv_loaded{side}"], 16)

                for load in (load_k1, load_k2, load_qv):
                    for side in SIDES:
                        load(side, 0)
                with sp.Fori(1, NC) as i:
                    for side in SIDES:
                        wait_in_loop(sp, s, f"gram{side}", i)
                        wait_in_loop(sp, s, f"dd{side}", i)
                        wait_in_loop(sp, s, f"eg{side}", i)
                        load_k1(side, i)
                    for side in SIDES:
                        wait_in_loop(sp, s, f"ks_done{side}", i)
                        load_k2(side, i)
                    for side in SIDES:
                        wait_in_loop(sp, s, f"vt_done{side}", i)
                        wait_in_loop(sp, s, f"qg{side}", i)
                        load_qv(side, i)
                for side in SIDES:
                    sp.wait_ge(s[f"o_added{side}"], NC)
                sp.dma_start(a.dn_o.rearrange("h p t -> p h t"), o[:]).then_inc(s["o_stored"], 16)
                sp.wait_ge(s["o_stored"], 16)

            @block.tensor
            def _(pe):
                def each(out, left, right):
                    for h in HEADS:
                        mm = nc.tensor.matmul(out[:, h, :], left[:, h, :], right[:, h, :], start=True, stop=True)
                    return mm

                def turn(out, src):
                    for h in HEADS:
                        mm = nc.tensor.transpose(out[:, h, :], src[:, h, :], c.ident[:])
                    return mm

                def gram(side, i):
                    pe.wait_ge(s[f"k1_loaded{side}"], 32 * i + 32)
                    pe.wait_ge(s[f"p_copied{side}"], 6 * i)
                    each(inner(side, 0), k1[:, side], k1[:, side]).then_inc(s[f"gram{side}"], 1)

                def turn_first(side, i):
                    pe.wait_ge(s[f"y0{side}"], i + 1)
                    turn(inner(side, 1), y[:, side]).then_inc(s[f"t0{side}"], 1)

                def product(side, i, lv):
                    pe.wait_ge(s[f"masked{side}"], 6 * i + lv)
                    if lv == 1:
                        pe.wait_ge(s[f"x0{side}"], i + 1)
                    else:
                        pe.wait_ge(s[f"x_updated{side}"], 5 * i + lv - 1)
                        pe.wait_ge(s[f"y_copied{side}"], 5 * i + lv - 1)
                    each(inner(side, 0), um[:, side, lv % 2], x[:, side]).then_inc(s[f"p_done{side}"], 1)

                def step(side, i, lv):
                    pe.wait_ge(s[f"p_copied{side}"], 6 * i + lv)
                    if lv < LEVELS - 1:
                        each(inner(side, 1), y[:, side], p[:, side]).then_inc(s[f"xp_done{side}"], 1)
                    else:
                        each(inner(side, 1), p[:, side], y[:, side]).then_inc(s[f"xp_done{side}"], 1)

                def turn_x(side, i, lv):
                    pe.wait_ge(s[f"x_updated{side}"], 5 * i + lv)
                    turn(inner(side, 0), x[:, side]).then_inc(s[f"xt_done{side}"], 1)

                def key_query(side, i):
                    pe.wait_ge(s[f"k2_loaded{side}"], 16 * i + 16)
                    pe.wait_ge(s[f"qv_loaded{side}"], 32 * i + 32)
                    pe.wait_ge(s[f"o_added{side}"], i)
                    each(outer(side, 0), k2[:, side], q[:, side]).then_inc(s[f"kq_done{side}"], 1)

                def turn_k(side, i):
                    pe.wait_ge(s[f"state{side}"], i + 1)
                    turn(outer(side, 1), k2[:, side]).then_inc(s[f"kt_done{side}"], 1)

                def turn_v(side, i):
                    pe.wait_ge(s[f"att{side}"], i + 1)
                    turn(outer(side, 0), v[:, side]).then_inc(s[f"vt_done{side}"], 1)

                def scan_ks(side, j):
                    pe.wait_ge(s[f"state{side}"], j + 1)
                    pe.wait_ge(s[f"vv{side}"], j + 1)
                    each(outer(side, 0), k2[:, side], state[:, side]).then_inc(s[f"ks_done{side}"], 1)

                def scan_solve(side, j):
                    pe.wait_ge(s[f"r{side}"], j + 1)
                    pe.wait_ge(s[f"yf{side}"], j + 1)
                    pe.wait_ge(s[f"kk{side}"], j + 1)
                    each(outer(side, 1), yf[:, side], r[:, side]).then_inc(s[f"tr_done{side}"], 1)

                def scan_out(side, j):
                    pe.wait_ge(s[f"qg{side}"], j + 1)
                    pe.wait_ge(s[f"vn{side}"], j + 1)
                    for h in HEADS:
                        nc.tensor.matmul(outer(side, 0)[:, h, :], state[:, side, h, :], qg[:, side, h, :],
                                         start=True, stop=False)
                        mm = nc.tensor.matmul(outer(side, 0)[:, h, :], vn[:, side, h, :], att[:, side, h, :],
                                              start=False, stop=True)
                    mm.then_inc(s[f"out_done{side}"], 1)

                def scan_state(side, j):
                    pe.wait_ge(s[f"vd{side}"], j + 1)
                    each(outer(side, 1), kk[:, side], vd[:, side]).then_inc(s[f"ds_done{side}"], 1)

                def iteration(i, j):
                    local, scan = i is not None, j is not None
                    for side in SIDES:
                        if local:
                            gram(side, i)
                    for side in SIDES:
                        if scan:
                            scan_ks(side, j)
                    for side in SIDES:
                        if local:
                            turn_first(side, i)
                    for side in SIDES:
                        if scan:
                            scan_solve(side, j)
                    for lv in range(1, LEVELS):
                        for side in SIDES:
                            if local:
                                product(side, i, lv)
                        if scan and lv <= 2:
                            scan_out(lv - 1, j)
                        if local and lv >= 3 and lv <= 5:
                            (key_query, turn_k, turn_v)[lv - 3](0, i)
                        for side in SIDES:
                            if local:
                                step(side, i, lv)
                        if scan and lv <= 2:
                            scan_state(lv - 1, j)
                        if local and lv >= 3 and lv <= 5:
                            (key_query, turn_k, turn_v)[lv - 3](1, i)
                        for side in SIDES:
                            if local and lv < LEVELS - 1:
                                turn_x(side, i, lv)

                iteration(0, None)
                with pe.Fori(1, NC) as i:
                    iteration(i, i - 1)
                iteration(None, NC - 1)

            @block.scalar
            def _(act):
                def evacuate(done, count, dst, src, name, side):
                    act.wait_ge(s[f"{done}{side}"], count)
                    nc.scalar.copy(dst, src).then_inc(s[f"{name}{side}"], 1)

                def local(i):
                    for side in SIDES:
                        act.wait_ge(s[f"dd{side}"], i + 1)
                        nc.scalar.activation(dt[:, side], dd[:, side], ACT.Exp).then_inc(s[f"dt{side}"], 1)
                    for side in SIDES:
                        act.wait_ge(s[f"k1_loaded{side}"], 32 * i + 32)
                        act.wait_ge(s[f"qg{side}"], i)
                        nc.scalar.activation(eg[:, side], row[:, side], ACT.Exp).then_inc(s[f"eg{side}"], 1)
                    for side in SIDES:
                        evacuate("t0", i + 1, x[:, side], inner(side, 1), "x0", side)
                    for lv in range(1, LEVELS):
                        for side in SIDES:
                            evacuate("p_done", 6 * i + lv, p[:, side], inner(side, 0), "p_copied", side)
                        if lv == 4:
                            for side in SIDES:
                                if side == 1:
                                    evacuate("xt_done", 5 * i + lv, y[:, 0], inner(0, 0), "y_copied", 0)
                                evacuate("kt_done", i + 1, kk[:, side], outer(side, 1), "kk", side)
                            evacuate("xt_done", 5 * i + lv, y[:, 1], inner(1, 0), "y_copied", 1)
                        elif lv < LEVELS - 1:
                            for side in SIDES:
                                evacuate("xt_done", 5 * i + lv, y[:, side], inner(side, 0), "y_copied", side)

                with act.Fori(0, NC) as i:
                    local(i)

            @block.gpsimd
            def _(pool):
                for side in SIDES:
                    nc.gpsimd.memset(state[:, side], 0.0).then_inc(s[f"state{side}"], 1)
                nc.gpsimd.memset(o[:], 0.0).then_inc(s["zeroed"], 1)
                pool.wait_ge(s["masks_loaded"], 16)

                def scalars(side, i):
                    heads = slice(side * DN_HEADS, (side + 1) * DN_HEADS)
                    pool.wait_ge(s[f"u{side}"], i)
                    nc.gpsimd.tensor_copy(sc1[:, side], c.tok[:, bass.ds(chunk_of(side, i), 1), :, heads].squeeze(1)) \
                        .then_inc(s[f"scalars1{side}"], 1)

                def v_scalars(side, i):
                    pool.wait_ge(s[f"vv{side}"], i)
                    nc.gpsimd.tensor_copy(vs[:, side], c.v_scale[:, bass.ds(chunk_of(side, i), 1), :].squeeze(1)) \
                        .then_inc(s[f"vs{side}"], 1)

                def scan_scalars(side, i):
                    heads = slice(side * DN_HEADS, (side + 1) * DN_HEADS)
                    pool.wait_ge(s[f"state{side}"], i + 1)
                    nc.gpsimd.tensor_copy(sc2[:, side], c.tok[:, bass.ds(chunk_of(side, i), 1), :, heads].squeeze(1)) \
                        .then_inc(s[f"scalars2{side}"], 1)

                for side in SIDES:
                    scalars(side, 0)
                def local(i):
                    for side in SIDES:
                        v_scalars(side, i)
                    for lv in range(1, LEVELS):
                        for side in SIDES:
                            pool.wait_ge(s[f"u{side}"], i + 1)
                            if lv <= 2:
                                pool.wait_ge(s[f"xp_done{side}"], 6 * i)
                            else:
                                pool.wait_ge(s[f"p_done{side}"], 6 * i + lv - 2)
                            nc.gpsimd.tensor_tensor(um[:, side, lv % 2], u[:, side], mask(side, lv), ALU.mult) \
                                .then_inc(s[f"masked{side}"], 1)
                        if lv == 3:
                            for side in SIDES:
                                scan_scalars(side, i)
                        if lv == 4:
                            for side in SIDES:
                                pool.wait_ge(s[f"qv_loaded{side}"], 32 * i + 32)
                                pool.wait_ge(s[f"eg{side}"], i + 1)
                                pool.wait_ge(s[f"o_added{side}"], i)
                                nc.gpsimd.tensor_tensor(qg[:, side], q[:, side], eg[:, side], ALU.mult) \
                                    .then_inc(s[f"qg{side}"], 1)

                with pool.Fori(0, NC - 1) as i:
                    local(i)
                    for side in SIDES:
                        scalars(side, i + 1)
                local(NC - 1)

            @block.vector
            def _(dve):
                def decays(side, i):
                    dve.wait_ge(s[f"k1_loaded{side}"], 32 * i + 32)
                    dve.wait_ge(s[f"scalars1{side}"], i + 1)
                    dve.wait_ge(s[f"dt{side}"], i)
                    for h in HEADS:
                        op = nc.vector.tensor_scalar(dd[:, side, h, :], row[:, side, h, :], sc1[:, side, T_G, h:h + 1],
                                                     0.0, ALU.subtract, ALU.min)
                    op.then_inc(s[f"dd{side}"], 1)

                def system(side, i):
                    dve.wait_ge(s[f"dt{side}"], i + 1)
                    nc.vector.tensor_tensor(dt[:, side], dt[:, side], mask(side, LEVELS), ALU.mult).then_inc(s[f"dtm{side}"], 1)
                    dve.wait_ge(s[f"dtm{side}"], i + 1)
                    dve.wait_ge(s[f"gram{side}"], i + 1)
                    dve.wait_ge(s[f"masked{side}"], 6 * i)
                    for h in HEADS:
                        op = nc.vector.scalar_tensor_tensor(out=u[:, side, h, :], in0=inner(side, 0)[:, h, :],
                                                            scalar=sc1[:, side, T_BETA, h:h + 1], in1=dt[:, side, h, :],
                                                            op0=ALU.mult, op1=ALU.mult)
                    op.then_inc(s[f"u{side}"], 1)
                    dve.wait_ge(s[f"u{side}"], i + 1)
                    nc.vector.tensor_tensor(y_part[:, side], u[:, side], mask(side, 0), ALU.mult).then_inc(s[f"y0_part{side}"], 1)
                    dve.wait_ge(s[f"y0_part{side}"], i + 1)
                    dve.wait_ge(s[f"yf{side}"], i)
                    nc.vector.tensor_tensor(y[:, side], y_part[:, side], ident, ALU.add).then_inc(s[f"y0{side}"], 1)

                def update(side, i, lv):
                    dve.wait_ge(s[f"xp_done{side}"], 6 * i + lv)
                    if lv < LEVELS - 1:
                        if lv > 1:
                            dve.wait_ge(s[f"x_updated{side}"], 5 * i + lv - 1)
                        nc.vector.tensor_tensor(x[:, side], x[:, side], inner(side, 1), ALU.subtract) \
                            .then_inc(s[f"x_updated{side}"], 1)
                    else:
                        nc.vector.tensor_tensor(yf[:, side], y[:, side], inner(side, 1), ALU.subtract) \
                            .then_inc(s[f"yf{side}"], 1)

                def attend(side, i):
                    dve.wait_ge(s[f"kq_done{side}"], i + 1)
                    nc.vector.tensor_tensor(att[:, side], outer(side, 0), dt[:, side], ALU.mult).then_inc(s[f"att{side}"], 1)

                def values(side, i):
                    dve.wait_ge(s[f"vt_done{side}"], i + 1)
                    dve.wait_ge(s[f"vs{side}"], i + 1)
                    dve.wait_ge(s[f"r{side}"], i)
                    nc.vector.tensor_tensor(vv[:, side], outer(side, 0), per_head(vs[:, side]), ALU.mult) \
                        .then_inc(s[f"vv{side}"], 1)

                def remainder(side, j):
                    dve.wait_ge(s[f"ks_done{side}"], j + 1)
                    dve.wait_ge(s[f"vv{side}"], j + 1)
                    dve.wait_ge(s[f"scalars2{side}"], j + 1)
                    for h in HEADS:
                        op = nc.vector.scalar_tensor_tensor(out=r[:, side, h, :], in0=outer(side, 0)[:, h, :],
                                                            scalar=sc2[:, side, T_NEG, h:h + 1], in1=vv[:, side, h, :],
                                                            op0=ALU.mult, op1=ALU.add)
                    op.then_inc(s[f"r{side}"], 1)

                def new_values(side, j):
                    dve.wait_ge(s[f"tr_done{side}"], j + 1)
                    nc.vector.tensor_tensor(vn[:, side], outer(side, 1), per_head(sc2[:, side, T_BETA, :]), ALU.mult) \
                        .then_inc(s[f"vn{side}"], 1)
                    nc.vector.tensor_tensor(vd[:, side], outer(side, 1), per_head(sc2[:, side, T_BETA_END, :]), ALU.mult) \
                        .then_inc(s[f"vd{side}"], 1)

                def output(side, j):
                    at = chunk_of(side, j) * P
                    dve.wait_ge(s[f"o_added{1 - side}"], j)
                    dve.wait_ge(s[f"out_done{side}"], j + 1)
                    there = o[:, :, bass.ds(at, P)]
                    nc.vector.tensor_tensor(there, outer(side, 0), there, ALU.add).then_inc(s[f"o_added{side}"], 1)

                def new_state(side, j):
                    dve.wait_ge(s[f"ds_done{side}"], j + 1)
                    dve.wait_ge(s[f"state{side}"], j + 1)
                    for h in HEADS:
                        op = nc.vector.scalar_tensor_tensor(out=state[:, side, h, :], in0=state[:, side, h, :],
                                                            scalar=sc2[:, side, T_CHUNK, h:h + 1],
                                                            in1=outer(side, 1)[:, h, :], op0=ALU.mult, op1=ALU.add)
                    op.then_inc(s[f"state{side}"], 1)

                def iteration(i, j):
                    local, scan = i is not None, j is not None
                    for side in SIDES:
                        if local:
                            decays(side, i)
                    for side in SIDES:
                        if scan:
                            remainder(side, j)
                    for side in SIDES:
                        if local:
                            system(side, i)
                    for side in SIDES:
                        if scan:
                            new_values(side, j)
                    for lv in range(1, LEVELS):
                        if scan and lv <= 2:
                            output(lv - 1, j)
                        if local and lv == 3:
                            attend(0, i)
                        if local and lv == 5:
                            values(0, i)
                        for side in SIDES:
                            if local:
                                update(side, i, lv)
                        if scan and lv <= 2:
                            new_state(lv - 1, j)
                        if local and lv == 3:
                            attend(1, i)
                        if local and lv == 5:
                            values(1, i)

                dve.wait_ge(s["masks_loaded"], 16)
                dve.wait_ge(s["zeroed"], 1)
                iteration(0, None)
                with dve.Fori(1, NC) as i:
                    iteration(i, i - 1)
                iteration(None, NC - 1)


N_UNITS = NC
MAX_PLAN = [3, 3, 3, 3, 2, 2, 0, 0]
PAIRS = NC // 2
K_ROWS = DH + NQ


def attention(nc, a, c, l):
    side = "q_loaded max_done max_part max_neg turned q2 q2_loaded k_loaded"
    names = " ".join(f"{n}{u}" for n in side.split() for u in range(2)) + \
        (" v_loaded const_loaded ones_set scores_done exp_done pv_done unit_done unit_read o_done o_copied "
         "o_stored0 o_stored1 passed")
    NB = ATT_HEADS * NQ
    with ExitStack() as stack, semaphores(nc, names) as s:
        b = Buffers(nc, stack, "att")
        k1 = b.sbuf("k1", [P, KV_HEADS, SEQ], F32R)
        k2 = b.sbuf("k2", [K_ROWS, KV_HEADS, SEQ], F32R)
        v = b.sbuf("v", [P, KV_HEADS, NC, DH + 1])
        quarter = b.sbuf("quarter", [NQ, NQ, P])
        q1 = b.sbuf("q1", [P, 2, QB], F32R)
        q2 = b.sbuf("q2", [K_ROWS, 2, QB], F32R)
        probs = b.sbuf("probs", [P, 2, 2, QB])
        part = b.sbuf("part", [P, 2, NQ, NQ])
        top = b.sbuf("top", [P, 2, NQ])
        o = b.sbuf("o", [DH + 1, 2, QB])
        ps = b.banks()
        with nc.Block() as block:

            @block.sync
            def _(sp):
                for kv in range(KV_HEADS):
                    sp.dma_start(k1[0:DH, kv, :].bitcast(F32), a.att_k[kv, 0:DH]).then_inc(s[f"k_loaded{kv}"], 16)
                    sp.dma_start(k1[DH:P, kv, :].bitcast(F32), a.att_k[kv, 0:DH]).then_inc(s[f"k_loaded{kv}"], 16)
                    sp.dma_start(k2[0:DH, kv, :].bitcast(F32), a.att_k[kv, DH:P]).then_inc(s[f"k_loaded{kv}"], 16)
                    sp.dma_start(v[:, kv, :, 0:DH], a.att_v[:, :, kv, :]).then_inc(s["v_loaded"], 16)
                sp.dma_start(quarter[:], a.quarter).then_inc(s["const_loaded"], 16)

                def load_q(kv, i):
                    head = kv * GROUP + i // NQ
                    at = (i % NQ) * QB
                    sp.dma_start(q1[:, kv, :].bitcast(F32), a.att_q[head, :, bass.ds(at, QB)]).then_inc(s[f"q_loaded{kv}"], 16)
                    sp.dma_start(q2[0:DH, kv, :].bitcast(F32), a.att_q[head, 0:DH, bass.ds(at, QB)]).then_inc(s[f"q2_loaded{kv}"], 16)

                for kv in range(2):
                    load_q(kv, 0)
                with sp.Fori(0, NB // 2 - 1) as i:
                    for kv in range(2):
                        wait_in_loop(sp, s, "scores_done", (i * 2 + kv + 1) * PAIRS)
                        load_q(kv, i + 1)
                        wait_in_loop(sp, s, "o_copied", i * 2 + kv + 1)
                        sp.dma_start(a.att_o[kv * GROUP + i // NQ, :, bass.ds((i % NQ) * QB, QB)], o[:, kv, :]) \
                            .then_inc(s[f"o_stored{kv}"], 16)
                for kv in range(2):
                    sp.wait_ge(s["o_copied"], NB - 1 + kv)
                    sp.dma_start(a.att_o[kv * GROUP + GROUP - 1, :, SEQ - QB:SEQ], o[:, kv, :]) \
                        .then_inc(s[f"o_stored{kv}"], 16)
                for kv in range(2):
                    sp.wait_ge(s[f"o_stored{kv}"], 16 * (NB // 2))

            @block.gpsimd
            def _(pool):
                nc.gpsimd.memset(v[:, :, :, DH:DH + 1], 1.0).then_inc(s["ones_set"], 1)

            @block.tensor
            def _(pe):
                def max_unit(kv, i, n, u):
                    tile, keys = u // NQ, u % NQ
                    if u == 0:
                        pe.wait_ge(s[f"q2_loaded{kv}"], 16 * i + 16)
                    pe.wait_ge(s["unit_read"], n * N_UNITS + u + 1)
                    nc.tensor.matmul(ps[:, 4 + u % 2, :], q2[0:DH, kv, tile * P:(tile + 1) * P],
                                     k1[0:DH, kv, keys * QB:(keys + 1) * QB], start=True, stop=True) \
                        .then_inc(s["unit_done"], 1)

                def turn_max(kv, i):
                    pe.wait_ge(s[f"max_neg{kv}"], i + 1)
                    nc.tensor.transpose(ps[0:NQ, 7, 0:P], top[:, kv, :], c.ident[:]).then_inc(s[f"turned{kv}"], 1)

                def scores(kv, i, n, pair):
                    pe.wait_ge(s["exp_done"], n * PAIRS + pair + 1)
                    if pair == 0:
                        pe.wait_ge(s[f"q_loaded{kv}"], 16 * i + 16)
                        pe.wait_ge(s[f"q2{kv}"], i + 1)
                    for m in range(2):
                        keys = slice((2 * pair + m) * P, (2 * pair + m + 1) * P)
                        out = ps[:, 2 * (pair % 2) + m, :]
                        nc.tensor.matmul(out, k1[:, kv, keys], q1[:, kv, :], start=True, stop=False)
                        mm = nc.tensor.matmul(out, k2[:, kv, keys], q2[:, kv, :], start=False, stop=True)
                    mm.then_inc(s["scores_done"], 1)

                def values(kv, n, pair):
                    pe.wait_ge(s["exp_done"], n * PAIRS + pair + 3)
                    if pair == 0:
                        pe.wait_ge(s["o_copied"], n)
                    for m in range(2):
                        mm = nc.tensor.matmul(ps[0:DH + 1, 6, :], v[:, kv, 2 * pair + m, :], probs[:, pair % 2, m, :],
                                              start=(pair == 0 and m == 0), stop=(pair == PAIRS - 1 and m == 1))
                    mm.then_inc(s["pv_done"], 1)

                def blocks(kv, i, n, nxt):
                    u = 0
                    for pair in range(PAIRS + 1):
                        if pair < PAIRS:
                            scores(kv, i, n, pair)
                            for _ in range(MAX_PLAN[pair] if nxt else 0):
                                max_unit(*nxt, u)
                                u += 1
                        if pair > 0:
                            values(kv, n, pair - 1)
                        if pair == PAIRS - 1 and nxt:
                            turn_max(nxt[0], nxt[1])

                pe.sem_inc(s["exp_done"], 2)
                for kv in range(KV_HEADS):
                    pe.wait_ge(s[f"k_loaded{kv}"], 48)
                pe.wait_ge(s["v_loaded"], 32)
                pe.wait_ge(s["ones_set"], 2)
                for u in range(N_UNITS):
                    max_unit(0, 0, 0, u)
                turn_max(0, 0)
                with pe.Fori(0, NB // 2 - 1) as i:
                    blocks(0, i, i * 2, (1, i, i * 2 + 1))
                    blocks(1, i, i * 2 + 1, (0, i + 1, i * 2 + 2))
                last = NB // 2 - 1
                blocks(0, last, NB - 2, (1, last, NB - 1))
                blocks(1, last, NB - 1, None)

            @block.scalar
            def _(act):
                with act.Fori(0, NB // 2) as i:
                    for kv in range(2):
                        n = i * 2 + kv
                        for pair in range(PAIRS):
                            act.wait_ge(s["scores_done"], n * PAIRS + pair + 1)
                            act.wait_ge(s["pv_done"], n * PAIRS + pair + 1)
                            nc.scalar.activation(probs[:, pair % 2], ps[:, 2 * (pair % 2):2 * (pair % 2) + 2, :], ACT.Exp,
                                                 scale=SCALE).then_inc(s["exp_done"], 1)

            @block.vector
            def _(dve):
                def maxima(kv, i, n):
                    dve.wait_ge(s[f"turned{kv}"], i)
                    for u in range(N_UNITS):
                        dve.wait_ge(s["unit_done"], n * N_UNITS + u + 1)
                        nc.vector.tensor_reduce(part[:, kv, u // NQ, u % NQ:u % NQ + 1], ps[:, 4 + u % 2, :], AX.X, ALU.max) \
                            .then_inc(s["unit_read"], 1)
                    dve.wait_ge(s["unit_read"], n * N_UNITS + N_UNITS + 2)
                    nc.vector.tensor_reduce(top[:, kv, :], part[:, kv], AX.X, ALU.max).then_inc(s[f"max_part{kv}"], 1)
                    dve.wait_ge(s[f"max_part{kv}"], i + 1)
                    nc.vector.tensor_scalar(top[:, kv, :], top[:, kv, :], -1.0, None, ALU.mult).then_inc(s[f"max_neg{kv}"], 1)
                    dve.wait_ge(s[f"turned{kv}"], i + 1)
                    turned = ps[0:NQ, 7, 0:P].unsqueeze(1).broadcast_to([NQ, NQ, P])
                    nc.vector.tensor_tensor(q2[DH:K_ROWS, kv, :].rearrange("r (t q) -> r t q", q=P), turned, quarter[:],
                                            ALU.mult).then_inc(s[f"q2{kv}"], 1)

                def output(kv, i, n):
                    dve.wait_ge(s["pv_done"], n * PAIRS + PAIRS + 2)
                    dve.wait_ge(s[f"o_stored{kv}"], 16 * i)
                    nc.vector.tensor_copy(o[:, kv, :], ps[0:DH + 1, 6, :]).then_inc(s["o_copied"], 1)

                nc.vector.memset(k2[DH:K_ROWS, :, :].bitcast(F32), 1.0).then_inc(s["ones_set"], 1)
                dve.sem_inc(s["unit_read"], 2)
                dve.wait_ge(s["const_loaded"], 16)
                dve.sem_inc(s["pv_done"], 2)
                maxima(0, 0, 0)
                with dve.Fori(0, NB // 2 - 1) as i:
                    maxima(1, i, i * 2 + 1)
                    output(0, i, i * 2)
                    maxima(0, i + 1, i * 2 + 2)
                    output(1, i, i * 2 + 1)
                maxima(1, NB // 2 - 1, NB - 1)
                output(0, NB // 2 - 1, NB - 2)
                output(1, NB // 2 - 1, NB - 1)


def branch_scales(nc, a, c, l):
    names = "x_loaded0 x_loaded1 squared summed mean root inv turned copied stored den_loaded den_done passed"
    with ExitStack() as stack, semaphores(nc, names) as s:
        b = Buffers(nc, stack, "bs")
        x = b.sbuf("x", [P, 2, SEQ])
        sq = b.sbuf("sq", [P, 2, SEQ])
        mean = b.sbuf("mean", [P, DN_HEADS, NC])
        inv = b.sbuf("inv", [P, DN_HEADS, NC])
        rows = b.sbuf("rows", [P // 2, P])
        den = b.sbuf("den", [P, P])
        den_inv = b.sbuf("den_inv", [P, P])
        ps = b.banks()
        n_rows = DN_HEADS * NC
        with nc.Block() as block:

            @block.sync
            def _(sp):
                for h in range(ATT_HEADS):
                    sp.dma_start(den[h * NC:(h + 1) * NC, :], a.att_o[h, DH].rearrange("(c p) -> c p", p=P)) \
                        .then_inc(s["den_loaded"], 16)
                for h in range(DN_HEADS):
                    if h >= 2:
                        sp.wait_ge(s["squared"], h - 1)
                    sp.dma_start(x[:, h % 2, :], a.dn_o[h]).then_inc(s[f"x_loaded{h % 2}"], 16)
                sp.wait_ge(s["den_done"], 1)
                sp.dma_start(a.den_rows.rearrange("h (c p) -> (h c) p", p=P), den_inv[:]).then_inc(s["stored"], 16)
                sp.wait_ge(s["copied"], 1)
                sp.dma_start(a.o_rows.rearrange("h (c p) -> (h c) p", p=P), rows[0:n_rows, :]).then_inc(s["stored"], 16)
                sp.wait_ge(s["stored"], 32)

            @block.scalar
            def _(act):
                for h in range(DN_HEADS):
                    act.wait_ge(s[f"x_loaded{h % 2}"], 16 * (h // 2 + 1))
                    if h >= 2:
                        act.wait_ge(s["summed"], h - 1)
                    nc.scalar.activation(sq[:, h % 2, :], x[:, h % 2, :], ACT.Square).then_inc(s["squared"], 1)
                act.wait_ge(s["mean"], 1)
                nc.scalar.activation(inv[:], mean[:], ACT.Sqrt).then_inc(s["root"], 1)

            @block.tensor
            def _(pe):
                for h in range(DN_HEADS):
                    pe.wait_ge(s["squared"], h + 1)
                    for n in range(NC):
                        col = h * NC + n
                        mm = nc.tensor.matmul(ps[:, 0, col:col + 1], sq[:, h % 2, n * P:(n + 1) * P], c.ones[:, 0:1],
                                              start=True, stop=True)
                    mm.then_inc(s["summed"], 1)
                pe.wait_ge(s["inv"], 1)
                nc.tensor.transpose(ps[0:n_rows, 1, 0:P], mean[:].rearrange("p h c -> p (h c)"), c.ident[:]) \
                    .then_inc(s["turned"], 1)

            @block.vector
            def _(dve):
                dve.wait_ge(s["den_loaded"], 16 * ATT_HEADS)
                nc.vector.reciprocal(den_inv[:], den[:]).then_inc(s["den_done"], 1)
                dve.wait_ge(s["summed"], DN_HEADS)
                nc.vector.scalar_tensor_tensor(out=mean[:].rearrange("p h c -> p (h c)"), in0=ps[:, 0, 0:n_rows],
                                               scalar=1.0 / DN_D, in1=c.q_eps[:].rearrange("p h c -> p (h c)"),
                                               op0=ALU.mult, op1=ALU.add).then_inc(s["mean"], 1)
                dve.wait_ge(s["root"], 1)
                nc.vector.reciprocal(mean[:], inv[:]).then_inc(s["inv"], 1)
                dve.wait_ge(s["turned"], 1)
                nc.vector.tensor_copy(rows[0:n_rows, :], ps[0:n_rows, 1, 0:P]).then_inc(s["copied"], 1)


def output_projection(nc, a, c, l):
    names = ("w_loaded0 w_loaded1 x_loaded0 x_loaded1 z_loaded0 z_loaded1 r_loaded0 r_loaded1 scaled gated y_hi y_lo "
             "w_hi w_lo proj_done psum_free squared summed xr_loaded0 xr_loaded1 x_stored0 x_stored1 small_loaded "
             "passed")
    with ExitStack() as stack, semaphores(nc, names) as s:
        b = Buffers(nc, stack, "out")
        y_hi = b.sbuf("y_hi", [P, KT, SEQ], F32R)
        y_lo = b.sbuf("y_lo", [P, KT, SEQ], F32R)
        w_raw = b.sbuf("w_raw", [P, 2, KT * P])
        w_hi = b.sbuf("w_hi", [P, 2, KT, P], F32R)
        w_lo = b.sbuf("w_lo", [P, 2, KT, P], F32R)
        norm = b.sbuf("norm", [P, 1])
        x = b.sbuf("x", [P, 2, SEQ])
        r = b.sbuf("r", [P, 1, SEQ])
        z = b.sbuf("z", [P, 1, SEQ])
        acc = c.sq_acc
        ps = b.banks()
        with nc.Block() as block:

            @block.sync
            def _(sp):
                sp.dma_start(norm[:], a.dn_norm_w[l]).then_inc(s["small_loaded"], 16)
                for k in range(KT):
                    if k >= 2:
                        sp.wait_ge(s["y_lo"], k - 1)
                    if k < DN_HEADS:
                        sp.dma_start(x[:, k % 2, :], a.dn_o[k]).then_inc(s[f"x_loaded{k % 2}"], 32)
                    else:
                        h = 2 * (k - DN_HEADS)
                        for half in range(2):
                            sp.dma_start(x[half * DH:(half + 1) * DH, k % 2, :], a.att_o[h + half, 0:DH]) \
                                .then_inc(s[f"x_loaded{k % 2}"], 16)
                    if k >= 1:
                        sp.wait_ge(s["scaled"], k)
                    if k < DN_HEADS:
                        sp.dma_start(r[:, 0, :], a.o_rows[k].partition_broadcast(P)).then_inc(s["r_loaded0"], 32)
                    else:
                        for half in range(2):
                            sp.dma_start(r[half * DH:(half + 1) * DH, 0, :], a.den_rows[h + half].partition_broadcast(DH)) \
                                .then_inc(s["r_loaded0"], 16)
                    if k >= 1:
                        sp.wait_ge(s["gated"], k)
                    sp.dma_start(z[:, 0, :], a.proj[T_Z + k]).then_inc(s["z_loaded0"], 16)
                    if k < 2:
                        sp.dma_start(w_raw[:, k, :], a.w_out[l, k]).then_inc(s[f"w_loaded{k}"], 16)
                sp.wait_ge(s["y_lo"], KT)
                with sp.Fori(0, KT // 2) as i:
                    for u in range(2):
                        wait_in_loop(sp, s, f"x_stored{u}", 16 * i)
                        wait_in_loop(sp, s, "squared", i * 2)
                        sp.dma_start(x[:, u, :], a.x_res[i * 2 + u]).then_inc(s[f"xr_loaded{u}"], 16)
                    for u in range(2):
                        wait_in_loop(sp, s, "psum_free", 2 * (i * 2 + u) + 4)
                        sp.dma_start(a.x_res[i * 2 + u], x[:, u, :]).then_inc(s[f"x_stored{u}"], 16)
                        wait_in_loop(sp, s, "w_lo", i * 2 + u + 1)
                        at = (i * 2 + u + 2) % KT
                        sp.dma_start(w_raw[:, u, :], a.w_out[l, at]).then_inc(s[f"w_loaded{u}"], 16)
                for u in range(2):
                    sp.wait_ge(s[f"x_stored{u}"], 16 * (KT // 2))
                    sp.wait_ge(s[f"w_loaded{u}"], 16 * (KT // 2 + 1))

            @block.tensor
            def _(pe):
                pe.wait_ge(s["y_lo"], KT)
                with pe.Fori(0, KT // 2) as i:
                    for u in range(2):
                        t = i * 2 + u
                        pe.wait_ge(s["w_lo"], t + 1)
                        for half in range(2):
                            pe.wait_ge(s["psum_free"], 2 * t + half + 1)
                            for k in range(KT):
                                for w, y in ((w_hi, y_hi), (w_hi, y_lo), (w_lo, y_hi)):
                                    for n in range(2):
                                        at = half * HALF + n * QB
                                        mm = nc.tensor.matmul(
                                            ps[:, 2 * half + n, :], w[:, u, k, :], y[:, k, at:at + QB],
                                            start=(k == 0 and w is w_hi and y is y_hi), stop=(k == KT - 1 and w is w_lo))
                            mm.then_inc(s["proj_done"], 1)

            @block.gpsimd
            def _(pool):
                pool.sem_inc(s["psum_free"], 2)

            @block.scalar
            def _(act):
                for k in range(KT):
                    act.wait_ge(s["gated"], k + 1)
                    nc.scalar.copy(y_hi[:, k, :], x[:, k % 2, :]).then_inc(s["y_hi"], 1)

                def split_hi(t, i, u):
                    act.wait_ge(s[f"w_loaded{u}"], 16 * i + 16)
                    if isinstance(t, int):
                        pass
                    else:
                        act.wait_ge(s["proj_done"], 2 * (t + 1) - 4)
                    nc.scalar.copy(w_hi[:, u].rearrange("p k m -> p (k m)"), w_raw[:, u, :]).then_inc(s["w_hi"], 1)

                for u in range(2):
                    act.wait_ge(s[f"w_loaded{u}"], 16)
                    nc.scalar.copy(w_hi[:, u].rearrange("p k m -> p (k m)"), w_raw[:, u, :]).then_inc(s["w_hi"], 1)
                with act.Fori(0, KT // 2) as i:
                    for u in range(2):
                        t = i * 2 + u
                        act.wait_ge(s["psum_free"], 2 * t + 4)
                        act.wait_ge(s["summed"], t + 1)
                        nc.scalar.activation(z[:, 0, :], x[:, u, :], ACT.Square).then_inc(s["squared"], 1)
                        act.wait_ge(s[f"w_loaded{u}"], 16 * i + 32)
                        act.wait_ge(s["proj_done"], 2 * t + 2)
                        nc.scalar.copy(w_hi[:, u].rearrange("p k m -> p (k m)"), w_raw[:, u, :]).then_inc(s["w_hi"], 1)

            @block.vector
            def _(dve):
                dve.wait_ge(s["small_loaded"], 16)

                def split_y(k):
                    dve.wait_ge(s["y_hi"], k + 1)
                    nc.vector.tensor_tensor(y_lo[:, k, :], x[:, k % 2, :], y_hi[:, k, :].bitcast(F32),
                                            ALU.subtract).then_inc(s["y_lo"], 1)

                for k in range(KT):
                    dve.wait_ge(s[f"x_loaded{k % 2}"], 32 * (k // 2 + 1))
                    dve.wait_ge(s["r_loaded0"], 32 * (k + 1))
                    if k < DN_HEADS:
                        nc.vector.scalar_tensor_tensor(out=x[:, k % 2, :], in0=x[:, k % 2, :], scalar=norm[:, 0:1],
                                                       in1=r[:, 0, :], op0=ALU.mult, op1=ALU.mult).then_inc(s["scaled"], 1)
                    else:
                        nc.vector.tensor_tensor(x[:, k % 2, :], x[:, k % 2, :], r[:, 0, :], ALU.mult).then_inc(s["scaled"], 1)
                    dve.wait_ge(s["scaled"], k + 1)
                    dve.wait_ge(s["z_loaded0"], 16 * (k + 1))
                    nc.vector.tensor_tensor(x[:, k % 2, :], x[:, k % 2, :], z[:, 0, :], ALU.mult).then_inc(s["gated"], 1)
                    if k:
                        split_y(k - 1)
                split_y(KT - 1)

                def split_w(u):
                    nc.vector.tensor_tensor(w_lo[:, u].rearrange("p k m -> p (k m)"), w_raw[:, u, :],
                                            w_hi[:, u].rearrange("p k m -> p (k m)").bitcast(F32),
                                            ALU.subtract).then_inc(s["w_lo"], 1)

                for u in range(2):
                    dve.wait_ge(s["w_hi"], u + 1)
                    split_w(u)
                nc.vector.memset(acc[:], 0.0).then_inc(s["summed"], 1)
                with dve.Fori(0, KT // 2) as i:
                    for u in range(2):
                        t = i * 2 + u
                        dve.wait_ge(s[f"xr_loaded{u}"], 16 * i + 16)
                        for half in range(2):
                            dve.wait_ge(s["proj_done"], 2 * t + half + 1)
                            xs = x[:, u, half * HALF:(half + 1) * HALF]
                            nc.vector.tensor_tensor(xs, ps[:, 2 * half:2 * half + 2, :].rearrange("p b n -> p (b n)"), xs,
                                                    ALU.add).then_inc(s["psum_free"], 1)
                        dve.wait_ge(s["squared"], t + 1)
                        dve.wait_ge(s["summed"], t + 1)
                        nc.vector.tensor_tensor(acc[:], acc[:], z[:, 0, :], ALU.add).then_inc(s["summed"], 1)
                        dve.wait_ge(s["w_hi"], t + 3)
                        split_w(u)


def layer_rest(nc, a, c, l):
    if PHASES >= 2:
        token_tables(nc, a, c, l)
        attention_inputs(nc, a, c, l)
    if PHASES >= 3:
        delta_net(nc, a, c, l)
    if PHASES >= 4:
        attention(nc, a, c, l)
    if PHASES >= 5:
        branch_scales(nc, a, c, l)
        with ExitStack() as stack:
            c.sq_acc = stack.enter_context(nc.sbuf_tensor("sq_acc", [P, SEQ], F32))
            output_projection(nc, a, c, l)
            token_scales(nc, a, c, "layer")


def finish(nc, a, c):
    with ExitStack() as stack, semaphores(nc, "const_loaded x_loaded0 x_loaded1 normed stored0 stored1 passed") as s:
        b = Buffers(nc, stack, "fin")
        x = b.sbuf("x", [P, 2, SEQ])
        r = b.sbuf("r", [P, SEQ])
        w = b.sbuf("w", [P, KT])
        with nc.Block() as block:

            @block.sync
            def _(sp):
                sp.dma_start(w[:], a.norm_w[DEPTH]).then_inc(s["const_loaded"], 16)
                sp.dma_start(r[:], a.x_scale.partition_broadcast(P)).then_inc(s["const_loaded"], 16)
                for k in range(KT):
                    if k >= 2:
                        sp.wait_ge(s[f"stored{k % 2}"], 16 * (k // 2))
                    sp.dma_start(x[:, k % 2, :], a.x_res[k]).then_inc(s[f"x_loaded{k % 2}"], 16)

            @block.vector
            def _(dve):
                dve.wait_ge(s["const_loaded"], 32)
                for k in range(KT):
                    dve.wait_ge(s[f"x_loaded{k % 2}"], 16 * (k // 2 + 1))
                    nc.vector.scalar_tensor_tensor(out=x[:, k % 2, :], in0=x[:, k % 2, :], scalar=w[:, k:k + 1],
                                                   in1=r[:], op0=ALU.mult, op1=ALU.mult).then_inc(s["normed"], 1)

            @block.scalar
            def _(act):
                for k in range(KT):
                    act.wait_ge(s["normed"], k + 1)
                    act.dma_start(a.out[k], x[:, k % 2, :]).then_inc(s[f"stored{k % 2}"], 16)
                for u in range(2):
                    act.wait_ge(s[f"stored{u}"], 16 * (KT // 2))


class Arrays:
    pass


def constants():
    f = np.float32
    i = np.arange(P)
    j, t = i[:, None], i[None, :]
    masks = np.zeros((P, N_DIR, LEVELS + 1, P), f)
    for lv in range(LEVELS):
        s = 1 << lv
        upper = (j // (2 * s) == t // (2 * s)) & (j // s < t // s)
        masks[:, 0, lv] = upper
        masks[:, 1, lv] = upper.T
    masks[:, 0, LEVELS] = j <= t
    masks[:, 1, LEVELS] = j >= t
    masks[:, :, 0] *= -1
    ind = np.zeros((P, 2), f)
    ind[:DH, 0] = 1
    ind[DH:, 1] = 1
    half = DH // 2
    inv = (f(10000.0) ** (-np.arange(0, half, 2, dtype=f) / f(half))).astype(f)
    tok = np.arange(SEQ)
    ang = np.zeros((P, SEQ), f)
    sign = np.zeros((P, 1))
    for p in range(P):
        d = p % DH
        pos = (tok // DH if d < half else tok % DH).astype(f)
        ang[p] = pos * inv[d % (half // 2)]
        sign[p] = -1 if d % half < half // 2 else 1
    cos = np.cos(ang.astype(np.float64)).astype(f)
    sin = (sign * np.sin(ang.astype(np.float64))).astype(f)
    quarter = np.zeros((NQ, NQ, 1), f)
    quarter[np.arange(NQ), np.arange(NQ)] = 1
    return {"masks": masks, "ident": np.eye(P, dtype=f), "ones": np.ones((P, P), f), "halves": ind,
            "rope": np.stack([cos, sin]), "quarter": np.ascontiguousarray(np.broadcast_to(quarter, (NQ, NQ, P)))}


PHASES = 99


def build(nc, a):
    c = Arrays()
    dram = lambda n, shape, dt=F32: nc.dram_tensor(n, shape, dt, kind="Internal").ap()
    a.x_res = dram("x_res", (KT, P, SEQ))
    a.x_scale = dram("x_scale", (SEQ,))
    a.ba = dram("ba", (2 * W_BA, SEQ))
    a.proj = dram("proj", (N_TILES, P, SEQ))
    scratch(a, dram)
    with ExitStack() as stack:
        sb = lambda n, shape: stack.enter_context(nc.sbuf_tensor(n, shape, F32))
        c.ident = sb("c_ident", [P, P])
        c.ones = sb("c_ones", [P, P])
        c.eps = sb("c_eps", [P, 2])
        c.halves = sb("c_halves", [P, 2])
        c.sums = sb("c_sums", [P, T_Z - T_Q, NC, 2])
        c.tok = sb("c_tok", [P, NC, TABLES, ITEMS])
        c.v_scale = sb("c_v_scale", [P, NC, DN_HEADS])
        c.q_eps = sb("c_q_eps", [P, DN_HEADS, NC])
        c.sq_acc = None
        with semaphores(nc, "loaded set_up") as s:
            with nc.Block() as block:
                @block.sync
                def _(sp):
                    sp.dma_start(c.ident[:], a.ident).then_inc(s["loaded"], 16)
                    sp.dma_start(c.ones[:], a.ones).then_inc(s["loaded"], 16)
                    sp.dma_start(c.halves[:], a.halves).then_inc(s["loaded"], 16)
                    sp.wait_ge(s["loaded"], 48)

                @block.vector
                def _(dve):
                    nc.vector.memset(c.eps[:], EPS).then_inc(s["set_up"], 1)
        with ExitStack() as inner:
            c.sq_acc = inner.enter_context(nc.sbuf_tensor("sq_acc_in", [P, SEQ], F32))
            load_input(nc, a, c)
            token_scales(nc, a, c, "input")
        with nc.Fori(0, DEPTH) as l:
            if PHASES >= 1:
                input_projection(nc, a, c, l)
            layer_rest(nc, a, c, l)
        finish(nc, a, c)


_SHAPES = ["x_in", "w_in", "w_ba", "norm_w", "decay", "dn_norm_w", "qk_norm_w", "w_out",
           "masks", "ident", "ones", "halves", "rope", "quarter"]


def lay_out(x, norm_w, w_in, conv_w, a_log, dt_bias, dn_norm_w, q_norm_w, k_norm_w, w_out, final_norm_w):
    depth = w_in.shape[0]
    g = {"x_in": np.asarray(x)[0].T.reshape(KT, P, SEQ)}
    w = np.asarray(w_in)
    conv = DN_HEADS * P
    at_z = 3 * conv
    at_ba = at_z + conv
    at_q = at_ba + W_BA
    at_v = at_q + ATT_HEADS * DH + KV_HEADS * DH
    at_gate = at_v + KV_HEADS * DH
    order = np.concatenate([np.arange(2 * conv, 3 * conv), np.arange(0, 2 * conv), np.arange(at_q, at_gate),
                            np.arange(at_z, at_ba), np.arange(at_gate, w.shape[2])])
    tiles = w[:, :, order].reshape(depth, KT, P, N_TILES, P).transpose(0, 3, 2, 1, 4).reshape(depth, N_TILES, P, KT * P)
    taps = np.zeros((depth, N_TILES, P, WCOLS - KT * P), w.dtype)
    conv_order = order[:CONV_TILES * P]
    taps[:, :CONV_TILES, :, :CONV_K] = np.asarray(conv_w)[:, :, conv_order].reshape(
        depth, CONV_K, CONV_TILES, P).transpose(0, 2, 3, 1)
    g["w_in"] = np.concatenate([tiles, taps], axis=3)
    g["w_ba"] = w[:, :, at_ba:at_q].reshape(depth, KT, P, W_BA).transpose(0, 2, 1, 3)
    norms = np.concatenate([np.asarray(norm_w), np.asarray(final_norm_w)[None]])
    g["norm_w"] = norms.reshape(depth + 1, KT, P).transpose(0, 2, 1)
    g["decay"] = np.stack([np.asarray(a_log).reshape(depth, ITEMS), np.asarray(dt_bias).reshape(depth, ITEMS)], axis=1)
    g["dn_norm_w"] = np.asarray(dn_norm_w)[:, :, None]
    swap = np.arange(DH).reshape(4, DH // 4)[[1, 0, 3, 2]].reshape(-1)
    q, k = np.asarray(q_norm_w), np.asarray(k_norm_w)
    g["qk_norm_w"] = np.stack([np.concatenate([v, v], axis=1) for v in (q, q[:, swap], k, k[:, swap])], axis=2)
    g["w_out"] = np.asarray(w_out).reshape(depth, KT, P, KT, P).transpose(0, 3, 2, 1, 4).reshape(depth, KT, P, KT * P)
    g.update(constants())
    return {n: np.ascontiguousarray(v) for n, v in g.items()}


def kernel(**inputs):
    import concourse.bacc as bacc
    from concourse.bass_utils import run_bass_kernel_spmd

    nc = bacc.Bacc("TRN2", target_bir_lowering=False, num_devices=1)
    g = lay_out(**inputs)
    a, arrays = Arrays(), {}
    a_dict = a.__dict__
    for name in _SHAPES:
        arrays[f"in_{name}"] = g[name]
        a_dict[name] = nc.dram_tensor(f"in_{name}", g[name].shape, mybir.dt.from_np(g[name].dtype),
                                      kind="ExternalInput").ap()
    a.out = nc.dram_tensor("out_T", (KT, P, SEQ), F32, kind="ExternalOutput").ap()
    build(nc, a)
    r = run_bass_kernel_spmd(nc, [arrays], core_ids=[0])
    out = r.results[0]["out_T"]
    return np.ascontiguousarray(out.reshape(D_MODEL, SEQ).T)[None]
```

```python
from contextlib import ExitStack, contextmanager

import numpy as np

import concourse.bass as bass
from concourse import mybir

P = 128
F32 = mybir.dt.float32
F32R = mybir.dt.float32r
ALU = mybir.AluOpType
ACT = mybir.ActivationFunctionType
AX = mybir.AxisListType

SEQ = 2048
D_MODEL = 1024
DEPTH = 2
KT = D_MODEL // P
NC = SEQ // P
QB = 512
NQ = SEQ // QB
HALF = SEQ // 2
CONV_K = 5
PADW = SEQ + CONV_K - 1
EPS = 1e-6

DN_HEADS = 4
N_DIR = 2
ITEMS = N_DIR * DN_HEADS
ATT_HEADS = 8
KV_HEADS = 2
GROUP = ATT_HEADS // KV_HEADS
DH = 64
SCALE = float(DH) ** -0.5
LEVELS = 7

CONV_TILES = 3 * DN_HEADS
T_V, T_Q, T_K = 0, DN_HEADS, 2 * DN_HEADS
T_AQ = CONV_TILES
T_AK = T_AQ + ATT_HEADS // 2
T_AV = T_AK + 1
T_Z = T_AV + 1
N_TILES = T_Z + 8
WCOLS = KT * P + 8
W_BA = 2 * ITEMS


@contextmanager
def semaphores(nc, names):
    with ExitStack() as stack:
        sems = {n: stack.enter_context(nc.semaphore(n)) for n in names.split()}
        yield sems
        for s in sems.values():
            nc.sync.sem_clear(s)
        nc.all_engine_barrier()


class Buffers:

    def __init__(self, nc, stack, phase):
        self.nc, self.stack, self.phase = nc, stack, phase

    def sbuf(self, name, shape, dtype=F32):
        return self.stack.enter_context(self.nc.sbuf_tensor(f"{self.phase}_sb_{name}", shape, dtype))

    def banks(self):
        return self.stack.enter_context(self.nc.psum_tensor(f"{self.phase}_banks", [P, 8, QB], F32))


def wait_in_loop(sp, s, name, value):
    sp.wait_ge(s[name], value)
    sp.sem_inc(s["passed"], 1)


def load_input(nc, a, c):
    with ExitStack() as stack, semaphores(nc, "x_loaded0 x_loaded1 x_stored0 x_stored1 squared summed passed") as s:
        b = Buffers(nc, stack, "load")
        x = b.sbuf("x", [P, 2, SEQ])
        sq = b.sbuf("sq", [P, 2, SEQ])
        acc = c.sq_acc
        with nc.Block() as block:

            @block.sync
            def _(sp):
                with sp.Fori(0, KT // 2) as i:
                    for u in range(2):
                        wait_in_loop(sp, s, "squared", 2 * i)
                        wait_in_loop(sp, s, f"x_stored{u}", 16 * i)
                        sp.dma_start(x[:, u, :], a.x_in[i * 2 + u]).then_inc(s[f"x_loaded{u}"], 16)
                    for u in range(2):
                        wait_in_loop(sp, s, f"x_loaded{u}", 16 * i + 16)
                        sp.dma_start(a.x_res[i * 2 + u], x[:, u, :]).then_inc(s[f"x_stored{u}"], 16)
                for u in range(2):
                    sp.wait_ge(s[f"x_stored{u}"], KT // 2 * 16)

            @block.scalar
            def _(act):
                with act.Fori(0, KT // 2) as i:
                    for u in range(2):
                        act.wait_ge(s[f"x_loaded{u}"], 16 * i + 16)
                        act.wait_ge(s["summed"], 2 * i + u)
                        nc.scalar.activation(sq[:, u, :], x[:, u, :], ACT.Square).then_inc(s["squared"], 1)

            @block.vector
            def _(dve):
                nc.vector.memset(acc[:], 0.0).then_inc(s["summed"], 1)
                with dve.Fori(0, KT // 2) as i:
                    for u in range(2):
                        dve.wait_ge(s["squared"], 2 * i + u + 1)
                        dve.wait_ge(s["summed"], 2 * i + u + 1)
                        nc.vector.tensor_tensor(acc[:], acc[:], sq[:, u, :], ALU.add).then_inc(s["summed"], 1)


def token_scales(nc, a, c, when):
    with ExitStack() as stack, semaphores(nc, "sums root scale turned copied stored") as s:
        b = Buffers(nc, stack, "scales_" + when)
        table = b.sbuf("table", [P, NC])
        inv = b.sbuf("inv", [P, NC])
        rows = b.sbuf("rows", [NC, P])
        ps = b.banks()
        with nc.Block() as block:

            @block.tensor
            def _(pe):
                for t in range(NC):
                    mm = nc.tensor.matmul(ps[:, 0, t:t + 1], c.sq_acc[:, t * P:(t + 1) * P], c.ones[:, 0:1],
                                          start=True, stop=True)
                mm.then_inc(s["sums"], 1)
                pe.wait_ge(s["scale"], 1)
                nc.tensor.transpose(ps[0:NC, 1, 0:P], inv[:], c.ident[:]).then_inc(s["turned"], 1)

            @block.scalar
            def _(act):
                act.wait_ge(s["sums"], 1)
                nc.scalar.activation(table[:], ps[:, 0, 0:NC], ACT.Sqrt, bias=c.eps[:, 0:1],
                                     scale=1.0 / D_MODEL).then_inc(s["root"], 1)

            @block.vector
            def _(dve):
                dve.wait_ge(s["root"], 1)
                nc.vector.reciprocal(inv[:], table[:]).then_inc(s["scale"], 1)
                dve.wait_ge(s["turned"], 1)
                nc.vector.tensor_copy(rows[:], ps[0:NC, 1, 0:P]).then_inc(s["copied"], 1)

            @block.sync
            def _(sp):
                sp.wait_ge(s["copied"], 1)
                sp.dma_start(a.x_scale.rearrange("(c p) -> c p", p=P), rows[:]).then_inc(s["stored"], 16)
                sp.wait_ge(s["stored"], 16)


def input_projection(nc, a, c, l):
    names = ("x_loaded0 x_loaded1 scale_loaded small_loaded normed h_hi h_lo w_loaded0 w_loaded1 w_hi w_lo "
             "proj_done psum_free passed "
             "conv_step taps_kept conv_done out_ready out_stored0 out_stored1 ba_hi ba_split ba_stored edges "
             "squared stats_done")
    with ExitStack() as stack, semaphores(nc, names) as s:
        b = Buffers(nc, stack, "proj")
        h_hi = b.sbuf("h_hi", [P, KT, SEQ], F32R)
        h_lo = b.sbuf("h_lo", [P, KT, SEQ], F32R)
        pad = b.sbuf("pad", [P, 2, PADW])
        out = b.sbuf("out", [P, 2, SEQ])
        w_raw = b.sbuf("w_raw", [P, 2, WCOLS])
        w_hi = b.sbuf("w_hi", [P, 2, KT, P], F32R)
        w_lo = b.sbuf("w_lo", [P, 2, KT, P], F32R)
        nw = b.sbuf("nw", [P, KT])
        sq = b.sbuf("sq", [P, SEQ])
        taps = b.sbuf("taps", [P, 2, WCOLS - KT * P])
        ba_raw = b.sbuf("ba_raw", [P, KT, W_BA])
        ba_w = b.sbuf("ba_w", [P, KT, 2 * W_BA], F32R)
        ps = b.banks()
        scale = out[:, 1, :]

        with nc.Block() as block:

            @block.sync
            def _(sp):
                sp.dma_start(nw[:], a.norm_w[l]).then_inc(s["small_loaded"], 16)
                sp.dma_start(ba_raw[:], a.w_ba[l]).then_inc(s["small_loaded"], 16)
                sp.dma_start(scale, a.x_scale.partition_broadcast(P)).then_inc(s["scale_loaded"], 16)
                for k in range(KT):
                    if k >= 2:
                        sp.wait_ge(s["h_lo"], k - 1)
                    sp.dma_start(pad[:, k % 2, 0:SEQ], a.x_res[k]).then_inc(s[f"x_loaded{k % 2}"], 16)
                    if k < 2:
                        sp.dma_start(w_raw[:, k, :], a.w_in[l, k]).then_inc(s[f"w_loaded{k}"], 16)
                sp.wait_ge(s["out_ready"], 1)
                sp.dma_start(a.ba, out[0:2 * W_BA, 0, :]).then_inc(s["ba_stored"], 16)
                sp.wait_ge(s["ba_stored"], 16)
                for u in range(2):
                    sp.sem_inc(s[f"out_stored{u}"], 16)
                with sp.Fori(0, N_TILES // 2 - 1) as i:
                    for u in range(2):
                        t = i * 2 + u
                        wait_in_loop(sp, s, "w_lo", t + 1)
                        sp.dma_start(w_raw[:, u, :], a.w_in[l, t + 2]).then_inc(s[f"w_loaded{u}"], 16)
                        wait_in_loop(sp, s, "out_ready", t + 2)
                        sp.dma_start(a.proj[t], out[:, u, :]).then_inc(s[f"out_stored{u}"], 16)
                for u in range(2):
                    t = N_TILES - 2 + u
                    sp.wait_ge(s["out_ready"], t + 2)
                    sp.dma_start(a.proj[t], out[:, u, :]).then_inc(s[f"out_stored{u}"], 16)
                for u in range(2):
                    sp.wait_ge(s[f"out_stored{u}"], 16 * (N_TILES // 2 + 1))

            @block.tensor
            def _(pe):
                pe.wait_ge(s["ba_split"], 2)
                pe.wait_ge(s["w_hi"], 1)
                pe.wait_ge(s["w_lo"], 1)
                for k in range(KT):
                    pe.wait_ge(s["h_lo"], k + 1)
                    for part, h in enumerate((h_hi, h_lo)):
                        for n in range(NQ):
                            mm = nc.tensor.matmul(ps[0:2 * W_BA, 4 + n, :], ba_w[:, k, :],
                                                  h[:, k, n * QB:(n + 1) * QB],
                                                  start=(k == 0 and part == 0), stop=(k == KT - 1 and part == 1))
                    if k == KT - 1:
                        mm.then_inc(s["proj_done"], 2)
                    for w, h in ((w_hi, h_hi), (w_hi, h_lo), (w_lo, h_hi)):
                        for n in range(NQ):
                            mm = nc.tensor.matmul(ps[:, n, :], w[:, 0, k, :], h[:, k, n * QB:(n + 1) * QB],
                                                  start=(k == 0 and w is w_hi and h is h_hi), stop=(k == KT - 1 and w is w_lo))
                mm.then_inc(s["proj_done"], 2)

                def tile_half(i, u, half, sums=()):
                    t = i * 2 + u
                    pe.wait_ge(s["w_hi"], t + 1)
                    pe.wait_ge(s["w_lo"], t + 1)
                    pe.wait_ge(s["psum_free"], 2 * t + half + 1)
                    between = list(sums)
                    for k in range(KT):
                        for w, h in ((w_hi, h_hi), (w_hi, h_lo), (w_lo, h_hi)):
                            if between:
                                between.pop(0)()
                            for n in range(2):
                                at = half * HALF + n * QB
                                mm = nc.tensor.matmul(
                                    ps[:, 2 * half + n, :], w[:, u, k, :], h[:, k, at:at + QB],
                                    start=(k == 0 and w is w_hi and h is h_hi), stop=(k == KT - 1 and w is w_lo))
                    mm.then_inc(s["proj_done"], 1)

                def square_sum(i, u, n):
                    t = i * 2 + u
                    if n == 0:
                        pe.wait_ge(s["squared"], t + 3)
                    col = (t - T_Q) * 2 * NC + 2 * n
                    mm = nc.tensor.matmul(ps[:, 4, bass.ds(col, 2)], sq[:, n * P:(n + 1) * P], c.halves[:],
                                          start=True, stop=True)
                    if n == NC - 1:
                        mm.then_inc(s["stats_done"], 1)

                for half in range(2):
                    tile_half(0, 1, half)
                with pe.Fori(1, T_Q // 2 + 1) as i:
                    for u in range(2):
                        for half in range(2):
                            tile_half(i, u, half)
                pe.wait_ge(s["out_ready"], 1)
                with pe.Fori(T_Q // 2 + 1, T_Z // 2 + 1) as i:
                    for u in range(2):
                        tile_half(i, u, 0)
                        tile_half(i, u, 1, [lambda n=n: square_sum(i - 1, u, n) for n in range(NC)])
                with pe.Fori(T_Z // 2 + 1, N_TILES // 2) as i:
                    for u in range(2):
                        for half in range(2):
                            tile_half(i, u, half)

            @block.gpsimd
            def _(pool):
                pool.sem_inc(s["squared"], T_Q + 2)
                with pool.Fori(T_Q // 2, T_Z // 2) as i:
                    for u in range(2):
                        t = i * 2 + u
                        pool.wait_ge(s["out_ready"], t + 2)
                        pool.wait_ge(s["stats_done"], t - T_Q)
                        nc.gpsimd.tensor_tensor(sq[:], out[:, u, :], out[:, u, :], ALU.mult).then_inc(s["squared"], 1)

            @block.scalar
            def _(act):
                act.wait_ge(s["small_loaded"], 32)
                nc.scalar.copy(ba_w[:, :, 0:W_BA], ba_raw[:]).then_inc(s["ba_hi"], 1)
                for k in range(KT):
                    act.wait_ge(s["normed"], k + 1)
                    nc.scalar.copy(h_hi[:, k, :], pad[:, k % 2, 0:SEQ]).then_inc(s["h_hi"], 1)
                    if k == 0:
                        act.wait_ge(s["w_loaded0"], 16)
                        nc.scalar.copy(w_hi[:, 0].rearrange("p k m -> p (k m)"), w_raw[:, 0, 0:KT * P]).then_inc(s["w_hi"], 1)

                def split_hi(t, i, u):
                    act.wait_ge(s[f"w_loaded{u}"], 16 * i + 16)
                    act.wait_ge(s["proj_done"], 2 * t)
                    nc.scalar.copy(w_hi[:, u].rearrange("p k m -> p (k m)"), w_raw[:, u, 0:KT * P]).then_inc(s["w_hi"], 1)

                def evacuate(t, u, half, dst, func):
                    act.wait_ge(s["proj_done"], 2 * t + half + 3)
                    src = ps[:, 2 * half:2 * half + 2, :].rearrange("p b n -> p (b n)")
                    return nc.scalar.activation(dst, src, func)

                act.wait_ge(s["proj_done"], 2)
                nc.scalar.copy(out[0:2 * W_BA, 0, :], ps[0:2 * W_BA, 4:8, :].rearrange("p b n -> p (b n)")) \
                    .then_inc(s["out_ready"], 1)
                act.wait_ge(s["out_ready"], 1)
                act.sem_inc(s["psum_free"], 2)
                with act.Fori(0, CONV_TILES // 2) as i:
                    for u in range(2):
                        t = i * 2 + u
                        split_hi(t + 1, i + u, 1 - u)
                        for half in range(2):
                            lo = CONV_K // 2 + half * HALF
                            act.wait_ge(s["conv_done"], t + 1)
                            evacuate(t, u, half, pad[:, u, lo:lo + HALF], ACT.Copy).then_inc(s["psum_free"], 1)
                        act.wait_ge(s["conv_done"], t + 3)
                        nc.scalar.activation(out[:, u, :], out[:, u, :], ACT.Silu).then_inc(s["out_ready"], 1)

                def plain(i, u, func, more, squares=False):
                    t = i * 2 + u
                    if more:
                        split_hi(t + 1, i + u, 1 - u)
                    act.wait_ge(s[f"out_stored{u}"], 16 * i + 16)
                    if squares:
                        act.wait_ge(s["squared"], t + 1)
                    for half in range(2):
                        e = evacuate(t, u, half, out[:, u, half * HALF:(half + 1) * HALF], func)
                        e.then_inc(s["psum_free"], 1)
                    act.wait_ge(s["psum_free"], 2 * t + 4)
                    act.sem_inc(s["out_ready"], 1)

                with act.Fori(T_AQ // 2, T_Z // 2) as i:
                    for u in range(2):
                        plain(i, u, ACT.Copy, True, True)
                for u in range(2):
                    plain(T_Z // 2, u, ACT.Silu, True, True)
                with act.Fori(T_Z // 2 + 1, N_TILES // 2 - 1) as i:
                    for u in range(2):
                        plain(i, u, ACT.Silu, True)
                plain(N_TILES // 2 - 1, 0, ACT.Silu, True)
                plain(N_TILES // 2 - 1, 1, ACT.Silu, False)

            @block.vector
            def _(dve):
                dve.wait_ge(s["scale_loaded"], 16)
                dve.wait_ge(s["small_loaded"], 32)

                def split_h(k):
                    dve.wait_ge(s["h_hi"], k + 1)
                    nc.vector.tensor_tensor(h_lo[:, k, :], pad[:, k % 2, 0:SEQ], h_hi[:, k, :].bitcast(F32),
                                            ALU.subtract).then_inc(s["h_lo"], 1)

                def keep_taps(t, i, u):
                    dve.wait_ge(s[f"w_loaded{u}"], 16 * i + 16)
                    nc.vector.tensor_copy(taps[:, u, :], w_raw[:, u, KT * P:WCOLS]).then_inc(s["taps_kept"], 1)

                def split_w(t, u):
                    dve.wait_ge(s["w_hi"], t + 1)
                    nc.vector.tensor_tensor(w_lo[:, u].rearrange("p k m -> p (k m)"), w_raw[:, u, 0:KT * P],
                                            w_hi[:, u].rearrange("p k m -> p (k m)").bitcast(F32),
                                            ALU.subtract).then_inc(s["w_lo"], 1)

                for k in range(KT):
                    dve.wait_ge(s[f"x_loaded{k % 2}"], 16 * (k // 2) + 16)
                    nc.vector.scalar_tensor_tensor(out=pad[:, k % 2, 0:SEQ], in0=pad[:, k % 2, 0:SEQ],
                                                   scalar=nw[:, k:k + 1], in1=scale, op0=ALU.mult,
                                                   op1=ALU.mult).then_inc(s["normed"], 1)
                    if k >= 1:
                        split_h(k - 1)
                    if k == 1:
                        keep_taps(0, 0, 0)
                        split_w(0, 0)
                        dve.wait_ge(s["ba_hi"], 1)
                        nc.vector.tensor_tensor(ba_w[:, :, W_BA:2 * W_BA], ba_raw[:],
                                                ba_w[:, :, 0:W_BA].bitcast(F32), ALU.subtract).then_inc(s["ba_split"], 2)
                split_h(KT - 1)
                dve.wait_ge(s["h_lo"], KT)
                nc.vector.memset(pad[:, :, 0:CONV_K // 2], 0.0).then_inc(s["edges"], 1)
                nc.vector.memset(pad[:, :, PADW - CONV_K // 2:PADW], 0.0).then_inc(s["edges"], 1)
                dve.wait_ge(s["edges"], 2)
                dve.sem_inc(s["conv_done"], 2)
                with dve.Fori(0, CONV_TILES // 2) as i:
                    for u in range(2):
                        t = i * 2 + u
                        dve.wait_ge(s["conv_done"], t + 2)
                        keep_taps(t + 1, i + u, 1 - u)
                        split_w(t + 1, 1 - u)
                        dve.wait_ge(s["psum_free"], 2 * t + 4)
                        dve.wait_ge(s["squared"], t + 1)
                        dve.wait_ge(s[f"out_stored{u}"], 16 * i + 16)
                        dve.wait_ge(s["taps_kept"], t + 1)
                        for j in range(CONV_K):
                            if j:
                                dve.wait_ge(s["conv_step"], t * (CONV_K - 1) + j)
                            src = pad[:, u, j:j + SEQ]
                            done = s["conv_step"] if j < CONV_K - 1 else s["conv_done"]
                            if j == 0:
                                nc.vector.tensor_scalar(out[:, u, :], src, taps[:, u, j:j + 1], None, ALU.mult).then_inc(done, 1)
                            else:
                                nc.vector.scalar_tensor_tensor(out=out[:, u, :], in0=src, scalar=taps[:, u, j:j + 1],
                                                               in1=out[:, u, :], op0=ALU.mult, op1=ALU.add).then_inc(done, 1)
                with dve.Fori(CONV_TILES // 2, N_TILES // 2 - 1) as i:
                    for u in range(2):
                        split_w(i * 2 + u + 1, 1 - u)
                split_w(N_TILES - 1, 1)
                dve.wait_ge(s["stats_done"], T_Z - T_Q)
                nc.vector.tensor_copy(c.sums[:].rearrange("p t c h -> p (t c h)"),
                                      ps[:, 4, 0:(T_Z - T_Q) * 2 * NC]).then_inc(s["edges"], 1)
TABLES = 5
T_G, T_NEG, T_BETA, T_BETA_END, T_CHUNK = range(TABLES)
DN_D = P
N_QK = ATT_HEADS // 2 + 1


def scratch(a, dram):
    a.g_rows = dram("g_rows", (NC, ITEMS, P))
    a.qk_rows = dram("qk_rows", (N_QK * 2, SEQ))
    a.att_q = dram("att_q", (ATT_HEADS, P, SEQ))
    a.att_k = dram("att_k", (KV_HEADS, P, SEQ))
    a.att_v = dram("att_v", (P, NC, KV_HEADS, DH))
    a.dn_o = dram("dn_o", (DN_HEADS, P, SEQ))
    a.att_o = dram("att_o", (ATT_HEADS, DH + 1, SEQ))
    a.den_rows = dram("den_rows", (ATT_HEADS, SEQ))
    a.o_rows = dram("o_rows", (DN_HEADS, SEQ))


def token_tables(nc, a, c, l):
    names = ("loaded ba_turned act_step dve_step summed g_copied turned copied stored att_root")
    n_ba = 2 * ITEMS
    with ExitStack() as stack, semaphores(nc, names) as s:
        b = Buffers(nc, stack, "tab")
        ba = b.sbuf("ba", [2 * W_BA, SEQ])
        masks = b.sbuf("masks", [P, N_DIR, P])
        decay = b.sbuf("decay", [P, 2, ITEMS])
        x = b.sbuf("x", [P, NC, n_ba])
        low = b.sbuf("low", [P, NC, n_ba])
        beta = b.sbuf("beta", [P, NC, ITEMS])
        pos = b.sbuf("pos", [P, NC, ITEMS])
        mag = b.sbuf("mag", [P, NC, ITEMS])
        e = b.sbuf("e", [P, NC, ITEMS])
        u = b.sbuf("u", [P, NC, ITEMS])
        ln = b.sbuf("ln", [P, NC, ITEMS])
        inv = b.sbuf("inv", [P, NC, ITEMS])
        g = b.sbuf("g", [P, NC, ITEMS])
        rate = b.sbuf("rate", [P, ITEMS])
        end = b.sbuf("end", [P, NC, ITEMS])
        kk = b.sbuf("kk", [P, DN_HEADS, NC])
        rk2 = b.sbuf("rk2", [P, DN_HEADS, NC])
        att = b.sbuf("att", [P, N_QK, 2, NC])
        att_inv = b.sbuf("att_inv", [P, N_QK * 2 * NC])
        rows = b.sbuf("rows", [P, 3, P])
        ps = b.banks()
        n_att = N_QK * 2 * NC
        with nc.Block() as block:

            @block.sync
            def _(sp):
                sp.dma_start(ba[:], a.ba).then_inc(s["loaded"], 16)
                sp.dma_start(masks[:], a.masks[:, :, LEVELS, :]).then_inc(s["loaded"], 16)
                sp.dma_start(decay[:], a.decay[l].partition_broadcast(P)).then_inc(s["loaded"], 16)
                sp.wait_ge(s["copied"], 1)
                sp.dma_start(a.g_rows.rearrange("c i t -> (c i) t"), rows[:, 0, :]).then_inc(s["stored"], 16)
                sp.wait_ge(s["copied"], 3)
                qk = a.qk_rows.rearrange("r (c p) -> (r c) p", p=P)
                sp.dma_start(qk[0:P], rows[:, 1, :]).then_inc(s["stored"], 16)
                sp.dma_start(qk[P:n_att], rows[0:n_att - P, 2, :]).then_inc(s["stored"], 16)
                sp.wait_ge(s["stored"], 48)

            @block.tensor
            def _(pe):
                pe.wait_ge(s["loaded"], 48)
                for n in range(NC):
                    mm = nc.tensor.transpose(ps[:, 0, n * 2 * W_BA:(n + 1) * 2 * W_BA], ba[:, n * P:(n + 1) * P],
                                             c.ident[0:2 * W_BA, 0:2 * W_BA])
                mm.then_inc(s["ba_turned"], 1)
                pe.wait_ge(s["dve_step"], 11)
                for d in range(N_DIR):
                    h = slice(d * DN_HEADS, (d + 1) * DN_HEADS)
                    nc.tensor.matmul(ps[:, 1 + d, 0:NC * DN_HEADS], masks[:, d, :], g[:, :, h], start=True, stop=True)
                nc.tensor.matmul(ps[:, 3, 0:NC * ITEMS], c.ones[:], g[:].rearrange("p c i -> p (c i)"),
                                 start=True, stop=True).then_inc(s["summed"], 1)
                pe.wait_ge(s["g_copied"], 2)
                nc.tensor.transpose(ps[:, 4, 0:P], e[:].rearrange("p c i -> p (c i)"), c.ident[:]).then_inc(s["turned"], 1)
                pe.wait_ge(s["att_root"], 2)
                nc.tensor.transpose(ps[:, 5, 0:P], att_inv[:, 0:P], c.ident[:])
                nc.tensor.transpose(ps[0:n_att - P, 6, 0:P], att_inv[:, P:n_att], c.ident[:]).then_inc(s["turned"], 1)

            @block.scalar
            def _(act):
                act.wait_ge(s["loaded"], 48)
                nc.scalar.activation(rate[:], decay[:, 0, :], ACT.Exp).then_inc(s["act_step"], 1)
                act.wait_ge(s["dve_step"], 2)
                nc.scalar.activation(beta[:], x[:, :, 0:ITEMS], ACT.Exp, scale=-1.0).then_inc(s["act_step"], 1)
                act.wait_ge(s["dve_step"], 5)
                nc.scalar.activation(e[:], mag[:], ACT.Exp, scale=-1.0).then_inc(s["act_step"], 1)
                act.wait_ge(s["dve_step"], 6)
                nc.scalar.activation(ln[:], u[:], ACT.Ln).then_inc(s["act_step"], 1)
                act.wait_ge(s["g_copied"], 3)
                nc.scalar.activation(c.tok[:, :, T_NEG, :], e[:], ACT.Exp).then_inc(s["act_step"], 1)
                nc.scalar.activation(c.tok[:, :, T_CHUNK, :], mag[:], ACT.Exp).then_inc(s["act_step"], 1)
                nc.scalar.activation(end[:], pos[:], ACT.Exp).then_inc(s["act_step"], 1)
                act.wait_ge(s["dve_step"], 12)
                nc.scalar.activation(c.v_scale[:], kk[:].rearrange("p h c -> p c h"), ACT.Sqrt).then_inc(s["act_step"], 1)
                first = T_AQ - T_Q
                nc.scalar.activation(att[:].rearrange("p t h c -> p t c h"), c.sums[:, first:first + N_QK], ACT.Sqrt,
                                     bias=c.eps[:, 0:1], scale=1.0 / DH).then_inc(s["att_root"], 1)

            @block.vector
            def _(dve):
                step = s["dve_step"]
                dve.wait_ge(s["ba_turned"], 1)
                parts = ps[:, 0, :].rearrange("p (c w) -> p c w", w=2 * W_BA)
                nc.vector.tensor_copy(low[:], parts[:, :, W_BA:2 * W_BA]).then_inc(step, 1)
                dve.wait_ge(step, 1)
                nc.vector.tensor_tensor(x[:], parts[:, :, 0:W_BA], low[:], ALU.add).then_inc(step, 1)
                dve.wait_ge(step, 2)
                bias = decay[:, 1, :].unsqueeze(1).broadcast_to([P, NC, ITEMS])
                nc.vector.tensor_tensor(u[:], x[:, :, ITEMS:n_ba], bias, ALU.add).then_inc(step, 1)
                dve.wait_ge(step, 3)
                nc.vector.tensor_scalar(pos[:], u[:], 0.0, None, ALU.max).then_inc(step, 1)
                nc.vector.scalar_tensor_tensor(out=mag[:], in0=u[:], scalar=-1.0, in1=u[:], op0=ALU.mult,
                                               op1=ALU.max).then_inc(step, 1)
                dve.wait_ge(s["act_step"], 3)
                dve.wait_ge(step, 5)
                nc.vector.tensor_scalar(u[:], e[:], 1.0, None, ALU.add).then_inc(step, 1)
                dve.wait_ge(step, 6)
                nc.vector.scalar_tensor_tensor(out=g[:], in0=u[:], scalar=-1.0, in1=e[:], op0=ALU.add,
                                               op1=ALU.subtract).then_inc(step, 1)
                nc.vector.reciprocal(inv[:], u[:]).then_inc(step, 1)
                dve.wait_ge(step, 8)
                nc.vector.tensor_tensor(g[:], g[:], inv[:], ALU.mult).then_inc(step, 1)
                dve.wait_ge(step, 9)
                dve.wait_ge(s["act_step"], 4)
                nc.vector.tensor_tensor(ln[:], ln[:], g[:], ALU.subtract).then_inc(s["g_copied"], 1)
                dve.wait_ge(s["g_copied"], 1)
                nc.vector.scalar_tensor_tensor(out=ln[:], in0=ln[:], scalar=1.0, in1=pos[:], op0=ALU.mult,
                                               op1=ALU.add).then_inc(step, 1)
                dve.wait_ge(step, 10)
                nc.vector.scalar_tensor_tensor(out=g[:], in0=ln[:], scalar=-1.0,
                                               in1=rate[:].unsqueeze(1).broadcast_to([P, NC, ITEMS]),
                                               op0=ALU.mult, op1=ALU.mult).then_inc(step, 1)
                k0 = T_K - T_Q
                nc.vector.scalar_tensor_tensor(out=kk[:], in0=c.sums[:, k0:k0 + DN_HEADS, :, 0], scalar=EPS,
                                               in1=c.sums[:, k0:k0 + DN_HEADS, :, 1], op0=ALU.add, op1=ALU.add).then_inc(step, 1)
                dve.wait_ge(step, 12)
                nc.vector.reciprocal(rk2[:], kk[:]).then_inc(step, 1)
                nc.vector.scalar_tensor_tensor(out=c.q_eps[:], in0=c.sums[:, 0:DN_HEADS, :, 0], scalar=EPS,
                                               in1=c.sums[:, 0:DN_HEADS, :, 1], op0=ALU.add, op1=ALU.add).then_inc(step, 1)
                dve.wait_ge(step, 14)
                nc.vector.tensor_scalar(c.q_eps[:], c.q_eps[:], EPS * DN_D, None, ALU.mult).then_inc(step, 1)
                nc.vector.tensor_scalar(beta[:], beta[:], 1.0, None, ALU.add).then_inc(step, 1)
                dve.wait_ge(step, 16)
                nc.vector.reciprocal(inv[:], beta[:]).then_inc(step, 1)
                dve.wait_ge(step, 17)
                for d in range(N_DIR):
                    h = slice(d * DN_HEADS, (d + 1) * DN_HEADS)
                    nc.vector.tensor_tensor(c.tok[:, :, T_BETA, h], inv[:, :, h], rk2[:].rearrange("p h c -> p c h"),
                                            ALU.mult).then_inc(step, 1)
                dve.wait_ge(s["summed"], 1)
                for d in range(N_DIR):
                    h = slice(d * DN_HEADS, (d + 1) * DN_HEADS)
                    cum = ps[:, 1 + d, 0:NC * DN_HEADS].rearrange("p (c h) -> p c h", h=DN_HEADS)
                    nc.vector.tensor_copy(e[:, :, h], cum).then_inc(step, 1)
                nc.vector.tensor_copy(mag[:], ps[:, 3, 0:NC * ITEMS].rearrange("p (c i) -> p c i", i=ITEMS)).then_inc(step, 1)
                dve.wait_ge(step, 22)
                nc.vector.tensor_copy(c.tok[:, :, T_G, :], e[:]).then_inc(s["g_copied"], 1)
                nc.vector.tensor_tensor(pos[:], mag[:], e[:], ALU.subtract).then_inc(s["g_copied"], 1)
                dve.wait_ge(s["act_step"], 7)
                nc.vector.tensor_scalar(c.tok[:, :, T_NEG, :], c.tok[:, :, T_NEG, :], -1.0, None, ALU.mult).then_inc(step, 1)
                nc.vector.tensor_tensor(c.tok[:, :, T_BETA_END, :], c.tok[:, :, T_BETA, :], end[:], ALU.mult).then_inc(step, 1)
                dve.wait_ge(s["turned"], 1)
                nc.vector.tensor_copy(rows[:, 0, :], ps[:, 4, 0:P]).then_inc(s["copied"], 1)
                dve.wait_ge(s["att_root"], 1)
                nc.vector.reciprocal(att_inv[:], att[:].rearrange("p t h c -> p (t h c)")).then_inc(s["att_root"], 1)
                dve.wait_ge(s["turned"], 2)
                nc.vector.tensor_copy(rows[:, 1, :], ps[:, 5, 0:P]).then_inc(s["copied"], 1)
                nc.vector.tensor_copy(rows[0:n_att - P, 2, :], ps[0:n_att - P, 6, 0:P]).then_inc(s["copied"], 1)


def attention_inputs(nc, a, c, l):
    names = ("const_loaded x_loaded0 x_loaded1 y_loaded0 y_loaded1 r_loaded0 r_loaded1 v_loaded "
             "cos_done sin_done rotated scaled hi lo stored0 stored1 v_turned v_copied v_stored passed")
    with ExitStack() as stack, semaphores(nc, names) as s:
        b = Buffers(nc, stack, "rot")
        rope = b.sbuf("rope", [P, 2, SEQ])
        w = b.sbuf("w", [P, 4])
        x = b.sbuf("x", [P, 2, SEQ])
        y = b.sbuf("y", [P, 2, SEQ])
        r = b.sbuf("r", [P, 2, SEQ])
        hi = b.sbuf("hi", [P, 2, SEQ], F32R)
        lo = b.sbuf("lo", [P, 2, SEQ], F32R)
        v = b.sbuf("v", [P, SEQ])
        vt = b.sbuf("vt", [P, NC, P])
        ps = b.banks()
        quarter = DH // 4
        with nc.Block() as block:

            @block.sync
            def _(sp):
                sp.dma_start(rope[:], a.rope.rearrange("f p n -> p f n")).then_inc(s["const_loaded"], 16)
                sp.dma_start(w[:], a.qk_norm_w[l]).then_inc(s["const_loaded"], 16)
                sp.dma_start(v[:], a.proj[T_AV]).then_inc(s["v_loaded"], 16)
                for t in range(N_QK):
                    u = t % 2
                    if t >= 2:
                        sp.wait_ge(s["lo"], t - 1)
                    src = a.proj[T_AQ + t]
                    sp.dma_start(x[:, u, :], src).then_inc(s[f"x_loaded{u}"], 16)
                    for q in range(0, P // quarter):
                        sp.dma_start(y[q * quarter:(q + 1) * quarter, u, :],
                                     src[(q ^ 1) * quarter:((q ^ 1) + 1) * quarter]).then_inc(s[f"y_loaded{u}"], 16)
                    for half in range(2):
                        sp.dma_start(r[half * DH:(half + 1) * DH, u, :],
                                     a.qk_rows[2 * t + half].partition_broadcast(DH)).then_inc(s[f"r_loaded{u}"], 16)
                    if t == 1:
                        sp.wait_ge(s["v_copied"], NQ)
                        sp.dma_start(a.att_v.rearrange("p c k d -> p c (k d)"), vt[:]).then_inc(s["v_stored"], 16)
                sp.wait_ge(s["v_stored"], 16)

            @block.gpsimd
            def _(pool):
                for t in range(N_QK):
                    u = t % 2
                    pool.wait_ge(s["sin_done"], t + 1)
                    pool.wait_ge(s["cos_done"], t + 1)
                    nc.gpsimd.tensor_tensor(x[:, u, :], x[:, u, :], y[:, u, :], ALU.add).then_inc(s["rotated"], 1)

            @block.tensor
            def _(pe):
                pe.wait_ge(s["v_loaded"], 16)
                for n in range(NQ):
                    for m in range(NQ):
                        at = (n * NQ + m) * P
                        mm = nc.tensor.transpose(ps[:, n, m * P:(m + 1) * P], v[:, at:at + P], c.ident[:])
                    mm.then_inc(s["v_turned"], 1)

            @block.scalar
            def _(act):
                for n in range(NQ):
                    act.wait_ge(s["v_turned"], n + 1)
                    nc.scalar.copy(vt[:, n * NQ:(n + 1) * NQ, :].rearrange("p c d -> p (c d)"), ps[:, n, :]) \
                        .then_inc(s["v_copied"], 1)
                def store(t):
                    act.wait_ge(s["lo"], t + 1)
                    dst = a.att_q if t < N_QK - 1 else a.att_k
                    for half in range(2):
                        head = (2 * t if t < N_QK - 1 else 0) + half
                        rows = slice(half * DH, (half + 1) * DH)
                        for part, at in ((hi, 0), (lo, DH)):
                            act.dma_start(dst[head, at:at + DH], part[rows, t % 2, :].bitcast(F32)) \
                                .then_inc(s[f"stored{t % 2}"], 16)

                for t in range(N_QK):
                    u = t % 2
                    act.wait_ge(s["scaled"], t + 1)
                    if t >= 2:
                        act.wait_ge(s[f"stored{u}"], 64 * (t // 2))
                    nc.scalar.copy(hi[:, u, :], x[:, u, :]).then_inc(s["hi"], 1)
                    if t:
                        store(t - 1)
                store(N_QK - 1)
                act.wait_ge(s["stored0"], 3 * 64)
                act.wait_ge(s["stored1"], 2 * 64)

            @block.vector
            def _(dve):
                dve.wait_ge(s["const_loaded"], 32)

                def split(t):
                    dve.wait_ge(s["hi"], t + 1)
                    nc.vector.tensor_tensor(lo[:, t % 2, :], x[:, t % 2, :], hi[:, t % 2, :].bitcast(F32),
                                            ALU.subtract).then_inc(s["lo"], 1)

                for t in range(N_QK):
                    u = t % 2
                    col = 0 if t < N_QK - 1 else 2
                    dve.wait_ge(s[f"y_loaded{u}"], 16 * 8 * (t // 2 + 1))
                    nc.vector.scalar_tensor_tensor(out=y[:, u, :], in0=y[:, u, :], scalar=w[:, col + 1:col + 2],
                                                   in1=rope[:, 1, :], op0=ALU.mult, op1=ALU.mult).then_inc(s["sin_done"], 1)
                    dve.wait_ge(s[f"x_loaded{u}"], 16 * (t // 2 + 1))
                    nc.vector.scalar_tensor_tensor(out=x[:, u, :], in0=x[:, u, :], scalar=w[:, col:col + 1],
                                                   in1=rope[:, 0, :], op0=ALU.mult, op1=ALU.mult).then_inc(s["cos_done"], 1)
                    if t:
                        split(t - 1)
                    dve.wait_ge(s["rotated"], t + 1)
                    dve.wait_ge(s[f"r_loaded{u}"], 32 * (t // 2 + 1))
                    nc.vector.tensor_tensor(x[:, u, :], x[:, u, :], r[:, u, :], ALU.mult).then_inc(s["scaled"], 1)
                split(N_QK - 1)


SIDES = range(N_DIR)
HEADS = range(DN_HEADS)


def chunk_of(side, i):
    return i if side == 0 else i * -1 + (NC - 1)


def delta_net(nc, a, c, l):
    per_side = ("k1_loaded k2_loaded qv_loaded scalars1 scalars2 dd dt eg u y0 y0_part t0 x0 masked p_done p_copied "
                "xp_done x_updated xt_done y_copied yf kq_done att kt_done kk vt_done vv qg "
                "ks_done r tr_done vn vd out_done o_added ds_done state vs gram dtm ")
    names = " ".join(f"{n}{side}" for n in per_side.split() for side in SIDES) + " masks_loaded zeroed o_stored passed"
    with ExitStack() as stack, semaphores(nc, names) as s:
        b = Buffers(nc, stack, "dn")
        pair = lambda name: b.sbuf(name, [P, N_DIR, DN_HEADS, P])
        masks = b.sbuf("masks", [P, N_DIR, LEVELS + 1, P])
        k1, row, k2, q, v = (pair(n) for n in ("k1", "row", "k2", "q", "v"))
        dd, eg, dt, u, y_part = (pair(n) for n in ("dd", "eg", "dt", "u", "y_part"))
        x, y, p, yf = (pair(n) for n in ("x", "y", "p", "yf"))
        att, qg, kk, vv = (pair(n) for n in ("att", "qg", "kk", "vv"))
        r, vn, vd, state = (pair(n) for n in ("r", "vn", "vd", "state"))
        um = b.sbuf("um", [P, N_DIR, 2, DN_HEADS, P])
        sc1 = b.sbuf("sc1", [P, N_DIR, TABLES, DN_HEADS])
        sc2 = b.sbuf("sc2", [P, N_DIR, TABLES, DN_HEADS])
        vs = b.sbuf("vs", [P, N_DIR, DN_HEADS])
        o = b.sbuf("out", [P, DN_HEADS, SEQ])
        ps = b.banks()
        bank = lambda n: ps[:, n, :].rearrange("p (h t) -> p h t", h=DN_HEADS)
        inner, outer = (lambda side, n: bank(2 * side + n)), (lambda side, n: bank(4 + 2 * side + n))
        mask = lambda side, lv: masks[:, side, lv, :].unsqueeze(1).broadcast_to([P, DN_HEADS, P])
        ident = c.ident[:].unsqueeze(1).broadcast_to([P, DN_HEADS, P])
        per_head = lambda t: t.unsqueeze(2).broadcast_to([P, DN_HEADS, P])

        with nc.Block() as block:

            @block.sync
            def _(sp):
                sp.dma_start(masks[:], a.masks).then_inc(s["masks_loaded"], 16)

                def channels(first, side, i):
                    at = chunk_of(side, i) * P
                    return a.proj[first:first + DN_HEADS, :, bass.ds(at, P)].rearrange("h p t -> p h t")

                def load_k1(side, i):
                    sp.dma_start(k1[:, side], channels(T_K, side, i)).then_inc(s[f"k1_loaded{side}"], 16)
                    rows = a.g_rows[chunk_of(side, i), side * DN_HEADS:(side + 1) * DN_HEADS]
                    sp.dma_start(row[:, side], rows.partition_broadcast(P)).then_inc(s[f"k1_loaded{side}"], 16)

                def load_k2(side, i):
                    sp.dma_start(k2[:, side], channels(T_K, side, i)).then_inc(s[f"k2_loaded{side}"], 16)

                def load_qv(side, i):
                    sp.dma_start(q[:, side], channels(T_Q, side, i)).then_inc(s[f"qv_loaded{side}"], 16)
                    sp.dma_start(v[:, side], channels(T_V, side, i)).then_inc(s[f"qv_loaded{side}"], 16)

                for load in (load_k1, load_k2, load_qv):
                    for side in SIDES:
                        load(side, 0)
                with sp.Fori(1, NC) as i:
                    for side in SIDES:
                        wait_in_loop(sp, s, f"gram{side}", i)
                        wait_in_loop(sp, s, f"dd{side}", i)
                        wait_in_loop(sp, s, f"eg{side}", i)
                        load_k1(side, i)
                    for side in SIDES:
                        wait_in_loop(sp, s, f"ks_done{side}", i)
                        load_k2(side, i)
                    for side in SIDES:
                        wait_in_loop(sp, s, f"vt_done{side}", i)
                        wait_in_loop(sp, s, f"qg{side}", i)
                        load_qv(side, i)
                for side in SIDES:
                    sp.wait_ge(s[f"o_added{side}"], NC)
                sp.dma_start(a.dn_o.rearrange("h p t -> p h t"), o[:]).then_inc(s["o_stored"], 16)
                sp.wait_ge(s["o_stored"], 16)

            @block.tensor
            def _(pe):
                def each(out, left, right):
                    for h in HEADS:
                        mm = nc.tensor.matmul(out[:, h, :], left[:, h, :], right[:, h, :], start=True, stop=True)
                    return mm

                def turn(out, src):
                    for h in HEADS:
                        mm = nc.tensor.transpose(out[:, h, :], src[:, h, :], c.ident[:])
                    return mm

                def gram(side, i):
                    pe.wait_ge(s[f"k1_loaded{side}"], 32 * i + 32)
                    pe.wait_ge(s[f"p_copied{side}"], 6 * i)
                    each(inner(side, 0), k1[:, side], k1[:, side]).then_inc(s[f"gram{side}"], 1)

                def turn_first(side, i):
                    pe.wait_ge(s[f"y0{side}"], i + 1)
                    turn(inner(side, 1), y[:, side]).then_inc(s[f"t0{side}"], 1)

                def product(side, i, lv):
                    pe.wait_ge(s[f"masked{side}"], 6 * i + lv)
                    if lv == 1:
                        pe.wait_ge(s[f"x0{side}"], i + 1)
                    else:
                        pe.wait_ge(s[f"x_updated{side}"], 5 * i + lv - 1)
                        pe.wait_ge(s[f"y_copied{side}"], 5 * i + lv - 1)
                    each(inner(side, 0), um[:, side, lv % 2], x[:, side]).then_inc(s[f"p_done{side}"], 1)

                def step(side, i, lv):
                    pe.wait_ge(s[f"p_copied{side}"], 6 * i + lv)
                    if lv < LEVELS - 1:
                        each(inner(side, 1), y[:, side], p[:, side]).then_inc(s[f"xp_done{side}"], 1)
                    else:
                        each(inner(side, 1), p[:, side], y[:, side]).then_inc(s[f"xp_done{side}"], 1)

                def turn_x(side, i, lv):
                    pe.wait_ge(s[f"x_updated{side}"], 5 * i + lv)
                    turn(inner(side, 0), x[:, side]).then_inc(s[f"xt_done{side}"], 1)

                def key_query(side, i):
                    pe.wait_ge(s[f"k2_loaded{side}"], 16 * i + 16)
                    pe.wait_ge(s[f"qv_loaded{side}"], 32 * i + 32)
                    pe.wait_ge(s[f"o_added{side}"], i)
                    each(outer(side, 0), k2[:, side], q[:, side]).then_inc(s[f"kq_done{side}"], 1)

                def turn_k(side, i):
                    pe.wait_ge(s[f"state{side}"], i + 1)
                    turn(outer(side, 1), k2[:, side]).then_inc(s[f"kt_done{side}"], 1)

                def turn_v(side, i):
                    pe.wait_ge(s[f"att{side}"], i + 1)
                    turn(outer(side, 0), v[:, side]).then_inc(s[f"vt_done{side}"], 1)

                def scan_ks(side, j):
                    pe.wait_ge(s[f"state{side}"], j + 1)
                    pe.wait_ge(s[f"vv{side}"], j + 1)
                    each(outer(side, 0), k2[:, side], state[:, side]).then_inc(s[f"ks_done{side}"], 1)

                def scan_solve(side, j):
                    pe.wait_ge(s[f"r{side}"], j + 1)
                    pe.wait_ge(s[f"yf{side}"], j + 1)
                    pe.wait_ge(s[f"kk{side}"], j + 1)
                    each(outer(side, 1), yf[:, side], r[:, side]).then_inc(s[f"tr_done{side}"], 1)

                def scan_out(side, j):
                    pe.wait_ge(s[f"qg{side}"], j + 1)
                    pe.wait_ge(s[f"vn{side}"], j + 1)
                    for h in HEADS:
                        nc.tensor.matmul(outer(side, 0)[:, h, :], state[:, side, h, :], qg[:, side, h, :],
                                         start=True, stop=False)
                        mm = nc.tensor.matmul(outer(side, 0)[:, h, :], vn[:, side, h, :], att[:, side, h, :],
                                              start=False, stop=True)
                    mm.then_inc(s[f"out_done{side}"], 1)

                def scan_state(side, j):
                    pe.wait_ge(s[f"vd{side}"], j + 1)
                    each(outer(side, 1), kk[:, side], vd[:, side]).then_inc(s[f"ds_done{side}"], 1)

                def iteration(i, j):
                    local, scan = i is not None, j is not None
                    for side in SIDES:
                        if local:
                            gram(side, i)
                    for side in SIDES:
                        if scan:
                            scan_ks(side, j)
                    for side in SIDES:
                        if local:
                            turn_first(side, i)
                    for side in SIDES:
                        if scan:
                            scan_solve(side, j)
                    for lv in range(1, LEVELS):
                        for side in SIDES:
                            if local:
                                product(side, i, lv)
                        if scan and lv <= 2:
                            scan_out(lv - 1, j)
                        if local and lv >= 3 and lv <= 5:
                            (key_query, turn_k, turn_v)[lv - 3](0, i)
                        for side in SIDES:
                            if local:
                                step(side, i, lv)
                        if scan and lv <= 2:
                            scan_state(lv - 1, j)
                        if local and lv >= 3 and lv <= 5:
                            (key_query, turn_k, turn_v)[lv - 3](1, i)
                        for side in SIDES:
                            if local and lv < LEVELS - 1:
                                turn_x(side, i, lv)

                iteration(0, None)
                with pe.Fori(1, NC) as i:
                    iteration(i, i - 1)
                iteration(None, NC - 1)

            @block.scalar
            def _(act):
                def evacuate(done, count, dst, src, name, side):
                    act.wait_ge(s[f"{done}{side}"], count)
                    nc.scalar.copy(dst, src).then_inc(s[f"{name}{side}"], 1)

                def local(i):
                    for side in SIDES:
                        act.wait_ge(s[f"dd{side}"], i + 1)
                        nc.scalar.activation(dt[:, side], dd[:, side], ACT.Exp).then_inc(s[f"dt{side}"], 1)
                    for side in SIDES:
                        act.wait_ge(s[f"k1_loaded{side}"], 32 * i + 32)
                        act.wait_ge(s[f"qg{side}"], i)
                        nc.scalar.activation(eg[:, side], row[:, side], ACT.Exp).then_inc(s[f"eg{side}"], 1)
                    for side in SIDES:
                        evacuate("t0", i + 1, x[:, side], inner(side, 1), "x0", side)
                    for lv in range(1, LEVELS):
                        for side in SIDES:
                            evacuate("p_done", 6 * i + lv, p[:, side], inner(side, 0), "p_copied", side)
                        if lv == 4:
                            for side in SIDES:
                                if side == 1:
                                    evacuate("xt_done", 5 * i + lv, y[:, 0], inner(0, 0), "y_copied", 0)
                                evacuate("kt_done", i + 1, kk[:, side], outer(side, 1), "kk", side)
                            evacuate("xt_done", 5 * i + lv, y[:, 1], inner(1, 0), "y_copied", 1)
                        elif lv < LEVELS - 1:
                            for side in SIDES:
                                evacuate("xt_done", 5 * i + lv, y[:, side], inner(side, 0), "y_copied", side)

                with act.Fori(0, NC) as i:
                    local(i)

            @block.gpsimd
            def _(pool):
                for side in SIDES:
                    nc.gpsimd.memset(state[:, side], 0.0).then_inc(s[f"state{side}"], 1)
                nc.gpsimd.memset(o[:], 0.0).then_inc(s["zeroed"], 1)
                pool.wait_ge(s["masks_loaded"], 16)

                def scalars(side, i):
                    heads = slice(side * DN_HEADS, (side + 1) * DN_HEADS)
                    pool.wait_ge(s[f"u{side}"], i)
                    nc.gpsimd.tensor_copy(sc1[:, side], c.tok[:, bass.ds(chunk_of(side, i), 1), :, heads].squeeze(1)) \
                        .then_inc(s[f"scalars1{side}"], 1)

                def v_scalars(side, i):
                    pool.wait_ge(s[f"vv{side}"], i)
                    nc.gpsimd.tensor_copy(vs[:, side], c.v_scale[:, bass.ds(chunk_of(side, i), 1), :].squeeze(1)) \
                        .then_inc(s[f"vs{side}"], 1)

                def scan_scalars(side, i):
                    heads = slice(side * DN_HEADS, (side + 1) * DN_HEADS)
                    pool.wait_ge(s[f"state{side}"], i + 1)
                    nc.gpsimd.tensor_copy(sc2[:, side], c.tok[:, bass.ds(chunk_of(side, i), 1), :, heads].squeeze(1)) \
                        .then_inc(s[f"scalars2{side}"], 1)

                for side in SIDES:
                    scalars(side, 0)
                def local(i):
                    for side in SIDES:
                        v_scalars(side, i)
                    for lv in range(1, LEVELS):
                        for side in SIDES:
                            pool.wait_ge(s[f"u{side}"], i + 1)
                            if lv <= 2:
                                pool.wait_ge(s[f"xp_done{side}"], 6 * i)
                            else:
                                pool.wait_ge(s[f"p_done{side}"], 6 * i + lv - 2)
                            nc.gpsimd.tensor_tensor(um[:, side, lv % 2], u[:, side], mask(side, lv), ALU.mult) \
                                .then_inc(s[f"masked{side}"], 1)
                        if lv == 3:
                            for side in SIDES:
                                scan_scalars(side, i)
                        if lv == 4:
                            for side in SIDES:
                                pool.wait_ge(s[f"qv_loaded{side}"], 32 * i + 32)
                                pool.wait_ge(s[f"eg{side}"], i + 1)
                                pool.wait_ge(s[f"o_added{side}"], i)
                                nc.gpsimd.tensor_tensor(qg[:, side], q[:, side], eg[:, side], ALU.mult) \
                                    .then_inc(s[f"qg{side}"], 1)

                with pool.Fori(0, NC - 1) as i:
                    local(i)
                    for side in SIDES:
                        scalars(side, i + 1)
                local(NC - 1)

            @block.vector
            def _(dve):
                def decays(side, i):
                    dve.wait_ge(s[f"k1_loaded{side}"], 32 * i + 32)
                    dve.wait_ge(s[f"scalars1{side}"], i + 1)
                    dve.wait_ge(s[f"dt{side}"], i)
                    for h in HEADS:
                        op = nc.vector.tensor_scalar(dd[:, side, h, :], row[:, side, h, :], sc1[:, side, T_G, h:h + 1],
                                                     0.0, ALU.subtract, ALU.min)
                    op.then_inc(s[f"dd{side}"], 1)

                def system(side, i):
                    dve.wait_ge(s[f"dt{side}"], i + 1)
                    nc.vector.tensor_tensor(dt[:, side], dt[:, side], mask(side, LEVELS), ALU.mult).then_inc(s[f"dtm{side}"], 1)
                    dve.wait_ge(s[f"dtm{side}"], i + 1)
                    dve.wait_ge(s[f"gram{side}"], i + 1)
                    dve.wait_ge(s[f"masked{side}"], 6 * i)
                    for h in HEADS:
                        op = nc.vector.scalar_tensor_tensor(out=u[:, side, h, :], in0=inner(side, 0)[:, h, :],
                                                            scalar=sc1[:, side, T_BETA, h:h + 1], in1=dt[:, side, h, :],
                                                            op0=ALU.mult, op1=ALU.mult)
                    op.then_inc(s[f"u{side}"], 1)
                    dve.wait_ge(s[f"u{side}"], i + 1)
                    nc.vector.tensor_tensor(y_part[:, side], u[:, side], mask(side, 0), ALU.mult).then_inc(s[f"y0_part{side}"], 1)
                    dve.wait_ge(s[f"y0_part{side}"], i + 1)
                    dve.wait_ge(s[f"yf{side}"], i)
                    nc.vector.tensor_tensor(y[:, side], y_part[:, side], ident, ALU.add).then_inc(s[f"y0{side}"], 1)

                def update(side, i, lv):
                    dve.wait_ge(s[f"xp_done{side}"], 6 * i + lv)
                    if lv < LEVELS - 1:
                        if lv > 1:
                            dve.wait_ge(s[f"x_updated{side}"], 5 * i + lv - 1)
                        nc.vector.tensor_tensor(x[:, side], x[:, side], inner(side, 1), ALU.subtract) \
                            .then_inc(s[f"x_updated{side}"], 1)
                    else:
                        nc.vector.tensor_tensor(yf[:, side], y[:, side], inner(side, 1), ALU.subtract) \
                            .then_inc(s[f"yf{side}"], 1)

                def attend(side, i):
                    dve.wait_ge(s[f"kq_done{side}"], i + 1)
                    nc.vector.tensor_tensor(att[:, side], outer(side, 0), dt[:, side], ALU.mult).then_inc(s[f"att{side}"], 1)

                def values(side, i):
                    dve.wait_ge(s[f"vt_done{side}"], i + 1)
                    dve.wait_ge(s[f"vs{side}"], i + 1)
                    dve.wait_ge(s[f"r{side}"], i)
                    nc.vector.tensor_tensor(vv[:, side], outer(side, 0), per_head(vs[:, side]), ALU.mult) \
                        .then_inc(s[f"vv{side}"], 1)

                def remainder(side, j):
                    dve.wait_ge(s[f"ks_done{side}"], j + 1)
                    dve.wait_ge(s[f"vv{side}"], j + 1)
                    dve.wait_ge(s[f"scalars2{side}"], j + 1)
                    for h in HEADS:
                        op = nc.vector.scalar_tensor_tensor(out=r[:, side, h, :], in0=outer(side, 0)[:, h, :],
                                                            scalar=sc2[:, side, T_NEG, h:h + 1], in1=vv[:, side, h, :],
                                                            op0=ALU.mult, op1=ALU.add)
                    op.then_inc(s[f"r{side}"], 1)

                def new_values(side, j):
                    dve.wait_ge(s[f"tr_done{side}"], j + 1)
                    nc.vector.tensor_tensor(vn[:, side], outer(side, 1), per_head(sc2[:, side, T_BETA, :]), ALU.mult) \
                        .then_inc(s[f"vn{side}"], 1)
                    nc.vector.tensor_tensor(vd[:, side], outer(side, 1), per_head(sc2[:, side, T_BETA_END, :]), ALU.mult) \
                        .then_inc(s[f"vd{side}"], 1)

                def output(side, j):
                    at = chunk_of(side, j) * P
                    dve.wait_ge(s[f"o_added{1 - side}"], j)
                    dve.wait_ge(s[f"out_done{side}"], j + 1)
                    there = o[:, :, bass.ds(at, P)]
                    nc.vector.tensor_tensor(there, outer(side, 0), there, ALU.add).then_inc(s[f"o_added{side}"], 1)

                def new_state(side, j):
                    dve.wait_ge(s[f"ds_done{side}"], j + 1)
                    dve.wait_ge(s[f"state{side}"], j + 1)
                    for h in HEADS:
                        op = nc.vector.scalar_tensor_tensor(out=state[:, side, h, :], in0=state[:, side, h, :],
                                                            scalar=sc2[:, side, T_CHUNK, h:h + 1],
                                                            in1=outer(side, 1)[:, h, :], op0=ALU.mult, op1=ALU.add)
                    op.then_inc(s[f"state{side}"], 1)

                def iteration(i, j):
                    local, scan = i is not None, j is not None
                    for side in SIDES:
                        if local:
                            decays(side, i)
                    for side in SIDES:
                        if scan:
                            remainder(side, j)
                    for side in SIDES:
                        if local:
                            system(side, i)
                    for side in SIDES:
                        if scan:
                            new_values(side, j)
                    for lv in range(1, LEVELS):
                        if scan and lv <= 2:
                            output(lv - 1, j)
                        if local and lv == 3:
                            attend(0, i)
                        if local and lv == 5:
                            values(0, i)
                        for side in SIDES:
                            if local:
                                update(side, i, lv)
                        if scan and lv <= 2:
                            new_state(lv - 1, j)
                        if local and lv == 3:
                            attend(1, i)
                        if local and lv == 5:
                            values(1, i)

                dve.wait_ge(s["masks_loaded"], 16)
                dve.wait_ge(s["zeroed"], 1)
                iteration(0, None)
                with dve.Fori(1, NC) as i:
                    iteration(i, i - 1)
                iteration(None, NC - 1)


N_UNITS = NC
MAX_PLAN = [3, 3, 3, 3, 2, 2, 0, 0]
PAIRS = NC // 2
MAX_DONE = 5
LAG = 2
SLOTS = 4
K_ROWS = DH + NQ


def attention(nc, a, c, l):
    names = ("max_part turned negated unit_done unit_read v_loaded const_loaded ones_set v_split "
             "scores_done exp_done hi_done lo_done pv_done o_copied o_stored0 o_stored1 k_loaded0 k_loaded1 passed "
             + " ".join(f"q_loaded{u} q2_loaded{u}" for u in range(SLOTS)))
    NB = ATT_HEADS * NQ
    ROUNDS = NB // SLOTS
    with ExitStack() as stack, semaphores(nc, names) as s:
        b = Buffers(nc, stack, "att")
        k1 = b.sbuf("k1", [P, KV_HEADS, SEQ], F32R)
        k2 = b.sbuf("k2", [K_ROWS, KV_HEADS, SEQ], F32R)
        v = b.sbuf("v", [P, KV_HEADS, NC, DH + 1])
        v_hi = b.sbuf("v_hi", [P, KV_HEADS, NC, DH + 1], F32R)
        v_lo = b.sbuf("v_lo", [P, KV_HEADS, NC, DH + 1], F32R)
        quarter = b.sbuf("quarter", [NQ, NQ, P])
        q1 = b.sbuf("q1", [P, SLOTS, QB], F32R)
        q2 = b.sbuf("q2", [K_ROWS, SLOTS, QB], F32R)
        probs = b.sbuf("probs", [P, 2, 2, QB])
        p_hi = b.sbuf("p_hi", [P, SLOTS, 2, QB], F32R)
        p_lo = b.sbuf("p_lo", [P, SLOTS, 2, QB], F32R)
        part = b.sbuf("part", [P, NQ, NQ])
        top = b.sbuf("top", [P, NQ])
        o = b.sbuf("o", [DH + 1, 2, QB])
        ps = b.banks()
        with nc.Block() as block:

            @block.sync
            def _(sp):
                for kv in range(KV_HEADS):
                    sp.dma_start(k1[0:DH, kv, :].bitcast(F32), a.att_k[kv, 0:DH]).then_inc(s[f"k_loaded{kv}"], 16)
                    sp.dma_start(k1[DH:P, kv, :].bitcast(F32), a.att_k[kv, 0:DH]).then_inc(s[f"k_loaded{kv}"], 16)
                    sp.dma_start(k2[0:DH, kv, :].bitcast(F32), a.att_k[kv, DH:P]).then_inc(s[f"k_loaded{kv}"], 16)
                    sp.dma_start(v[:, kv, :, 0:DH], a.att_v[:, :, kv, :]).then_inc(s["v_loaded"], 16)
                sp.dma_start(quarter[:], a.quarter).then_inc(s["const_loaded"], 16)

                def load_q(j, slot):
                    head = (slot % 2) * GROUP + j // 2
                    at = (j % 2 * 2 + slot // 2) * QB
                    sp.dma_start(q2[0:DH, slot, :].bitcast(F32), a.att_q[head, 0:DH, bass.ds(at, QB)]).then_inc(s[f"q2_loaded{slot}"], 16)
                    sp.dma_start(q1[:, slot, :].bitcast(F32), a.att_q[head, :, bass.ds(at, QB)]).then_inc(s[f"q_loaded{slot}"], 16)

                def store(j, slot):
                    head = (slot % 2) * GROUP + j // 2
                    at = (j % 2 * 2 + slot // 2) * QB
                    sp.dma_start(a.att_o[head, :, bass.ds(at, QB)], o[:, slot % 2, :]).then_inc(s[f"o_stored{slot % 2}"], 16)

                for slot in range(SLOTS):
                    load_q(0, slot)
                with sp.Fori(0, ROUNDS - 1) as j:
                    for slot in range(SLOTS):
                        wait_in_loop(sp, s, "scores_done", (j * SLOTS + slot + 1) * PAIRS)
                        load_q(j + 1, slot)
                        wait_in_loop(sp, s, "o_copied", j * SLOTS + slot + 1)
                        store(j, slot)
                for slot in range(SLOTS):
                    sp.wait_ge(s["o_copied"], NB - SLOTS + slot + 1)
                    store(ROUNDS - 1, slot)
                for kv in range(2):
                    sp.wait_ge(s[f"o_stored{kv}"], 16 * (NB // 2))

            @block.gpsimd
            def _(pool):
                nc.gpsimd.memset(v[:, :, :, DH:DH + 1], 1.0).then_inc(s["ones_set"], 1)

            @block.tensor
            def _(pe):
                def max_unit(j, slot, u):
                    tile, keys = u // NQ, u % NQ
                    n = j * SLOTS + slot
                    if u == 0:
                        pe.wait_ge(s[f"q2_loaded{slot}"], 16 * j + 16)
                    pe.wait_ge(s["unit_read"], n * N_UNITS + u + 1)
                    nc.tensor.matmul(ps[:, 4 + u % 2, :], q2[0:DH, slot, tile * P:(tile + 1) * P],
                                     k1[0:DH, slot % 2, keys * QB:(keys + 1) * QB], start=True, stop=True) \
                        .then_inc(s["unit_done"], 1)

                def turn_max(j, slot):
                    pe.wait_ge(s["max_part"], j * SLOTS + slot + 1)
                    nc.tensor.transpose(ps[0:NQ, 7, 0:P], top[:], c.ident[:]).then_inc(s["turned"], 1)

                def scores(j, slot, pair):
                    pe.wait_ge(s["exp_done"], (j * SLOTS + slot) * PAIRS + pair + 1)
                    if pair == 0:
                        pe.wait_ge(s[f"q_loaded{slot}"], 16 * j + 16)
                        pe.wait_ge(s["negated"], j * SLOTS + slot + 1)
                    for m in range(2):
                        keys = slice((2 * pair + m) * P, (2 * pair + m + 1) * P)
                        out = ps[:, 2 * (pair % 2) + m, :]
                        nc.tensor.matmul(out, k1[:, slot % 2, keys], q1[:, slot, :], start=True, stop=False)
                        mm = nc.tensor.matmul(out, k2[:, slot % 2, keys], q2[:, slot, :], start=False, stop=True)
                    mm.then_inc(s["scores_done"], 1)

                def values(j, slot, pair):
                    n = j * SLOTS + slot
                    pe.wait_ge(s["lo_done"], n * PAIRS + pair + 1 + 2)
                    if pair == 0:
                        pe.wait_ge(s["o_copied"], n)
                    kv, at = slot % 2, pair % SLOTS
                    for m in range(2):
                        tile = 2 * pair + m
                        for part_v, part_p in ((v_hi, p_hi), (v_hi, p_lo), (v_lo, p_hi)):
                            first = tile == 0 and part_v is v_hi and part_p is p_hi
                            mm = nc.tensor.matmul(ps[0:DH + 1, 6, :], part_v[:, kv, tile, :], part_p[:, at, m, :],
                                                  start=first, stop=(tile == NC - 1 and part_v is v_lo))
                    mm.then_inc(s["pv_done"], 1)

                def one_block(j, slot, before, after):
                    u = 0
                    for pair in range(PAIRS):
                        units = MAX_PLAN[pair] if after else 0
                        scores(j, slot, pair)
                        if pair == MAX_DONE + 1 and after:
                            turn_max(*after)
                        for _ in range((units + 1) // 2):
                            max_unit(*after, u)
                            u += 1
                        if pair >= LAG:
                            values(j, slot, pair - LAG)
                        elif before:
                            values(*before, PAIRS + pair - LAG)
                        for _ in range(units // 2):
                            max_unit(*after, u)
                            u += 1

                pe.sem_inc(s["exp_done"], 2)
                for kv in range(KV_HEADS):
                    pe.wait_ge(s[f"k_loaded{kv}"], 48)
                for u in range(N_UNITS):
                    max_unit(0, 0, u)
                turn_max(0, 0)
                pe.wait_ge(s["ones_set"], 2)
                pe.wait_ge(s["v_split"], 2)
                one_block(0, 0, None, (0, 1))
                for slot in range(1, SLOTS):
                    one_block(0, slot, (0, slot - 1), (slot // (SLOTS - 1), (slot + 1) % SLOTS))
                with pe.Fori(1, ROUNDS - 1) as j:
                    one_block(j, 0, (j - 1, SLOTS - 1), (j, 1))
                    for slot in range(1, SLOTS):
                        one_block(j, slot, (j, slot - 1), (j + slot // (SLOTS - 1), (slot + 1) % SLOTS))
                j = ROUNDS - 1
                one_block(j, 0, (j - 1, SLOTS - 1), (j, 1))
                for slot in range(1, SLOTS):
                    one_block(j, slot, (j, slot - 1), (j, slot + 1) if slot < SLOTS - 1 else None)
                for pair in range(PAIRS - LAG, PAIRS):
                    values(j, SLOTS - 1, pair)

            @block.scalar
            def _(act):
                with act.Fori(0, ROUNDS) as j:
                    for g in range(SLOTS * PAIRS):
                        n, pair = j * SLOTS + g // PAIRS, g % PAIRS
                        act.wait_ge(s["scores_done"], n * PAIRS + pair + 1)
                        act.wait_ge(s["lo_done"], n * PAIRS + pair + 1)
                        nc.scalar.activation(probs[:, pair % 2], ps[:, 2 * (pair % 2):2 * (pair % 2) + 2, :], ACT.Exp,
                                             scale=SCALE).then_inc(s["exp_done"], 1)
                        act.wait_ge(s["exp_done"], n * PAIRS + pair + 1 + 2)
                        act.wait_ge(s["pv_done"], n * PAIRS + pair + 1)
                        nc.scalar.activation(p_hi[:, pair % SLOTS], probs[:, pair % 2], ACT.Copy).then_inc(s["hi_done"], 1)

            @block.vector
            def _(dve):
                def read_units(n, units, u):
                    for w in range(u, u + units):
                        dve.wait_ge(s["unit_done"], n * N_UNITS + w + 1)
                        nc.vector.tensor_reduce(part[:, w // NQ, w % NQ:w % NQ + 1], ps[:, 4 + w % 2, :], AX.X, ALU.max) \
                            .then_inc(s["unit_read"], 1)

                def all_maxima(n):
                    dve.wait_ge(s["unit_read"], n * N_UNITS + N_UNITS + 2)
                    dve.wait_ge(s["turned"], n)
                    nc.vector.tensor_reduce(top[:], part[:], AX.X, ALU.max).then_inc(s["max_part"], 1)

                def minus_max(slot, n):
                    dve.wait_ge(s["turned"], n + 1)
                    turned = ps[0:NQ, 7, 0:P].unsqueeze(1).broadcast_to([NQ, NQ, P])
                    nc.vector.tensor_tensor(q2[DH:K_ROWS, slot, :].rearrange("r (t q) -> r t q", q=P), turned, quarter[:],
                                            ALU.mult).then_inc(s["negated"], 1)

                def low_part(n, pair):
                    dve.wait_ge(s["hi_done"], n * PAIRS + pair + 1)
                    dve.wait_ge(s["pv_done"], n * PAIRS + pair + 1)
                    nc.vector.tensor_tensor(p_lo[:, pair % SLOTS], probs[:, pair % 2], p_hi[:, pair % SLOTS].bitcast(F32),
                                            ALU.subtract).then_inc(s["lo_done"], 1)

                def output(n, kv, before):
                    dve.wait_ge(s["pv_done"], n * PAIRS + PAIRS + SLOTS)
                    dve.wait_ge(s[f"o_stored{kv}"], before)
                    nc.vector.tensor_copy(o[:, kv, :], ps[0:DH + 1, 6, :]).then_inc(s["o_copied"], 1)

                def one_block(n, slot, stored, after):
                    u = 0
                    for pair in range(PAIRS):
                        units = MAX_PLAN[pair] if after else 0
                        read_units(n + 1, (units + 1) // 2, u)
                        if pair > 0:
                            low_part(n, pair - 1)
                        elif stored is not None:
                            low_part(n - 1, PAIRS - 1)
                        read_units(n + 1, units // 2, u + (units + 1) // 2)
                        u += units
                        if pair == LAG - 1 and stored is not None:
                            output(n - 1, (slot + 1) % 2, stored)
                        if pair == MAX_DONE and after:
                            all_maxima(n + 1)
                        if pair == MAX_DONE + 1 and after:
                            minus_max((slot + 1) % SLOTS, n + 1)

                nc.vector.memset(k2[DH:K_ROWS, :, :].bitcast(F32), 1.0).then_inc(s["ones_set"], 1)
                dve.sem_inc(s["unit_read"], 2)
                dve.sem_inc(s["lo_done"], 2)
                dve.sem_inc(s["pv_done"], SLOTS)
                dve.wait_ge(s["const_loaded"], 16)
                read_units(0, N_UNITS, 0)
                all_maxima(0)
                minus_max(0, 0)
                dve.wait_ge(s["v_loaded"], 32)
                dve.wait_ge(s["ones_set"], 2)
                nc.vector.tensor_copy(v_hi[:], v[:]).then_inc(s["v_split"], 1)
                dve.wait_ge(s["v_split"], 1)
                nc.vector.tensor_tensor(v_lo[:], v[:], v_hi[:].bitcast(F32), ALU.subtract).then_inc(s["v_split"], 1)
                one_block(0, 0, None, True)
                for slot in range(1, SLOTS):
                    one_block(slot, slot, 16 * ((slot - 1) // 2), True)
                with dve.Fori(1, ROUNDS - 1) as j:
                    for slot in range(SLOTS):
                        one_block(j * SLOTS + slot, slot, j * (16 * SLOTS // 2) + 16 * ((slot - 1) // 2), True)
                for slot in range(SLOTS):
                    n = NB - SLOTS + slot
                    one_block(n, slot, 16 * ((n - 1) // 2), slot < SLOTS - 1)
                low_part(NB - 1, PAIRS - 1)
                output(NB - 1, 1, 16 * (NB // 2 - 1))


def branch_scales(nc, a, c, l):
    names = "x_loaded0 x_loaded1 squared summed mean root inv turned copied stored den_loaded den_done passed"
    with ExitStack() as stack, semaphores(nc, names) as s:
        b = Buffers(nc, stack, "bs")
        x = b.sbuf("x", [P, 2, SEQ])
        sq = b.sbuf("sq", [P, 2, SEQ])
        mean = b.sbuf("mean", [P, DN_HEADS, NC])
        inv = b.sbuf("inv", [P, DN_HEADS, NC])
        rows = b.sbuf("rows", [P // 2, P])
        den = b.sbuf("den", [P, P])
        den_inv = b.sbuf("den_inv", [P, P])
        ps = b.banks()
        n_rows = DN_HEADS * NC
        with nc.Block() as block:

            @block.sync
            def _(sp):
                for h in range(ATT_HEADS):
                    sp.dma_start(den[h * NC:(h + 1) * NC, :], a.att_o[h, DH].rearrange("(c p) -> c p", p=P)) \
                        .then_inc(s["den_loaded"], 16)
                for h in range(DN_HEADS):
                    if h >= 2:
                        sp.wait_ge(s["squared"], h - 1)
                    sp.dma_start(x[:, h % 2, :], a.dn_o[h]).then_inc(s[f"x_loaded{h % 2}"], 16)
                sp.wait_ge(s["den_done"], 1)
                sp.dma_start(a.den_rows.rearrange("h (c p) -> (h c) p", p=P), den_inv[:]).then_inc(s["stored"], 16)
                sp.wait_ge(s["copied"], 1)
                sp.dma_start(a.o_rows.rearrange("h (c p) -> (h c) p", p=P), rows[0:n_rows, :]).then_inc(s["stored"], 16)
                sp.wait_ge(s["stored"], 32)

            @block.scalar
            def _(act):
                for h in range(DN_HEADS):
                    act.wait_ge(s[f"x_loaded{h % 2}"], 16 * (h // 2 + 1))
                    if h >= 2:
                        act.wait_ge(s["summed"], h - 1)
                    nc.scalar.activation(sq[:, h % 2, :], x[:, h % 2, :], ACT.Square).then_inc(s["squared"], 1)
                act.wait_ge(s["mean"], 1)
                nc.scalar.activation(inv[:], mean[:], ACT.Sqrt).then_inc(s["root"], 1)

            @block.tensor
            def _(pe):
                for h in range(DN_HEADS):
                    pe.wait_ge(s["squared"], h + 1)
                    for n in range(NC):
                        col = h * NC + n
                        mm = nc.tensor.matmul(ps[:, 0, col:col + 1], sq[:, h % 2, n * P:(n + 1) * P], c.ones[:, 0:1],
                                              start=True, stop=True)
                    mm.then_inc(s["summed"], 1)
                pe.wait_ge(s["inv"], 1)
                nc.tensor.transpose(ps[0:n_rows, 1, 0:P], mean[:].rearrange("p h c -> p (h c)"), c.ident[:]) \
                    .then_inc(s["turned"], 1)

            @block.vector
            def _(dve):
                dve.wait_ge(s["den_loaded"], 16 * ATT_HEADS)
                nc.vector.reciprocal(den_inv[:], den[:]).then_inc(s["den_done"], 1)
                dve.wait_ge(s["summed"], DN_HEADS)
                nc.vector.scalar_tensor_tensor(out=mean[:].rearrange("p h c -> p (h c)"), in0=ps[:, 0, 0:n_rows],
                                               scalar=1.0 / DN_D, in1=c.q_eps[:].rearrange("p h c -> p (h c)"),
                                               op0=ALU.mult, op1=ALU.add).then_inc(s["mean"], 1)
                dve.wait_ge(s["root"], 1)
                nc.vector.reciprocal(mean[:], inv[:]).then_inc(s["inv"], 1)
                dve.wait_ge(s["turned"], 1)
                nc.vector.tensor_copy(rows[0:n_rows, :], ps[0:n_rows, 1, 0:P]).then_inc(s["copied"], 1)


def output_projection(nc, a, c, l):
    names = ("w_loaded0 w_loaded1 scaled gated y_hi y_lo w_hi w_lo proj_done psum_free squared summed "
             "xr_loaded0 xr_loaded1 x_stored0 x_stored1 small_loaded passed "
             + " ".join(f"tile_loaded{k}" for k in range(KT)))
    with ExitStack() as stack, semaphores(nc, names) as s:
        b = Buffers(nc, stack, "out")
        y_hi = b.sbuf("y_hi", [P, KT, SEQ], F32R)
        y_lo = b.sbuf("y_lo", [P, KT, SEQ], F32R)
        w_raw = b.sbuf("w_raw", [P, 2, KT * P])
        w_hi = b.sbuf("w_hi", [P, 2, KT, P], F32R)
        w_lo = b.sbuf("w_lo", [P, 2, KT, P], F32R)
        norm = b.sbuf("norm", [P, 1])
        x = b.sbuf("x", [P, 3, SEQ])
        acc = c.sq_acc
        ps = b.banks()
        with nc.Block() as block:

            @block.sync
            def _(sp):
                sp.dma_start(norm[:], a.dn_norm_w[l]).then_inc(s["small_loaded"], 16)
                for u in range(2):
                    sp.dma_start(w_raw[:, u, :], a.w_out[l, u]).then_inc(s[f"w_loaded{u}"], 16)
                for k in range(KT):
                    loaded = s[f"tile_loaded{k}"]
                    if k >= 3:
                        sp.wait_ge(s["y_lo"], k - 2)
                    if k < DN_HEADS:
                        sp.dma_start(x[:, k % 3, :], a.dn_o[k]).then_inc(loaded, 16)
                        sp.dma_start(y_hi[:, k, :].bitcast(F32), a.o_rows[k].partition_broadcast(P)).then_inc(loaded, 16)
                        sp.dma_start(y_lo[:, k, :].bitcast(F32), a.proj[T_Z + k]).then_inc(loaded, 16)
                    else:
                        for half in range(2):
                            h = 2 * (k - DN_HEADS) + half
                            rows = slice(half * DH, (half + 1) * DH)
                            sp.dma_start(x[rows, k % 3, :], a.att_o[h, 0:DH]).then_inc(loaded, 16)
                            sp.dma_start(y_hi[rows, k, :].bitcast(F32), a.den_rows[h].partition_broadcast(DH)).then_inc(loaded, 16)
                        sp.dma_start(y_lo[:, k, :].bitcast(F32), a.proj[T_Z + k]).then_inc(loaded, 16)
                sp.wait_ge(s["y_lo"], KT)
                with sp.Fori(0, KT // 2) as i:
                    for u in range(2):
                        wait_in_loop(sp, s, f"x_stored{u}", 16 * i)
                        wait_in_loop(sp, s, "squared", i * 2)
                        sp.dma_start(x[:, u, :], a.x_res[i * 2 + u]).then_inc(s[f"xr_loaded{u}"], 16)
                    for u in range(2):
                        wait_in_loop(sp, s, "psum_free", 2 * (i * 2 + u) + 6)
                        sp.dma_start(a.x_res[i * 2 + u], x[:, u, :]).then_inc(s[f"x_stored{u}"], 16)
                        wait_in_loop(sp, s, "w_lo", i * 2 + u + 1)
                        at = (i * 2 + u + 2) % KT
                        sp.dma_start(w_raw[:, u, :], a.w_out[l, at]).then_inc(s[f"w_loaded{u}"], 16)
                for u in range(2):
                    sp.wait_ge(s[f"x_stored{u}"], 16 * (KT // 2))
                    sp.wait_ge(s[f"w_loaded{u}"], 16 * (KT // 2 + 1))

            @block.tensor
            def _(pe):
                pe.wait_ge(s["w_lo"], 2)
                for k in range(KT):
                    pe.wait_ge(s["y_lo"], k + 1)
                    for u in range(2):
                        for w, y in ((w_hi, y_hi), (w_hi, y_lo), (w_lo, y_hi)):
                            for n in range(NQ):
                                mm = nc.tensor.matmul(ps[:, NQ * u + n, :], w[:, u, k, :], y[:, k, n * QB:(n + 1) * QB],
                                                      start=(k == 0 and w is w_hi and y is y_hi), stop=(k == KT - 1 and w is w_lo))
                        if k == KT - 1:
                            mm.then_inc(s["proj_done"], 2)
                with pe.Fori(1, KT // 2) as i:
                    for u in range(2):
                        t = i * 2 + u
                        pe.wait_ge(s["w_lo"], t + 1)
                        for half in range(2):
                            pe.wait_ge(s["psum_free"], 2 * t + half + 1)
                            for k in range(KT):
                                for w, y in ((w_hi, y_hi), (w_hi, y_lo), (w_lo, y_hi)):
                                    for n in range(2):
                                        at = half * HALF + n * QB
                                        mm = nc.tensor.matmul(
                                            ps[:, NQ * u + 2 * half + n, :], w[:, u, k, :], y[:, k, at:at + QB],
                                            start=(k == 0 and w is w_hi and y is y_hi), stop=(k == KT - 1 and w is w_lo))
                            mm.then_inc(s["proj_done"], 1)

            @block.gpsimd
            def _(pool):
                pool.sem_inc(s["psum_free"], 4)

            @block.scalar
            def _(act):
                for u in range(2):
                    act.wait_ge(s[f"w_loaded{u}"], 16)
                    nc.scalar.copy(w_hi[:, u].rearrange("p k m -> p (k m)"), w_raw[:, u, :]).then_inc(s["w_hi"], 1)
                for k in range(KT):
                    act.wait_ge(s["gated"], k + 1)
                    nc.scalar.copy(y_hi[:, k, :], x[:, k % 3, :]).then_inc(s["y_hi"], 1)
                with act.Fori(0, KT // 2) as i:
                    for u in range(2):
                        t = i * 2 + u
                        act.wait_ge(s["psum_free"], 2 * t + 6)
                        act.wait_ge(s["summed"], t + 1)
                        nc.scalar.activation(x[:, 2, :], x[:, u, :], ACT.Square).then_inc(s["squared"], 1)
                        act.wait_ge(s[f"w_loaded{u}"], 16 * i + 32)
                        act.wait_ge(s["proj_done"], 2 * t + 2)
                        nc.scalar.copy(w_hi[:, u].rearrange("p k m -> p (k m)"), w_raw[:, u, :]).then_inc(s["w_hi"], 1)

            @block.vector
            def _(dve):
                dve.wait_ge(s["small_loaded"], 16)

                def split_y(k):
                    dve.wait_ge(s["y_hi"], k + 1)
                    nc.vector.tensor_tensor(y_lo[:, k, :], x[:, k % 3, :], y_hi[:, k, :].bitcast(F32),
                                            ALU.subtract).then_inc(s["y_lo"], 1)

                def split_w(u):
                    nc.vector.tensor_tensor(w_lo[:, u].rearrange("p k m -> p (k m)"), w_raw[:, u, :],
                                            w_hi[:, u].rearrange("p k m -> p (k m)").bitcast(F32),
                                            ALU.subtract).then_inc(s["w_lo"], 1)

                for u in range(2):
                    dve.wait_ge(s["w_hi"], u + 1)
                    split_w(u)
                for k in range(KT):
                    xs = x[:, k % 3, :]
                    dve.wait_ge(s[f"tile_loaded{k}"], 48 if k < DN_HEADS else 80)
                    if k < DN_HEADS:
                        nc.vector.scalar_tensor_tensor(out=xs, in0=xs, scalar=norm[:, 0:1], in1=y_hi[:, k, :].bitcast(F32),
                                                       op0=ALU.mult, op1=ALU.mult).then_inc(s["scaled"], 1)
                    else:
                        nc.vector.tensor_tensor(xs, xs, y_hi[:, k, :].bitcast(F32), ALU.mult).then_inc(s["scaled"], 1)
                    dve.wait_ge(s["scaled"], k + 1)
                    nc.vector.tensor_tensor(xs, xs, y_lo[:, k, :].bitcast(F32), ALU.mult).then_inc(s["gated"], 1)
                    if k:
                        split_y(k - 1)
                split_y(KT - 1)
                dve.wait_ge(s["y_lo"], KT)
                nc.vector.memset(acc[:], 0.0).then_inc(s["summed"], 1)
                with dve.Fori(0, KT // 2) as i:
                    for u in range(2):
                        t = i * 2 + u
                        dve.wait_ge(s[f"xr_loaded{u}"], 16 * i + 16)
                        for half in range(2):
                            dve.wait_ge(s["proj_done"], 2 * t + half + 1)
                            xs = x[:, u, half * HALF:(half + 1) * HALF]
                            nc.vector.tensor_tensor(xs, ps[:, NQ * u + 2 * half:NQ * u + 2 * half + 2, :]
                                                    .rearrange("p b n -> p (b n)"), xs,
                                                    ALU.add).then_inc(s["psum_free"], 1)
                        dve.wait_ge(s["squared"], t + 1)
                        dve.wait_ge(s["summed"], t + 1)
                        nc.vector.tensor_tensor(acc[:], acc[:], x[:, 2, :], ALU.add).then_inc(s["summed"], 1)
                        dve.wait_ge(s["w_hi"], t + 3)
                        split_w(u)


def layer_rest(nc, a, c, l):
    if PHASES >= 2:
        token_tables(nc, a, c, l)
        attention_inputs(nc, a, c, l)
    if PHASES >= 3:
        delta_net(nc, a, c, l)
    if PHASES >= 4:
        attention(nc, a, c, l)
    if PHASES >= 5:
        branch_scales(nc, a, c, l)
        with ExitStack() as stack:
            c.sq_acc = stack.enter_context(nc.sbuf_tensor("sq_acc", [P, SEQ], F32))
            output_projection(nc, a, c, l)
            token_scales(nc, a, c, "layer")


def finish(nc, a, c):
    with ExitStack() as stack, semaphores(nc, "const_loaded x_loaded0 x_loaded1 normed stored0 stored1 passed") as s:
        b = Buffers(nc, stack, "fin")
        x = b.sbuf("x", [P, 2, SEQ])
        r = b.sbuf("r", [P, SEQ])
        w = b.sbuf("w", [P, KT])
        with nc.Block() as block:

            @block.sync
            def _(sp):
                sp.dma_start(w[:], a.norm_w[DEPTH]).then_inc(s["const_loaded"], 16)
                sp.dma_start(r[:], a.x_scale.partition_broadcast(P)).then_inc(s["const_loaded"], 16)
                for k in range(KT):
                    if k >= 2:
                        sp.wait_ge(s[f"stored{k % 2}"], 16 * (k // 2))
                    sp.dma_start(x[:, k % 2, :], a.x_res[k]).then_inc(s[f"x_loaded{k % 2}"], 16)

            @block.vector
            def _(dve):
                dve.wait_ge(s["const_loaded"], 32)
                for k in range(KT):
                    dve.wait_ge(s[f"x_loaded{k % 2}"], 16 * (k // 2 + 1))
                    nc.vector.scalar_tensor_tensor(out=x[:, k % 2, :], in0=x[:, k % 2, :], scalar=w[:, k:k + 1],
                                                   in1=r[:], op0=ALU.mult, op1=ALU.mult).then_inc(s["normed"], 1)

            @block.scalar
            def _(act):
                for k in range(KT):
                    act.wait_ge(s["normed"], k + 1)
                    act.dma_start(a.out[k], x[:, k % 2, :]).then_inc(s[f"stored{k % 2}"], 16)
                for u in range(2):
                    act.wait_ge(s[f"stored{u}"], 16 * (KT // 2))


class Arrays:
    pass


def constants():
    f = np.float32
    i = np.arange(P)
    j, t = i[:, None], i[None, :]
    masks = np.zeros((P, N_DIR, LEVELS + 1, P), f)
    for lv in range(LEVELS):
        s = 1 << lv
        upper = (j // (2 * s) == t // (2 * s)) & (j // s < t // s)
        masks[:, 0, lv] = upper
        masks[:, 1, lv] = upper.T
    masks[:, 0, LEVELS] = j <= t
    masks[:, 1, LEVELS] = j >= t
    masks[:, :, 0] *= -1
    ind = np.zeros((P, 2), f)
    ind[:DH, 0] = 1
    ind[DH:, 1] = 1
    half = DH // 2
    inv = (f(10000.0) ** (-np.arange(0, half, 2, dtype=f) / f(half))).astype(f)
    tok = np.arange(SEQ)
    ang = np.zeros((P, SEQ), f)
    sign = np.zeros((P, 1))
    for p in range(P):
        d = p % DH
        pos = (tok // DH if d < half else tok % DH).astype(f)
        ang[p] = pos * inv[d % (half // 2)]
        sign[p] = -1 if d % half < half // 2 else 1
    cos = np.cos(ang.astype(np.float64)).astype(f)
    sin = (sign * np.sin(ang.astype(np.float64))).astype(f)
    quarter = np.zeros((NQ, NQ, 1), f)
    quarter[np.arange(NQ), np.arange(NQ)] = -1
    return {"masks": masks, "ident": np.eye(P, dtype=f), "ones": np.ones((P, P), f), "halves": ind,
            "rope": np.stack([cos, sin]), "quarter": np.ascontiguousarray(np.broadcast_to(quarter, (NQ, NQ, P)))}


PHASES = 99


def build(nc, a):
    c = Arrays()
    dram = lambda n, shape, dt=F32: nc.dram_tensor(n, shape, dt, kind="Internal").ap()
    a.x_res = dram("x_res", (KT, P, SEQ))
    a.x_scale = dram("x_scale", (SEQ,))
    a.ba = dram("ba", (2 * W_BA, SEQ))
    a.proj = dram("proj", (N_TILES, P, SEQ))
    scratch(a, dram)
    with ExitStack() as stack:
        sb = lambda n, shape: stack.enter_context(nc.sbuf_tensor(n, shape, F32))
        c.ident = sb("c_ident", [P, P])
        c.ones = sb("c_ones", [P, P])
        c.eps = sb("c_eps", [P, 2])
        c.halves = sb("c_halves", [P, 2])
        c.sums = sb("c_sums", [P, T_Z - T_Q, NC, 2])
        c.tok = sb("c_tok", [P, NC, TABLES, ITEMS])
        c.v_scale = sb("c_v_scale", [P, NC, DN_HEADS])
        c.q_eps = sb("c_q_eps", [P, DN_HEADS, NC])
        c.sq_acc = None
        with semaphores(nc, "loaded set_up") as s:
            with nc.Block() as block:
                @block.sync
                def _(sp):
                    sp.dma_start(c.ident[:], a.ident).then_inc(s["loaded"], 16)
                    sp.dma_start(c.ones[:], a.ones).then_inc(s["loaded"], 16)
                    sp.dma_start(c.halves[:], a.halves).then_inc(s["loaded"], 16)
                    sp.wait_ge(s["loaded"], 48)

                @block.vector
                def _(dve):
                    nc.vector.memset(c.eps[:], EPS).then_inc(s["set_up"], 1)
        with ExitStack() as inner:
            c.sq_acc = inner.enter_context(nc.sbuf_tensor("sq_acc_in", [P, SEQ], F32))
            load_input(nc, a, c)
            token_scales(nc, a, c, "input")
        with nc.Fori(0, DEPTH) as l:
            if PHASES >= 1:
                input_projection(nc, a, c, l)
            layer_rest(nc, a, c, l)
        finish(nc, a, c)


_SHAPES = ["x_in", "w_in", "w_ba", "norm_w", "decay", "dn_norm_w", "qk_norm_w", "w_out",
           "masks", "ident", "ones", "halves", "rope", "quarter"]


def lay_out(x, norm_w, w_in, conv_w, a_log, dt_bias, dn_norm_w, q_norm_w, k_norm_w, w_out, final_norm_w):
    depth = w_in.shape[0]
    g = {"x_in": np.asarray(x)[0].T.reshape(KT, P, SEQ)}
    w = np.asarray(w_in)
    conv = DN_HEADS * P
    at_z = 3 * conv
    at_ba = at_z + conv
    at_q = at_ba + W_BA
    at_v = at_q + ATT_HEADS * DH + KV_HEADS * DH
    at_gate = at_v + KV_HEADS * DH
    order = np.concatenate([np.arange(2 * conv, 3 * conv), np.arange(0, 2 * conv), np.arange(at_q, at_gate),
                            np.arange(at_z, at_ba), np.arange(at_gate, w.shape[2])])
    tiles = w[:, :, order].reshape(depth, KT, P, N_TILES, P).transpose(0, 3, 2, 1, 4).reshape(depth, N_TILES, P, KT * P)
    taps = np.zeros((depth, N_TILES, P, WCOLS - KT * P), w.dtype)
    conv_order = order[:CONV_TILES * P]
    taps[:, :CONV_TILES, :, :CONV_K] = np.asarray(conv_w)[:, :, conv_order].reshape(
        depth, CONV_K, CONV_TILES, P).transpose(0, 2, 3, 1)
    g["w_in"] = np.concatenate([tiles, taps], axis=3)
    g["w_ba"] = w[:, :, at_ba:at_q].reshape(depth, KT, P, W_BA).transpose(0, 2, 1, 3)
    norms = np.concatenate([np.asarray(norm_w), np.asarray(final_norm_w)[None]])
    g["norm_w"] = norms.reshape(depth + 1, KT, P).transpose(0, 2, 1)
    g["decay"] = np.stack([np.asarray(a_log).reshape(depth, ITEMS), np.asarray(dt_bias).reshape(depth, ITEMS)], axis=1)
    g["dn_norm_w"] = np.asarray(dn_norm_w)[:, :, None]
    swap = np.arange(DH).reshape(4, DH // 4)[[1, 0, 3, 2]].reshape(-1)
    q, k = np.asarray(q_norm_w), np.asarray(k_norm_w)
    g["qk_norm_w"] = np.stack([np.concatenate([v, v], axis=1) for v in (q, q[:, swap], k, k[:, swap])], axis=2)
    g["w_out"] = np.asarray(w_out).reshape(depth, KT, P, KT, P).transpose(0, 3, 2, 1, 4).reshape(depth, KT, P, KT * P)
    g.update(constants())
    return {n: np.ascontiguousarray(v) for n, v in g.items()}


def kernel(**inputs):
    import concourse.bacc as bacc
    from concourse.bass_utils import run_bass_kernel_spmd

    nc = bacc.Bacc("TRN2", target_bir_lowering=False, num_devices=1)
    g = lay_out(**inputs)
    a, arrays = Arrays(), {}
    a_dict = a.__dict__
    for name in _SHAPES:
        arrays[f"in_{name}"] = g[name]
        a_dict[name] = nc.dram_tensor(f"in_{name}", g[name].shape, mybir.dt.from_np(g[name].dtype),
                                      kind="ExternalInput").ap()
    a.out = nc.dram_tensor("out_T", (KT, P, SEQ), F32, kind="ExternalOutput").ap()
    build(nc, a)
    r = run_bass_kernel_spmd(nc, [arrays], core_ids=[0])
    out = r.results[0]["out_T"]
    return np.ascontiguousarray(out.reshape(D_MODEL, SEQ).T)[None]
```

```python
from contextlib import ExitStack, contextmanager

import numpy as np

import concourse.bass as bass
from concourse import mybir

P = 128
F32 = mybir.dt.float32
F32R = mybir.dt.float32r
ALU = mybir.AluOpType
ACT = mybir.ActivationFunctionType
AX = mybir.AxisListType

SEQ = 2048
D_MODEL = 1024
DEPTH = 2
KT = D_MODEL // P
NC = SEQ // P
QB = 512
NQ = SEQ // QB
HALF = SEQ // 2
CONV_K = 5
PADW = SEQ + CONV_K - 1
EPS = 1e-6

DN_HEADS = 4
N_DIR = 2
ITEMS = N_DIR * DN_HEADS
ATT_HEADS = 8
KV_HEADS = 2
GROUP = ATT_HEADS // KV_HEADS
DH = 64
SCALE = float(DH) ** -0.5
LEVELS = 7

CONV_TILES = 3 * DN_HEADS
T_V, T_Q, T_K = 0, DN_HEADS, 2 * DN_HEADS
T_AQ = CONV_TILES
T_AK = T_AQ + ATT_HEADS // 2
T_AV = T_AK + 1
T_Z = T_AV + 1
N_TILES = T_Z + 8
WCOLS = KT * P + 8
W_BA = 2 * ITEMS


@contextmanager
def semaphores(nc, names):
    with ExitStack() as stack:
        sems = {n: stack.enter_context(nc.semaphore(n)) for n in names.split()}
        yield sems
        for s in sems.values():
            nc.sync.sem_clear(s)
        nc.all_engine_barrier()


class Buffers:

    def __init__(self, nc, stack, phase):
        self.nc, self.stack, self.phase = nc, stack, phase

    def sbuf(self, name, shape, dtype=F32):
        return self.stack.enter_context(self.nc.sbuf_tensor(f"{self.phase}_sb_{name}", shape, dtype))

    def banks(self):
        return self.stack.enter_context(self.nc.psum_tensor(f"{self.phase}_banks", [P, 8, QB], F32))


def wait_in_loop(sp, s, name, value):
    sp.wait_ge(s[name], value)
    sp.sem_inc(s["passed"], 1)


def load_input(nc, a, c):
    with ExitStack() as stack, semaphores(nc, "x_loaded0 x_loaded1 x_stored0 x_stored1 squared summed passed") as s:
        b = Buffers(nc, stack, "load")
        x = b.sbuf("x", [P, 2, SEQ])
        sq = b.sbuf("sq", [P, 2, SEQ])
        acc = c.sq_acc
        with nc.Block() as block:

            @block.sync
            def _(sp):
                with sp.Fori(0, KT // 2) as i:
                    for u in range(2):
                        wait_in_loop(sp, s, "squared", 2 * i)
                        wait_in_loop(sp, s, f"x_stored{u}", 16 * i)
                        sp.dma_start(x[:, u, :], a.x_in[i * 2 + u]).then_inc(s[f"x_loaded{u}"], 16)
                    for u in range(2):
                        wait_in_loop(sp, s, f"x_loaded{u}", 16 * i + 16)
                        sp.dma_start(a.x_res[i * 2 + u], x[:, u, :]).then_inc(s[f"x_stored{u}"], 16)
                for u in range(2):
                    sp.wait_ge(s[f"x_stored{u}"], KT // 2 * 16)

            @block.scalar
            def _(act):
                with act.Fori(0, KT // 2) as i:
                    for u in range(2):
                        act.wait_ge(s[f"x_loaded{u}"], 16 * i + 16)
                        act.wait_ge(s["summed"], 2 * i + u)
                        nc.scalar.activation(sq[:, u, :], x[:, u, :], ACT.Square).then_inc(s["squared"], 1)

            @block.vector
            def _(dve):
                nc.vector.memset(acc[:], 0.0).then_inc(s["summed"], 1)
                with dve.Fori(0, KT // 2) as i:
                    for u in range(2):
                        dve.wait_ge(s["squared"], 2 * i + u + 1)
                        dve.wait_ge(s["summed"], 2 * i + u + 1)
                        nc.vector.tensor_tensor(acc[:], acc[:], sq[:, u, :], ALU.add).then_inc(s["summed"], 1)


def token_scales(nc, a, c, when):
    with ExitStack() as stack, semaphores(nc, "sums root scale turned copied stored") as s:
        b = Buffers(nc, stack, "scales_" + when)
        table = b.sbuf("table", [P, NC])
        inv = b.sbuf("inv", [P, NC])
        rows = b.sbuf("rows", [NC, P])
        ps = b.banks()
        with nc.Block() as block:

            @block.tensor
            def _(pe):
                for t in range(NC):
                    mm = nc.tensor.matmul(ps[:, 0, t:t + 1], c.sq_acc[:, t * P:(t + 1) * P], c.ones[:, 0:1],
                                          start=True, stop=True)
                mm.then_inc(s["sums"], 1)
                pe.wait_ge(s["scale"], 1)
                nc.tensor.transpose(ps[0:NC, 1, 0:P], inv[:], c.ident[:]).then_inc(s["turned"], 1)

            @block.scalar
            def _(act):
                act.wait_ge(s["sums"], 1)
                nc.scalar.activation(table[:], ps[:, 0, 0:NC], ACT.Sqrt, bias=c.eps[:, 0:1],
                                     scale=1.0 / D_MODEL).then_inc(s["root"], 1)

            @block.vector
            def _(dve):
                dve.wait_ge(s["root"], 1)
                nc.vector.reciprocal(inv[:], table[:]).then_inc(s["scale"], 1)
                dve.wait_ge(s["turned"], 1)
                nc.vector.tensor_copy(rows[:], ps[0:NC, 1, 0:P]).then_inc(s["copied"], 1)

            @block.sync
            def _(sp):
                sp.wait_ge(s["copied"], 1)
                sp.dma_start(a.x_scale.rearrange("(c p) -> c p", p=P), rows[:]).then_inc(s["stored"], 16)
                sp.wait_ge(s["stored"], 16)


def input_projection(nc, a, c, l):
    names = ("x_loaded0 x_loaded1 x_loaded2 x_loaded3 scale_loaded small_loaded normed h_hi h_lo w_loaded0 w_loaded1 w_hi w_lo "
             "proj_done psum_free passed "
             "conv_step taps_kept conv_done out_ready out_stored0 out_stored1 ba_hi ba_split ba_stored edges "
             "squared stats_done")
    with ExitStack() as stack, semaphores(nc, names) as s:
        b = Buffers(nc, stack, "proj")
        h_hi = b.sbuf("h_hi", [P, KT, SEQ], F32R)
        h_lo = b.sbuf("h_lo", [P, KT, SEQ], F32R)
        pad = b.sbuf("pad", [P, 2, PADW])
        out = b.sbuf("out", [P, 2, SEQ])
        w_raw = b.sbuf("w_raw", [P, 2, WCOLS])
        w_hi = b.sbuf("w_hi", [P, 2, KT, P], F32R)
        w_lo = b.sbuf("w_lo", [P, 2, KT, P], F32R)
        nw = b.sbuf("nw", [P, KT])
        sq = b.sbuf("sq", [P, SEQ])
        taps = b.sbuf("taps", [P, 2, WCOLS - KT * P])
        ba_raw = b.sbuf("ba_raw", [P, KT, W_BA])
        ba_w = b.sbuf("ba_w", [P, KT, 2 * W_BA], F32R)
        ps = b.banks()
        scale = out[:, 1, :]
        xs = [pad[:, 0, 0:SEQ], pad[:, 1, 0:SEQ], out[:, 0, :], sq[:]]

        with nc.Block() as block:

            @block.sync
            def _(sp):
                sp.dma_start(nw[:], a.norm_w[l]).then_inc(s["small_loaded"], 16)
                sp.dma_start(ba_raw[:], a.w_ba[l]).then_inc(s["small_loaded"], 16)
                sp.dma_start(scale, a.x_scale.partition_broadcast(P)).then_inc(s["scale_loaded"], 16)
                for k in range(KT):
                    if k >= 4:
                        sp.wait_ge(s["h_lo"], k - 3)
                    sp.dma_start(xs[k % 4], a.x_res[k]).then_inc(s[f"x_loaded{k % 4}"], 16)
                    if k < 2:
                        sp.dma_start(w_raw[:, k, :], a.w_in[l, k]).then_inc(s[f"w_loaded{k}"], 16)
                sp.wait_ge(s["out_ready"], 1)
                sp.dma_start(a.ba, out[0:2 * W_BA, 0, :]).then_inc(s["ba_stored"], 16)
                sp.wait_ge(s["ba_stored"], 16)
                for u in range(2):
                    sp.sem_inc(s[f"out_stored{u}"], 16)
                with sp.Fori(0, N_TILES // 2 - 1) as i:
                    for u in range(2):
                        t = i * 2 + u
                        wait_in_loop(sp, s, "w_lo", t + 1)
                        sp.dma_start(w_raw[:, u, :], a.w_in[l, t + 2]).then_inc(s[f"w_loaded{u}"], 16)
                        wait_in_loop(sp, s, "out_ready", t + 2)
                        sp.dma_start(a.proj[t], out[:, u, :]).then_inc(s[f"out_stored{u}"], 16)
                for u in range(2):
                    t = N_TILES - 2 + u
                    sp.wait_ge(s["out_ready"], t + 2)
                    sp.dma_start(a.proj[t], out[:, u, :]).then_inc(s[f"out_stored{u}"], 16)
                for u in range(2):
                    sp.wait_ge(s[f"out_stored{u}"], 16 * (N_TILES // 2 + 1))

            @block.tensor
            def _(pe):
                pe.wait_ge(s["ba_split"], 2)
                pe.wait_ge(s["w_hi"], 1)
                pe.wait_ge(s["w_lo"], 1)
                for k in range(KT):
                    pe.wait_ge(s["h_lo"], k + 1)
                    for part, h in enumerate((h_hi, h_lo)):
                        for n in range(NQ):
                            mm = nc.tensor.matmul(ps[0:2 * W_BA, 4 + n, :], ba_w[:, k, :],
                                                  h[:, k, n * QB:(n + 1) * QB],
                                                  start=(k == 0 and part == 0), stop=(k == KT - 1 and part == 1))
                    if k == KT - 1:
                        mm.then_inc(s["proj_done"], 2)
                    for w, h in ((w_hi, h_hi), (w_hi, h_lo), (w_lo, h_hi)):
                        for n in range(NQ):
                            mm = nc.tensor.matmul(ps[:, n, :], w[:, 0, k, :], h[:, k, n * QB:(n + 1) * QB],
                                                  start=(k == 0 and w is w_hi and h is h_hi), stop=(k == KT - 1 and w is w_lo))
                mm.then_inc(s["proj_done"], 2)

                def tile_half(i, u, half, sums=()):
                    t = i * 2 + u
                    pe.wait_ge(s["w_hi"], t + 1)
                    pe.wait_ge(s["w_lo"], t + 1)
                    pe.wait_ge(s["psum_free"], 2 * t + half + 1)
                    between = list(sums)
                    for k in range(KT):
                        for w, h in ((w_hi, h_hi), (w_hi, h_lo), (w_lo, h_hi)):
                            if between:
                                between.pop(0)()
                            for n in range(2):
                                at = half * HALF + n * QB
                                mm = nc.tensor.matmul(
                                    ps[:, 2 * half + n, :], w[:, u, k, :], h[:, k, at:at + QB],
                                    start=(k == 0 and w is w_hi and h is h_hi), stop=(k == KT - 1 and w is w_lo))
                    mm.then_inc(s["proj_done"], 1)

                def square_sum(i, u, n):
                    t = i * 2 + u
                    if n == 0:
                        pe.wait_ge(s["squared"], t + 3)
                    col = (t - T_Q) * 2 * NC + 2 * n
                    mm = nc.tensor.matmul(ps[:, 4, bass.ds(col, 2)], sq[:, n * P:(n + 1) * P], c.halves[:],
                                          start=True, stop=True)
                    if n == NC - 1:
                        mm.then_inc(s["stats_done"], 1)

                for half in range(2):
                    tile_half(0, 1, half)
                with pe.Fori(1, T_Q // 2 + 1) as i:
                    for u in range(2):
                        for half in range(2):
                            tile_half(i, u, half)
                pe.wait_ge(s["out_ready"], 1)
                with pe.Fori(T_Q // 2 + 1, T_Z // 2 + 1) as i:
                    for u in range(2):
                        tile_half(i, u, 0)
                        tile_half(i, u, 1, [lambda n=n: square_sum(i - 1, u, n) for n in range(NC)])
                with pe.Fori(T_Z // 2 + 1, N_TILES // 2) as i:
                    for u in range(2):
                        for half in range(2):
                            tile_half(i, u, half)

            @block.gpsimd
            def _(pool):
                pool.sem_inc(s["squared"], T_Q + 2)
                with pool.Fori(T_Q // 2, T_Z // 2) as i:
                    for u in range(2):
                        t = i * 2 + u
                        pool.wait_ge(s["out_ready"], t + 2)
                        pool.wait_ge(s["stats_done"], t - T_Q)
                        nc.gpsimd.tensor_tensor(sq[:], out[:, u, :], out[:, u, :], ALU.mult).then_inc(s["squared"], 1)

            @block.scalar
            def _(act):
                act.wait_ge(s["small_loaded"], 32)
                nc.scalar.copy(ba_w[:, :, 0:W_BA], ba_raw[:]).then_inc(s["ba_hi"], 1)
                for k in range(KT):
                    act.wait_ge(s["normed"], k + 1)
                    nc.scalar.copy(h_hi[:, k, :], xs[k % 4]).then_inc(s["h_hi"], 1)
                    if k == 0:
                        act.wait_ge(s["w_loaded0"], 16)
                        nc.scalar.copy(w_hi[:, 0].rearrange("p k m -> p (k m)"), w_raw[:, 0, 0:KT * P]).then_inc(s["w_hi"], 1)

                def split_hi(t, i, u):
                    act.wait_ge(s[f"w_loaded{u}"], 16 * i + 16)
                    act.wait_ge(s["proj_done"], 2 * t)
                    nc.scalar.copy(w_hi[:, u].rearrange("p k m -> p (k m)"), w_raw[:, u, 0:KT * P]).then_inc(s["w_hi"], 1)

                def evacuate(t, u, half, dst, func):
                    act.wait_ge(s["proj_done"], 2 * t + half + 3)
                    src = ps[:, 2 * half:2 * half + 2, :].rearrange("p b n -> p (b n)")
                    return nc.scalar.activation(dst, src, func)

                act.wait_ge(s["proj_done"], 2)
                nc.scalar.copy(out[0:2 * W_BA, 0, :], ps[0:2 * W_BA, 4:8, :].rearrange("p b n -> p (b n)")) \
                    .then_inc(s["out_ready"], 1)
                act.wait_ge(s["out_ready"], 1)
                act.sem_inc(s["psum_free"], 2)
                with act.Fori(0, CONV_TILES // 2) as i:
                    for u in range(2):
                        t = i * 2 + u
                        split_hi(t + 1, i + u, 1 - u)
                        for half in range(2):
                            lo = CONV_K // 2 + half * HALF
                            act.wait_ge(s["conv_done"], t + 1)
                            evacuate(t, u, half, pad[:, u, lo:lo + HALF], ACT.Copy).then_inc(s["psum_free"], 1)
                        act.wait_ge(s["conv_done"], t + 3)
                        nc.scalar.activation(out[:, u, :], out[:, u, :], ACT.Silu).then_inc(s["out_ready"], 1)

                def plain(i, u, func, more, squares=False):
                    t = i * 2 + u
                    if more:
                        split_hi(t + 1, i + u, 1 - u)
                    act.wait_ge(s[f"out_stored{u}"], 16 * i + 16)
                    if squares:
                        act.wait_ge(s["squared"], t + 1)
                    for half in range(2):
                        e = evacuate(t, u, half, out[:, u, half * HALF:(half + 1) * HALF], func)
                        e.then_inc(s["psum_free"], 1)
                    act.wait_ge(s["psum_free"], 2 * t + 4)
                    act.sem_inc(s["out_ready"], 1)

                with act.Fori(T_AQ // 2, T_Z // 2) as i:
                    for u in range(2):
                        plain(i, u, ACT.Copy, True, True)
                for u in range(2):
                    plain(T_Z // 2, u, ACT.Silu, True, True)
                with act.Fori(T_Z // 2 + 1, N_TILES // 2 - 1) as i:
                    for u in range(2):
                        plain(i, u, ACT.Silu, True)
                plain(N_TILES // 2 - 1, 0, ACT.Silu, True)
                plain(N_TILES // 2 - 1, 1, ACT.Silu, False)

            @block.vector
            def _(dve):
                dve.wait_ge(s["scale_loaded"], 16)
                dve.wait_ge(s["small_loaded"], 32)

                def split_h(k):
                    dve.wait_ge(s["h_hi"], k + 1)
                    nc.vector.tensor_tensor(h_lo[:, k, :], xs[k % 4], h_hi[:, k, :].bitcast(F32),
                                            ALU.subtract).then_inc(s["h_lo"], 1)

                def keep_taps(t, i, u):
                    dve.wait_ge(s[f"w_loaded{u}"], 16 * i + 16)
                    nc.vector.tensor_copy(taps[:, u, :], w_raw[:, u, KT * P:WCOLS]).then_inc(s["taps_kept"], 1)

                def split_w(t, u):
                    dve.wait_ge(s["w_hi"], t + 1)
                    nc.vector.tensor_tensor(w_lo[:, u].rearrange("p k m -> p (k m)"), w_raw[:, u, 0:KT * P],
                                            w_hi[:, u].rearrange("p k m -> p (k m)").bitcast(F32),
                                            ALU.subtract).then_inc(s["w_lo"], 1)

                for k in range(KT):
                    dve.wait_ge(s[f"x_loaded{k % 4}"], 16 * (k // 4) + 16)
                    nc.vector.scalar_tensor_tensor(out=xs[k % 4], in0=xs[k % 4],
                                                   scalar=nw[:, k:k + 1], in1=scale, op0=ALU.mult,
                                                   op1=ALU.mult).then_inc(s["normed"], 1)
                    if k >= 1:
                        split_h(k - 1)
                    if k == 1:
                        keep_taps(0, 0, 0)
                        split_w(0, 0)
                        dve.wait_ge(s["ba_hi"], 1)
                        nc.vector.tensor_tensor(ba_w[:, :, W_BA:2 * W_BA], ba_raw[:],
                                                ba_w[:, :, 0:W_BA].bitcast(F32), ALU.subtract).then_inc(s["ba_split"], 2)
                split_h(KT - 1)
                dve.wait_ge(s["h_lo"], KT)
                nc.vector.memset(pad[:, :, 0:CONV_K // 2], 0.0).then_inc(s["edges"], 1)
                nc.vector.memset(pad[:, :, PADW - CONV_K // 2:PADW], 0.0).then_inc(s["edges"], 1)
                dve.wait_ge(s["edges"], 2)
                dve.sem_inc(s["conv_done"], 2)
                with dve.Fori(0, CONV_TILES // 2) as i:
                    for u in range(2):
                        t = i * 2 + u
                        dve.wait_ge(s["conv_done"], t + 2)
                        keep_taps(t + 1, i + u, 1 - u)
                        split_w(t + 1, 1 - u)
                        dve.wait_ge(s["psum_free"], 2 * t + 4)
                        dve.wait_ge(s["squared"], t + 1)
                        dve.wait_ge(s[f"out_stored{u}"], 16 * i + 16)
                        dve.wait_ge(s["taps_kept"], t + 1)
                        for j in range(CONV_K):
                            if j:
                                dve.wait_ge(s["conv_step"], t * (CONV_K - 1) + j)
                            src = pad[:, u, j:j + SEQ]
                            done = s["conv_step"] if j < CONV_K - 1 else s["conv_done"]
                            if j == 0:
                                nc.vector.tensor_scalar(out[:, u, :], src, taps[:, u, j:j + 1], None, ALU.mult).then_inc(done, 1)
                            else:
                                nc.vector.scalar_tensor_tensor(out=out[:, u, :], in0=src, scalar=taps[:, u, j:j + 1],
                                                               in1=out[:, u, :], op0=ALU.mult, op1=ALU.add).then_inc(done, 1)
                with dve.Fori(CONV_TILES // 2, N_TILES // 2 - 1) as i:
                    for u in range(2):
                        split_w(i * 2 + u + 1, 1 - u)
                split_w(N_TILES - 1, 1)
                dve.wait_ge(s["stats_done"], T_Z - T_Q)
                nc.vector.tensor_copy(c.sums[:].rearrange("p t c h -> p (t c h)"),
                                      ps[:, 4, 0:(T_Z - T_Q) * 2 * NC]).then_inc(s["edges"], 1)
TABLES = 5
T_G, T_NEG, T_BETA, T_BETA_END, T_CHUNK = range(TABLES)
DN_D = P
N_QK = ATT_HEADS // 2 + 1


def scratch(a, dram):
    a.g_rows = dram("g_rows", (NC, ITEMS, P))
    a.qk_rows = dram("qk_rows", (N_QK * 2, SEQ))
    a.att_q = dram("att_q", (ATT_HEADS, P, SEQ))
    a.att_k = dram("att_k", (KV_HEADS, P, SEQ))
    a.att_v = dram("att_v", (P, NC, KV_HEADS, DH))
    a.dn_o = dram("dn_o", (DN_HEADS, P, SEQ))
    a.att_o = dram("att_o", (ATT_HEADS, DH + 1, SEQ))
    a.den_rows = dram("den_rows", (ATT_HEADS, SEQ))
    a.o_rows = dram("o_rows", (DN_HEADS, SEQ))


def token_inputs(nc, a, c, l):
    names = ("loaded ba_turned act_step dve_step summed g_copied turned copied stored att_root "
             "const_loaded rows_loaded v_loaded v_turned v_copied v_stored swapped spread "
             "cos_done sin_done rotated scaled hi lo stored0 stored1 " + " ".join(f"x_loaded{t}" for t in range(N_QK)))
    n_ba = 2 * ITEMS
    with ExitStack() as stack, semaphores(nc, names) as s:
        b = Buffers(nc, stack, "tab")
        ba = b.sbuf("ba", [2 * W_BA, SEQ])
        masks = b.sbuf("masks", [P, N_DIR, P])
        decay = b.sbuf("decay", [P, 2, ITEMS])
        x = b.sbuf("x", [P, NC, n_ba])
        low = b.sbuf("low", [P, NC, n_ba])
        beta = b.sbuf("beta", [P, NC, ITEMS])
        pos = b.sbuf("pos", [P, NC, ITEMS])
        mag = b.sbuf("mag", [P, NC, ITEMS])
        e = b.sbuf("e", [P, NC, ITEMS])
        u = b.sbuf("u", [P, NC, ITEMS])
        ln = b.sbuf("ln", [P, NC, ITEMS])
        inv = b.sbuf("inv", [P, NC, ITEMS])
        g = b.sbuf("g", [P, NC, ITEMS])
        rate = b.sbuf("rate", [P, ITEMS])
        end = b.sbuf("end", [P, NC, ITEMS])
        kk = b.sbuf("kk", [P, DN_HEADS, NC])
        rk2 = b.sbuf("rk2", [P, DN_HEADS, NC])
        att = b.sbuf("att", [P, N_QK, 2, NC])
        att_inv = b.sbuf("att_inv", [P, N_QK * 2 * NC])
        rows = b.sbuf("rows", [P, 3, P])
        rope = b.sbuf("rope", [P, 2, SEQ])
        swap = b.sbuf("swap", [P, P])
        halves_t = b.sbuf("halves_t", [2, P])
        qk_w = b.sbuf("qk_w", [P, 4])
        q = b.sbuf("q", [P, N_QK, SEQ])
        inv_rms = b.sbuf("inv_rms", [2, N_QK, SEQ])
        sin_part = b.sbuf("sin_part", [P, 2, SEQ])
        hi = b.sbuf("hi", [P, 2, SEQ], F32R)
        lo = b.sbuf("lo", [P, 2, SEQ], F32R)
        v = b.sbuf("v", [P, SEQ])
        vt = b.sbuf("vt", [P, NC, P])
        ps = b.banks()
        flat = lambda bank: ps[:, bank:bank + NQ, :].rearrange("p b n -> p (b n)")
        n_att = N_QK * 2 * NC
        with nc.Block() as block:

            @block.sync
            def _(sp):
                sp.dma_start(ba[:], a.ba).then_inc(s["loaded"], 16)
                sp.dma_start(masks[:], a.masks[:, :, LEVELS, :]).then_inc(s["loaded"], 16)
                sp.dma_start(decay[:], a.decay[l].partition_broadcast(P)).then_inc(s["loaded"], 16)
                sp.dma_start(v[:], a.proj[T_AV]).then_inc(s["v_loaded"], 16)
                sp.dma_start(swap[:], a.swap).then_inc(s["const_loaded"], 16)
                sp.dma_start(halves_t[:], a.halves_t).then_inc(s["const_loaded"], 16)
                sp.dma_start(qk_w[:], a.qk_norm_w[l]).then_inc(s["const_loaded"], 16)
                sp.dma_start(rope[:], a.rope.rearrange("f p n -> p f n")).then_inc(s["const_loaded"], 16)
                for t in range(N_QK):
                    sp.dma_start(q[:, t, :], a.proj[T_AQ + t]).then_inc(s[f"x_loaded{t}"], 16)
                sp.wait_ge(s["copied"], 1)
                sp.dma_start(a.g_rows.rearrange("c i t -> (c i) t"), rows[:, 0, :]).then_inc(s["stored"], 16)
                sp.wait_ge(s["copied"], 3)
                qk = a.qk_rows.rearrange("r (c p) -> (r c) p", p=P)
                sp.dma_start(qk[0:P], rows[:, 1, :]).then_inc(s["stored"], 16)
                sp.dma_start(qk[P:n_att], rows[0:n_att - P, 2, :]).then_inc(s["stored"], 16)
                sp.wait_ge(s["stored"], 48)
                sp.dma_start(inv_rms[:], a.qk_rows.rearrange("(t h) n -> h t n", h=2)).then_inc(s["rows_loaded"], 16)
                sp.wait_ge(s["v_copied"], NQ)
                sp.dma_start(a.att_v.rearrange("p c k d -> p c (k d)"), vt[:]).then_inc(s["v_stored"], 16)
                sp.wait_ge(s["v_stored"], 16)

            @block.gpsimd
            def _(pool):
                for t in range(N_QK):
                    pool.wait_ge(s["sin_done"], t + 1)
                    pool.wait_ge(s["cos_done"], t + 1)
                    nc.gpsimd.tensor_tensor(q[:, t, :], q[:, t, :], sin_part[:, t % 2, :], ALU.add).then_inc(s["rotated"], 1)

            @block.tensor
            def _(pe):
                pe.wait_ge(s["loaded"], 48)
                for n in range(NC):
                    mm = nc.tensor.transpose(ps[:, 0, n * 2 * W_BA:(n + 1) * 2 * W_BA], ba[:, n * P:(n + 1) * P],
                                             c.ident[0:2 * W_BA, 0:2 * W_BA])
                mm.then_inc(s["ba_turned"], 1)
                pe.wait_ge(s["v_loaded"], 16)
                for n in range(NQ):
                    for m in range(NQ):
                        at = (n * NQ + m) * P
                        mm = nc.tensor.transpose(ps[:, NQ + n, m * P:(m + 1) * P], v[:, at:at + P], c.ident[:])
                    mm.then_inc(s["v_turned"], 1)
                pe.wait_ge(s["dve_step"], 11)
                for d in range(N_DIR):
                    h = slice(d * DN_HEADS, (d + 1) * DN_HEADS)
                    nc.tensor.matmul(ps[:, 1 + d, 0:NC * DN_HEADS], masks[:, d, :], g[:, :, h], start=True, stop=True)
                nc.tensor.matmul(ps[:, 3, 0:NC * ITEMS], c.ones[:], g[:].rearrange("p c i -> p (c i)"),
                                 start=True, stop=True).then_inc(s["summed"], 1)
                pe.wait_ge(s["v_copied"], NQ)
                pe.wait_ge(s["g_copied"], 2)
                nc.tensor.transpose(ps[:, 4, 0:P], e[:].rearrange("p c i -> p (c i)"), c.ident[:]).then_inc(s["turned"], 1)
                pe.wait_ge(s["att_root"], 2)
                nc.tensor.transpose(ps[:, 5, 0:P], att_inv[:, 0:P], c.ident[:])
                nc.tensor.transpose(ps[0:n_att - P, 6, 0:P], att_inv[:, P:n_att], c.ident[:]).then_inc(s["turned"], 1)
                pe.wait_ge(s["copied"], 3)
                pe.wait_ge(s["const_loaded"], 64)

                def swap_quarters(t):
                    pe.wait_ge(s[f"x_loaded{t}"], 16)
                    pe.wait_ge(s["sin_done"], t)
                    for n in range(NQ):
                        mm = nc.tensor.matmul(ps[:, n, :], swap[:], q[:, t, n * QB:(n + 1) * QB], start=True, stop=True)
                    mm.then_inc(s["swapped"], 1)

                swap_quarters(0)
                for t in range(N_QK):
                    if t + 1 < N_QK:
                        swap_quarters(t + 1)
                    pe.wait_ge(s["rows_loaded"], 16)
                    pe.wait_ge(s["scaled"], t)
                    for n in range(NQ):
                        mm = nc.tensor.matmul(ps[:, NQ + n, :], halves_t[:], inv_rms[:, t, n * QB:(n + 1) * QB],
                                              start=True, stop=True)
                    mm.then_inc(s["spread"], 1)

            @block.scalar
            def _(act):
                act.wait_ge(s["loaded"], 48)
                nc.scalar.activation(rate[:], decay[:, 0, :], ACT.Exp).then_inc(s["act_step"], 1)
                act.wait_ge(s["dve_step"], 2)
                nc.scalar.activation(beta[:], x[:, :, 0:ITEMS], ACT.Exp, scale=-1.0).then_inc(s["act_step"], 1)
                act.wait_ge(s["dve_step"], 5)
                nc.scalar.activation(e[:], mag[:], ACT.Exp, scale=-1.0).then_inc(s["act_step"], 1)
                for n in range(NQ):
                    act.wait_ge(s["v_turned"], n + 1)
                    nc.scalar.copy(vt[:, n * NQ:(n + 1) * NQ, :].rearrange("p c d -> p (c d)"), ps[:, NQ + n, :]) \
                        .then_inc(s["v_copied"], 1)
                act.wait_ge(s["dve_step"], 6)
                nc.scalar.activation(ln[:], u[:], ACT.Ln).then_inc(s["act_step"], 1)
                act.wait_ge(s["g_copied"], 3)
                nc.scalar.activation(c.tok[:, :, T_NEG, :], e[:], ACT.Exp).then_inc(s["act_step"], 1)
                nc.scalar.activation(c.tok[:, :, T_CHUNK, :], mag[:], ACT.Exp).then_inc(s["act_step"], 1)
                nc.scalar.activation(end[:], pos[:], ACT.Exp).then_inc(s["act_step"], 1)
                act.wait_ge(s["dve_step"], 12)
                nc.scalar.activation(c.v_scale[:], kk[:].rearrange("p h c -> p c h"), ACT.Sqrt).then_inc(s["act_step"], 1)
                first = T_AQ - T_Q
                nc.scalar.activation(att[:].rearrange("p t h c -> p t c h"), c.sums[:, first:first + N_QK], ACT.Sqrt,
                                     bias=c.eps[:, 0:1], scale=1.0 / DH).then_inc(s["att_root"], 1)

                def store(t):
                    act.wait_ge(s["lo"], t + 1)
                    dst = a.att_q if t < N_QK - 1 else a.att_k
                    for half in range(2):
                        head = (2 * t if t < N_QK - 1 else 0) + half
                        part = slice(half * DH, (half + 1) * DH)
                        for src, at in ((hi, 0), (lo, DH)):
                            act.dma_start(dst[head, at:at + DH], src[part, t % 2, :].bitcast(F32)) \
                                .then_inc(s[f"stored{t % 2}"], 16)

                for t in range(N_QK):
                    act.wait_ge(s["scaled"], t + 1)
                    if t >= 2:
                        act.wait_ge(s[f"stored{t % 2}"], 64 * (t // 2))
                    nc.scalar.copy(hi[:, t % 2, :], q[:, t, :]).then_inc(s["hi"], 1)
                    if t:
                        store(t - 1)
                store(N_QK - 1)
                act.wait_ge(s["stored0"], 3 * 64)
                act.wait_ge(s["stored1"], 2 * 64)

            @block.vector
            def _(dve):
                step = s["dve_step"]
                dve.wait_ge(s["ba_turned"], 1)
                parts = ps[:, 0, :].rearrange("p (c w) -> p c w", w=2 * W_BA)
                nc.vector.tensor_copy(low[:], parts[:, :, W_BA:2 * W_BA]).then_inc(step, 1)
                dve.wait_ge(step, 1)
                nc.vector.tensor_tensor(x[:], parts[:, :, 0:W_BA], low[:], ALU.add).then_inc(step, 1)
                dve.wait_ge(step, 2)
                bias = decay[:, 1, :].unsqueeze(1).broadcast_to([P, NC, ITEMS])
                nc.vector.tensor_tensor(u[:], x[:, :, ITEMS:n_ba], bias, ALU.add).then_inc(step, 1)
                dve.wait_ge(step, 3)
                nc.vector.tensor_scalar(pos[:], u[:], 0.0, None, ALU.max).then_inc(step, 1)
                nc.vector.scalar_tensor_tensor(out=mag[:], in0=u[:], scalar=-1.0, in1=u[:], op0=ALU.mult,
                                               op1=ALU.max).then_inc(step, 1)
                dve.wait_ge(s["act_step"], 3)
                dve.wait_ge(step, 5)
                nc.vector.tensor_scalar(u[:], e[:], 1.0, None, ALU.add).then_inc(step, 1)
                dve.wait_ge(step, 6)
                nc.vector.scalar_tensor_tensor(out=g[:], in0=u[:], scalar=-1.0, in1=e[:], op0=ALU.add,
                                               op1=ALU.subtract).then_inc(step, 1)
                nc.vector.reciprocal(inv[:], u[:]).then_inc(step, 1)
                dve.wait_ge(step, 8)
                nc.vector.tensor_tensor(g[:], g[:], inv[:], ALU.mult).then_inc(step, 1)
                dve.wait_ge(step, 9)
                dve.wait_ge(s["act_step"], 4)
                nc.vector.tensor_tensor(ln[:], ln[:], g[:], ALU.subtract).then_inc(s["g_copied"], 1)
                dve.wait_ge(s["g_copied"], 1)
                nc.vector.scalar_tensor_tensor(out=ln[:], in0=ln[:], scalar=1.0, in1=pos[:], op0=ALU.mult,
                                               op1=ALU.add).then_inc(step, 1)
                dve.wait_ge(step, 10)
                nc.vector.scalar_tensor_tensor(out=g[:], in0=ln[:], scalar=-1.0,
                                               in1=rate[:].unsqueeze(1).broadcast_to([P, NC, ITEMS]),
                                               op0=ALU.mult, op1=ALU.mult).then_inc(step, 1)
                k0 = T_K - T_Q
                nc.vector.scalar_tensor_tensor(out=kk[:], in0=c.sums[:, k0:k0 + DN_HEADS, :, 0], scalar=EPS,
                                               in1=c.sums[:, k0:k0 + DN_HEADS, :, 1], op0=ALU.add, op1=ALU.add).then_inc(step, 1)
                dve.wait_ge(step, 12)
                nc.vector.reciprocal(rk2[:], kk[:]).then_inc(step, 1)
                nc.vector.scalar_tensor_tensor(out=c.q_eps[:], in0=c.sums[:, 0:DN_HEADS, :, 0], scalar=EPS,
                                               in1=c.sums[:, 0:DN_HEADS, :, 1], op0=ALU.add, op1=ALU.add).then_inc(step, 1)
                dve.wait_ge(step, 14)
                nc.vector.tensor_scalar(c.q_eps[:], c.q_eps[:], EPS * DN_D, None, ALU.mult).then_inc(step, 1)
                nc.vector.tensor_scalar(beta[:], beta[:], 1.0, None, ALU.add).then_inc(step, 1)
                dve.wait_ge(step, 16)
                nc.vector.reciprocal(inv[:], beta[:]).then_inc(step, 1)
                dve.wait_ge(step, 17)
                for d in range(N_DIR):
                    h = slice(d * DN_HEADS, (d + 1) * DN_HEADS)
                    nc.vector.tensor_tensor(c.tok[:, :, T_BETA, h], inv[:, :, h], rk2[:].rearrange("p h c -> p c h"),
                                            ALU.mult).then_inc(step, 1)
                dve.wait_ge(s["summed"], 1)
                for d in range(N_DIR):
                    h = slice(d * DN_HEADS, (d + 1) * DN_HEADS)
                    cum = ps[:, 1 + d, 0:NC * DN_HEADS].rearrange("p (c h) -> p c h", h=DN_HEADS)
                    nc.vector.tensor_copy(e[:, :, h], cum).then_inc(step, 1)
                nc.vector.tensor_copy(mag[:], ps[:, 3, 0:NC * ITEMS].rearrange("p (c i) -> p c i", i=ITEMS)).then_inc(step, 1)
                dve.wait_ge(step, 22)
                nc.vector.tensor_copy(c.tok[:, :, T_G, :], e[:]).then_inc(s["g_copied"], 1)
                nc.vector.tensor_tensor(pos[:], mag[:], e[:], ALU.subtract).then_inc(s["g_copied"], 1)
                dve.wait_ge(s["act_step"], 7)
                nc.vector.tensor_scalar(c.tok[:, :, T_NEG, :], c.tok[:, :, T_NEG, :], -1.0, None, ALU.mult).then_inc(step, 1)
                nc.vector.tensor_tensor(c.tok[:, :, T_BETA_END, :], c.tok[:, :, T_BETA, :], end[:], ALU.mult).then_inc(step, 1)
                dve.wait_ge(s["turned"], 1)
                nc.vector.tensor_copy(rows[:, 0, :], ps[:, 4, 0:P]).then_inc(s["copied"], 1)
                dve.wait_ge(s["att_root"], 1)
                nc.vector.reciprocal(att_inv[:], att[:].rearrange("p t h c -> p (t h c)")).then_inc(s["att_root"], 1)
                dve.wait_ge(s["turned"], 2)
                nc.vector.tensor_copy(rows[:, 1, :], ps[:, 5, 0:P]).then_inc(s["copied"], 1)
                nc.vector.tensor_copy(rows[0:n_att - P, 2, :], ps[0:n_att - P, 6, 0:P]).then_inc(s["copied"], 1)

                def split(t):
                    dve.wait_ge(s["hi"], t + 1)
                    nc.vector.tensor_tensor(lo[:, t % 2, :], q[:, t, :], hi[:, t % 2, :].bitcast(F32),
                                            ALU.subtract).then_inc(s["lo"], 1)

                dve.wait_ge(s["const_loaded"], 64)

                def products(t):
                    col = 0 if t < N_QK - 1 else 2
                    dve.wait_ge(s["swapped"], t + 1)
                    nc.vector.scalar_tensor_tensor(out=sin_part[:, t % 2, :], in0=flat(0), scalar=qk_w[:, col + 1:col + 2],
                                                   in1=rope[:, 1, :], op0=ALU.mult, op1=ALU.mult).then_inc(s["sin_done"], 1)
                    dve.wait_ge(s[f"x_loaded{t}"], 16)
                    nc.vector.scalar_tensor_tensor(out=q[:, t, :], in0=q[:, t, :], scalar=qk_w[:, col:col + 1],
                                                   in1=rope[:, 0, :], op0=ALU.mult, op1=ALU.mult).then_inc(s["cos_done"], 1)

                products(0)
                for t in range(N_QK):
                    if t + 1 < N_QK:
                        products(t + 1)
                    if t:
                        split(t - 1)
                    dve.wait_ge(s["rotated"], t + 1)
                    dve.wait_ge(s["spread"], t + 1)
                    nc.vector.tensor_tensor(q[:, t, :], q[:, t, :], flat(NQ), ALU.mult).then_inc(s["scaled"], 1)
                split(N_QK - 1)




SIDES = range(N_DIR)
HEADS = range(DN_HEADS)


def chunk_of(side, i):
    return i if side == 0 else i * -1 + (NC - 1)


def delta_net(nc, a, c, l):
    per_side = ("k1_loaded k2_loaded qv_loaded scalars1 scalars2 dd dt eg u y0 y0_part t0 x0 masked p_done p_copied "
                "xp_done x_updated xt_done y_copied yf kq_done att kt_done kk vt_done vv qg "
                "ks_done r tr_done vn vd out_done o_added ds_done state vs gram dtm ")
    names = " ".join(f"{n}{side}" for n in per_side.split() for side in SIDES) + " masks_loaded zeroed o_stored passed"
    with ExitStack() as stack, semaphores(nc, names) as s:
        b = Buffers(nc, stack, "dn")
        pair = lambda name: b.sbuf(name, [P, N_DIR, DN_HEADS, P])
        masks = b.sbuf("masks", [P, N_DIR, LEVELS + 1, P])
        k1, row, k2, q, v = (pair(n) for n in ("k1", "row", "k2", "q", "v"))
        dd, eg, dt, u, y_part = (pair(n) for n in ("dd", "eg", "dt", "u", "y_part"))
        x, y, p, yf = (pair(n) for n in ("x", "y", "p", "yf"))
        att, qg, kk, vv = (pair(n) for n in ("att", "qg", "kk", "vv"))
        r, vn, vd, state = (pair(n) for n in ("r", "vn", "vd", "state"))
        um = b.sbuf("um", [P, N_DIR, 2, DN_HEADS, P])
        sc1 = b.sbuf("sc1", [P, N_DIR, TABLES, DN_HEADS])
        sc2 = b.sbuf("sc2", [P, N_DIR, TABLES, DN_HEADS])
        vs = b.sbuf("vs", [P, N_DIR, DN_HEADS])
        o = b.sbuf("out", [P, DN_HEADS, SEQ])
        ps = b.banks()
        bank = lambda n: ps[:, n, :].rearrange("p (h t) -> p h t", h=DN_HEADS)
        inner, outer = (lambda side, n: bank(2 * side + n)), (lambda side, n: bank(4 + 2 * side + n))
        mask = lambda side, lv: masks[:, side, lv, :].unsqueeze(1).broadcast_to([P, DN_HEADS, P])
        ident = c.ident[:].unsqueeze(1).broadcast_to([P, DN_HEADS, P])
        per_head = lambda t: t.unsqueeze(2).broadcast_to([P, DN_HEADS, P])

        with nc.Block() as block:

            @block.sync
            def _(sp):
                def channels(first, side, i):
                    at = chunk_of(side, i) * P
                    return a.proj[first:first + DN_HEADS, :, bass.ds(at, P)].rearrange("h p t -> p h t")

                def load_k1(side, i):
                    sp.dma_start(k1[:, side], channels(T_K, side, i)).then_inc(s[f"k1_loaded{side}"], 16)
                    rows = a.g_rows[chunk_of(side, i), side * DN_HEADS:(side + 1) * DN_HEADS]
                    sp.dma_start(row[:, side], rows.partition_broadcast(P)).then_inc(s[f"k1_loaded{side}"], 16)

                def load_k2(side, i):
                    sp.dma_start(k2[:, side], channels(T_K, side, i)).then_inc(s[f"k2_loaded{side}"], 16)

                def load_qv(side, i):
                    sp.dma_start(q[:, side], channels(T_Q, side, i)).then_inc(s[f"qv_loaded{side}"], 16)
                    sp.dma_start(v[:, side], channels(T_V, side, i)).then_inc(s[f"qv_loaded{side}"], 16)

                for side in SIDES:
                    load_k1(side, 0)
                sp.dma_start(masks[:], a.masks).then_inc(s["masks_loaded"], 16)
                for load in (load_k2, load_qv):
                    for side in SIDES:
                        load(side, 0)
                with sp.Fori(1, NC) as i:
                    for side in SIDES:
                        wait_in_loop(sp, s, f"gram{side}", i)
                        wait_in_loop(sp, s, f"dd{side}", i)
                        wait_in_loop(sp, s, f"eg{side}", i)
                        load_k1(side, i)
                    for side in SIDES:
                        wait_in_loop(sp, s, f"ks_done{side}", i)
                        load_k2(side, i)
                    for side in SIDES:
                        wait_in_loop(sp, s, f"vt_done{side}", i)
                        wait_in_loop(sp, s, f"qg{side}", i)
                        load_qv(side, i)
                out = a.dn_o.rearrange("h p t -> p h t")
                for side in SIDES:
                    sp.wait_ge(s[f"o_added{side}"], NC - 1)
                sp.dma_start(out[:, :, P:SEQ - P], o[:, :, P:SEQ - P]).then_inc(s["o_stored"], 16)
                for side in SIDES:
                    sp.wait_ge(s[f"o_added{side}"], NC)
                for at in (0, SEQ - P):
                    sp.dma_start(out[:, :, at:at + P], o[:, :, at:at + P]).then_inc(s["o_stored"], 16)
                sp.wait_ge(s["o_stored"], 48)

            @block.tensor
            def _(pe):
                def each(out, left, right):
                    for h in HEADS:
                        mm = nc.tensor.matmul(out[:, h, :], left[:, h, :], right[:, h, :], start=True, stop=True)
                    return mm

                def turn(out, src):
                    for h in HEADS:
                        mm = nc.tensor.transpose(out[:, h, :], src[:, h, :], c.ident[:])
                    return mm

                def gram(side, i):
                    pe.wait_ge(s[f"k1_loaded{side}"], 32 * i + 32)
                    pe.wait_ge(s[f"p_copied{side}"], 6 * i)
                    each(inner(side, 0), k1[:, side], k1[:, side]).then_inc(s[f"gram{side}"], 1)

                def turn_first(side, i):
                    pe.wait_ge(s[f"y0{side}"], i + 1)
                    turn(inner(side, 1), y[:, side]).then_inc(s[f"t0{side}"], 1)

                def product(side, i, lv):
                    pe.wait_ge(s[f"masked{side}"], 6 * i + lv)
                    if lv == 1:
                        pe.wait_ge(s[f"x0{side}"], i + 1)
                    else:
                        pe.wait_ge(s[f"x_updated{side}"], 5 * i + lv - 1)
                        pe.wait_ge(s[f"y_copied{side}"], 5 * i + lv - 1)
                    each(inner(side, 0), um[:, side, lv % 2], x[:, side]).then_inc(s[f"p_done{side}"], 1)

                def step(side, i, lv):
                    pe.wait_ge(s[f"p_copied{side}"], 6 * i + lv)
                    if lv < LEVELS - 1:
                        each(inner(side, 1), y[:, side], p[:, side]).then_inc(s[f"xp_done{side}"], 1)
                    else:
                        each(inner(side, 1), p[:, side], y[:, side]).then_inc(s[f"xp_done{side}"], 1)

                def turn_x(side, i, lv):
                    pe.wait_ge(s[f"x_updated{side}"], 5 * i + lv)
                    turn(inner(side, 0), x[:, side]).then_inc(s[f"xt_done{side}"], 1)

                def key_query(side, i):
                    pe.wait_ge(s[f"k2_loaded{side}"], 16 * i + 16)
                    pe.wait_ge(s[f"qv_loaded{side}"], 32 * i + 32)
                    pe.wait_ge(s[f"o_added{side}"], i)
                    each(outer(side, 0), k2[:, side], q[:, side]).then_inc(s[f"kq_done{side}"], 1)

                def turn_k(side, i):
                    pe.wait_ge(s[f"state{side}"], i + 1)
                    turn(outer(side, 1), k2[:, side]).then_inc(s[f"kt_done{side}"], 1)

                def turn_v(side, i):
                    pe.wait_ge(s[f"att{side}"], i + 1)
                    turn(outer(side, 0), v[:, side]).then_inc(s[f"vt_done{side}"], 1)

                def scan_ks(side, j):
                    pe.wait_ge(s[f"state{side}"], j + 1)
                    pe.wait_ge(s[f"vv{side}"], j + 1)
                    each(outer(side, 0), k2[:, side], state[:, side]).then_inc(s[f"ks_done{side}"], 1)

                def scan_solve(side, j):
                    pe.wait_ge(s[f"r{side}"], j + 1)
                    pe.wait_ge(s[f"yf{side}"], j + 1)
                    pe.wait_ge(s[f"kk{side}"], j + 1)
                    each(outer(side, 1), yf[:, side], r[:, side]).then_inc(s[f"tr_done{side}"], 1)

                def scan_out(side, j):
                    pe.wait_ge(s[f"qg{side}"], j + 1)
                    pe.wait_ge(s[f"vn{side}"], j + 1)
                    for h in HEADS:
                        nc.tensor.matmul(outer(side, 0)[:, h, :], state[:, side, h, :], qg[:, side, h, :],
                                         start=True, stop=False)
                        mm = nc.tensor.matmul(outer(side, 0)[:, h, :], vn[:, side, h, :], att[:, side, h, :],
                                              start=False, stop=True)
                    mm.then_inc(s[f"out_done{side}"], 1)

                def scan_state(side, j):
                    pe.wait_ge(s[f"vd{side}"], j + 1)
                    each(outer(side, 1), kk[:, side], vd[:, side]).then_inc(s[f"ds_done{side}"], 1)

                def iteration(i, j, following):
                    local, scan = i is not None, j is not None
                    for side in SIDES:
                        if scan:
                            scan_ks(side, j)
                    for side in SIDES:
                        if local:
                            turn_first(side, i)
                        if scan:
                            scan_solve(side, j)
                    for lv in range(1, LEVELS):
                        for side in SIDES:
                            if local:
                                product(side, i, lv)
                        if scan and lv <= 2:
                            scan_out(lv - 1, j)
                        if local and lv >= 3 and lv <= 5:
                            (key_query, turn_k, turn_v)[lv - 3](0, i)
                        for side in SIDES:
                            if following and lv == LEVELS - 1:
                                gram(side, i + 1)
                            if local:
                                step(side, i, lv)
                        if scan and lv <= 2:
                            scan_state(lv - 1, j)
                        if local and lv >= 3 and lv <= 5:
                            (key_query, turn_k, turn_v)[lv - 3](1, i)
                        for side in SIDES:
                            if local and lv < LEVELS - 1:
                                turn_x(side, i, lv)

                for side in SIDES:
                    gram(side, 0)
                iteration(0, None, True)
                with pe.Fori(1, NC - 1) as i:
                    iteration(i, i - 1, True)
                iteration(NC - 1, NC - 2, False)
                iteration(None, NC - 1, False)

            @block.scalar
            def _(act):
                def evacuate(done, count, dst, src, name, side):
                    act.wait_ge(s[f"{done}{side}"], count)
                    nc.scalar.copy(dst, src).then_inc(s[f"{name}{side}"], 1)

                def token_decays(i):
                    for side in SIDES:
                        act.wait_ge(s[f"dd{side}"], i + 1)
                        act.wait_ge(s[f"att{side}"], i)
                        nc.scalar.activation(dt[:, side], dd[:, side], ACT.Exp).then_inc(s[f"dt{side}"], 1)

                def chunk_decays(i):
                    for side in SIDES:
                        act.wait_ge(s[f"k1_loaded{side}"], 32 * i + 32)
                        act.wait_ge(s[f"qg{side}"], i)
                        nc.scalar.activation(eg[:, side], row[:, side], ACT.Exp).then_inc(s[f"eg{side}"], 1)

                def local(i, following):
                    for side in SIDES:
                        evacuate("t0", i + 1, x[:, side], inner(side, 1), "x0", side)
                    for lv in range(1, LEVELS):
                        for side in SIDES:
                            evacuate("p_done", 6 * i + lv, p[:, side], inner(side, 0), "p_copied", side)
                        if lv == 4:
                            for side in SIDES:
                                if side == 1:
                                    evacuate("xt_done", 5 * i + lv, y[:, 0], inner(0, 0), "y_copied", 0)
                                evacuate("kt_done", i + 1, kk[:, side], outer(side, 1), "kk", side)
                            evacuate("xt_done", 5 * i + lv, y[:, 1], inner(1, 0), "y_copied", 1)
                            if following:
                                token_decays(i + 1)
                        elif lv < LEVELS - 1:
                            for side in SIDES:
                                evacuate("xt_done", 5 * i + lv, y[:, side], inner(side, 0), "y_copied", side)
                    if following:
                        chunk_decays(i + 1)

                token_decays(0)
                chunk_decays(0)
                with act.Fori(0, NC - 1) as i:
                    local(i, True)
                local(NC - 1, False)

            @block.gpsimd
            def _(pool):
                for side in SIDES:
                    nc.gpsimd.memset(state[:, side], 0.0).then_inc(s[f"state{side}"], 1)
                nc.gpsimd.memset(o[:], 0.0).then_inc(s["zeroed"], 1)
                pool.wait_ge(s["masks_loaded"], 16)

                def scalars(side, i):
                    heads = slice(side * DN_HEADS, (side + 1) * DN_HEADS)
                    pool.wait_ge(s[f"u{side}"], i)
                    nc.gpsimd.tensor_copy(sc1[:, side], c.tok[:, bass.ds(chunk_of(side, i), 1), :, heads].squeeze(1)) \
                        .then_inc(s[f"scalars1{side}"], 1)

                def v_scalars(side, i):
                    pool.wait_ge(s[f"vv{side}"], i)
                    nc.gpsimd.tensor_copy(vs[:, side], c.v_scale[:, bass.ds(chunk_of(side, i), 1), :].squeeze(1)) \
                        .then_inc(s[f"vs{side}"], 1)

                def scan_scalars(side, i):
                    heads = slice(side * DN_HEADS, (side + 1) * DN_HEADS)
                    pool.wait_ge(s[f"state{side}"], i + 1)
                    nc.gpsimd.tensor_copy(sc2[:, side], c.tok[:, bass.ds(chunk_of(side, i), 1), :, heads].squeeze(1)) \
                        .then_inc(s[f"scalars2{side}"], 1)

                for side in SIDES:
                    scalars(side, 0)
                def local(i, following):
                    for side in SIDES:
                        v_scalars(side, i)
                    for lv in range(1, LEVELS):
                        for side in SIDES:
                            pool.wait_ge(s[f"u{side}"], i + 1)
                            if lv <= 2:
                                pool.wait_ge(s[f"xp_done{side}"], 6 * i)
                            else:
                                pool.wait_ge(s[f"p_done{side}"], 6 * i + lv - 2)
                            nc.gpsimd.tensor_tensor(um[:, side, lv % 2], u[:, side], mask(side, lv), ALU.mult) \
                                .then_inc(s[f"masked{side}"], 1)
                        if lv == 2 and following:
                            for side in SIDES:
                                scalars(side, i + 1)
                        if lv == 3:
                            for side in SIDES:
                                scan_scalars(side, i)
                        if lv == 4:
                            for side in SIDES:
                                pool.wait_ge(s[f"qv_loaded{side}"], 32 * i + 32)
                                pool.wait_ge(s[f"eg{side}"], i + 1)
                                pool.wait_ge(s[f"o_added{side}"], i)
                                nc.gpsimd.tensor_tensor(qg[:, side], q[:, side], eg[:, side], ALU.mult) \
                                    .then_inc(s[f"qg{side}"], 1)

                with pool.Fori(0, NC - 1) as i:
                    local(i, True)
                local(NC - 1, False)

            @block.vector
            def _(dve):
                def decays(side, i):
                    dve.wait_ge(s[f"k1_loaded{side}"], 32 * i + 32)
                    dve.wait_ge(s[f"scalars1{side}"], i + 1)
                    dve.wait_ge(s[f"dt{side}"], i)
                    for h in HEADS:
                        op = nc.vector.tensor_scalar(dd[:, side, h, :], row[:, side, h, :], sc1[:, side, T_G, h:h + 1],
                                                     0.0, ALU.subtract, ALU.min)
                    op.then_inc(s[f"dd{side}"], 1)

                def mask_decays(side, i):
                    dve.wait_ge(s[f"dt{side}"], i + 1)
                    nc.vector.tensor_tensor(dt[:, side], dt[:, side], mask(side, LEVELS), ALU.mult).then_inc(s[f"dtm{side}"], 1)

                def system(side, i):
                    dve.wait_ge(s[f"dtm{side}"], i + 1)
                    dve.wait_ge(s[f"gram{side}"], i + 1)
                    dve.wait_ge(s[f"masked{side}"], 6 * i)
                    for h in HEADS:
                        op = nc.vector.scalar_tensor_tensor(out=u[:, side, h, :], in0=inner(side, 0)[:, h, :],
                                                            scalar=sc1[:, side, T_BETA, h:h + 1], in1=dt[:, side, h, :],
                                                            op0=ALU.mult, op1=ALU.mult)
                    op.then_inc(s[f"u{side}"], 1)
                    dve.wait_ge(s[f"u{side}"], i + 1)
                    nc.vector.tensor_tensor(y_part[:, side], u[:, side], mask(side, 0), ALU.mult).then_inc(s[f"y0_part{side}"], 1)

                def first_inverse(side, i):
                    dve.wait_ge(s[f"y0_part{side}"], i + 1)
                    dve.wait_ge(s[f"yf{side}"], i)
                    nc.vector.tensor_tensor(y[:, side], y_part[:, side], ident, ALU.add).then_inc(s[f"y0{side}"], 1)

                def update(side, i, lv):
                    dve.wait_ge(s[f"xp_done{side}"], 6 * i + lv)
                    if lv < LEVELS - 1:
                        if lv > 1:
                            dve.wait_ge(s[f"x_updated{side}"], 5 * i + lv - 1)
                        nc.vector.tensor_tensor(x[:, side], x[:, side], inner(side, 1), ALU.subtract) \
                            .then_inc(s[f"x_updated{side}"], 1)
                    else:
                        nc.vector.tensor_tensor(yf[:, side], y[:, side], inner(side, 1), ALU.subtract) \
                            .then_inc(s[f"yf{side}"], 1)

                def attend(side, i):
                    dve.wait_ge(s[f"kq_done{side}"], i + 1)
                    nc.vector.tensor_tensor(att[:, side], outer(side, 0), dt[:, side], ALU.mult).then_inc(s[f"att{side}"], 1)

                def values(side, i):
                    dve.wait_ge(s[f"vt_done{side}"], i + 1)
                    dve.wait_ge(s[f"vs{side}"], i + 1)
                    dve.wait_ge(s[f"r{side}"], i)
                    nc.vector.tensor_tensor(vv[:, side], outer(side, 0), per_head(vs[:, side]), ALU.mult) \
                        .then_inc(s[f"vv{side}"], 1)

                def remainder(side, j):
                    dve.wait_ge(s[f"ks_done{side}"], j + 1)
                    dve.wait_ge(s[f"vv{side}"], j + 1)
                    dve.wait_ge(s[f"scalars2{side}"], j + 1)
                    for h in HEADS:
                        op = nc.vector.scalar_tensor_tensor(out=r[:, side, h, :], in0=outer(side, 0)[:, h, :],
                                                            scalar=sc2[:, side, T_NEG, h:h + 1], in1=vv[:, side, h, :],
                                                            op0=ALU.mult, op1=ALU.add)
                    op.then_inc(s[f"r{side}"], 1)

                def new_values(side, j):
                    dve.wait_ge(s[f"tr_done{side}"], j + 1)
                    nc.vector.tensor_tensor(vn[:, side], outer(side, 1), per_head(sc2[:, side, T_BETA, :]), ALU.mult) \
                        .then_inc(s[f"vn{side}"], 1)
                    nc.vector.tensor_tensor(vd[:, side], outer(side, 1), per_head(sc2[:, side, T_BETA_END, :]), ALU.mult) \
                        .then_inc(s[f"vd{side}"], 1)

                def output(side, j):
                    at = chunk_of(side, j) * P
                    dve.wait_ge(s[f"o_added{1 - side}"], j)
                    dve.wait_ge(s[f"out_done{side}"], j + 1)
                    there = o[:, :, bass.ds(at, P)]
                    nc.vector.tensor_tensor(there, outer(side, 0), there, ALU.add).then_inc(s[f"o_added{side}"], 1)

                def new_state(side, j):
                    dve.wait_ge(s[f"ds_done{side}"], j + 1)
                    dve.wait_ge(s[f"state{side}"], j + 1)
                    for h in HEADS:
                        op = nc.vector.scalar_tensor_tensor(out=state[:, side, h, :], in0=state[:, side, h, :],
                                                            scalar=sc2[:, side, T_CHUNK, h:h + 1],
                                                            in1=outer(side, 1)[:, h, :], op0=ALU.mult, op1=ALU.add)
                    op.then_inc(s[f"state{side}"], 1)

                def iteration(i, j, following):
                    local, scan = i is not None, j is not None
                    for side in SIDES:
                        if local:
                            first_inverse(side, i)
                        if scan:
                            remainder(side, j)
                    for side in SIDES:
                        if scan:
                            new_values(side, j)
                    for lv in range(1, LEVELS):
                        if scan and lv <= 2:
                            output(lv - 1, j)
                        if local and lv == 3:
                            attend(0, i)
                        if local and lv == 5:
                            values(0, i)
                        if following and lv == 5:
                            for side in SIDES:
                                mask_decays(side, i + 1)
                        for side in SIDES:
                            if following and lv == 6:
                                system(side, i + 1)
                            if local:
                                update(side, i, lv)
                        if scan and lv <= 2:
                            new_state(lv - 1, j)
                        if local and lv == 3:
                            attend(1, i)
                        if local and lv == 5:
                            values(1, i)
                        if following and lv == 3:
                            for side in SIDES:
                                decays(side, i + 1)

                dve.wait_ge(s["masks_loaded"], 16)
                dve.wait_ge(s["zeroed"], 1)
                for side in SIDES:
                    decays(side, 0)
                for side in SIDES:
                    mask_decays(side, 0)
                    system(side, 0)
                iteration(0, None, True)
                with dve.Fori(1, NC - 1) as i:
                    iteration(i, i - 1, True)
                iteration(NC - 1, NC - 2, False)
                iteration(None, NC - 1, False)


N_UNITS = NC
MAX_PLAN = [3, 3, 3, 3, 2, 2, 0, 0]
PAIRS = NC // 2
MAX_DONE = 5
LAG = 2
SLOTS = 4
K_ROWS = DH + NQ


def attention(nc, a, c, l):
    names = ("max_part turned negated unit_done unit_read v_loaded const_loaded ones_set v_split "
             "scores_done exp_done hi_done lo_done pv_done o_copied o_stored0 o_stored1 k_loaded0 k_loaded1 "
             "k_first0 k_first1 passed "
             + " ".join(f"q_loaded{u} q2_loaded{u}" for u in range(SLOTS)))
    NB = ATT_HEADS * NQ
    ROUNDS = NB // SLOTS
    with ExitStack() as stack, semaphores(nc, names) as s:
        b = Buffers(nc, stack, "att")
        k1 = b.sbuf("k1", [P, KV_HEADS, SEQ], F32R)
        k2 = b.sbuf("k2", [K_ROWS, KV_HEADS, SEQ], F32R)
        v = b.sbuf("v", [P, KV_HEADS, NC, DH + 1])
        v_hi = b.sbuf("v_hi", [P, KV_HEADS, NC, DH + 1], F32R)
        v_lo = b.sbuf("v_lo", [P, KV_HEADS, NC, DH + 1], F32R)
        quarter = b.sbuf("quarter", [NQ, NQ, P])
        q1 = b.sbuf("q1", [P, SLOTS, QB], F32R)
        q2 = b.sbuf("q2", [K_ROWS, SLOTS, QB], F32R)
        probs = b.sbuf("probs", [P, 2, 2, QB])
        p_hi = b.sbuf("p_hi", [P, SLOTS, 2, QB], F32R)
        p_lo = b.sbuf("p_lo", [P, SLOTS, 2, QB], F32R)
        part = b.sbuf("part", [P, NQ, NQ])
        top = b.sbuf("top", [P, NQ])
        o = b.sbuf("o", [DH + 1, 2, QB])
        ps = b.banks()
        with nc.Block() as block:

            @block.sync
            def _(sp):
                def load_q(j, slot):
                    head = (slot % 2) * GROUP + j // 2
                    at = (j % 2 * 2 + slot // 2) * QB
                    sp.dma_start(q2[0:DH, slot, :].bitcast(F32), a.att_q[head, 0:DH, bass.ds(at, QB)]) \
                        .then_inc(s[f"q2_loaded{slot}"], 16)
                    sp.dma_start(q1[:, slot, :].bitcast(F32), a.att_q[head, :, bass.ds(at, QB)]) \
                        .then_inc(s[f"q_loaded{slot}"], 16)

                def store(j, slot):
                    head = (slot % 2) * GROUP + j // 2
                    at = (j % 2 * 2 + slot // 2) * QB
                    sp.dma_start(a.att_o[head, :, bass.ds(at, QB)], o[:, slot % 2, :]).then_inc(s[f"o_stored{slot % 2}"], 16)

                for kv in range(KV_HEADS):
                    sp.dma_start(k1[0:DH, kv, :].bitcast(F32), a.att_k[kv, 0:DH]).then_inc(s[f"k_first{kv}"], 16)
                    load_q(0, kv)
                    if kv == 0:
                        sp.dma_start(quarter[:], a.quarter).then_inc(s["const_loaded"], 16)
                    sp.dma_start(k1[DH:P, kv, :].bitcast(F32), a.att_k[kv, 0:DH]).then_inc(s[f"k_loaded{kv}"], 16)
                    sp.dma_start(k2[0:DH, kv, :].bitcast(F32), a.att_k[kv, DH:P]).then_inc(s[f"k_loaded{kv}"], 16)
                for kv in range(KV_HEADS):
                    sp.dma_start(v[:, kv, :, 0:DH], a.att_v[:, :, kv, :]).then_inc(s["v_loaded"], 16)
                for slot in range(2, SLOTS):
                    load_q(0, slot)
                with sp.Fori(0, ROUNDS - 1) as j:
                    for slot in range(SLOTS):
                        wait_in_loop(sp, s, "scores_done", (j * SLOTS + slot + 1) * PAIRS)
                        load_q(j + 1, slot)
                        wait_in_loop(sp, s, "o_copied", j * SLOTS + slot + 1)
                        store(j, slot)
                for slot in range(SLOTS):
                    sp.wait_ge(s["o_copied"], NB - SLOTS + slot + 1)
                    store(ROUNDS - 1, slot)
                for kv in range(2):
                    sp.wait_ge(s[f"o_stored{kv}"], 16 * (NB // 2))

            @block.gpsimd
            def _(pool):
                nc.gpsimd.memset(v[:, :, :, DH:DH + 1], 1.0).then_inc(s["ones_set"], 1)

            @block.tensor
            def _(pe):
                def max_unit(j, slot, u):
                    tile, keys = u // NQ, u % NQ
                    n = j * SLOTS + slot
                    if u == 0:
                        pe.wait_ge(s[f"q2_loaded{slot}"], 16 * j + 16)
                    pe.wait_ge(s["unit_read"], n * N_UNITS + u + 1)
                    nc.tensor.matmul(ps[:, 4 + u % 2, :], q2[0:DH, slot, tile * P:(tile + 1) * P],
                                     k1[0:DH, slot % 2, keys * QB:(keys + 1) * QB], start=True, stop=True) \
                        .then_inc(s["unit_done"], 1)

                def turn_max(j, slot):
                    pe.wait_ge(s["max_part"], j * SLOTS + slot + 1)
                    nc.tensor.transpose(ps[0:NQ, 7, 0:P], top[:], c.ident[:]).then_inc(s["turned"], 1)

                def scores(j, slot, pair):
                    pe.wait_ge(s["exp_done"], (j * SLOTS + slot) * PAIRS + pair + 1)
                    if pair == 0:
                        pe.wait_ge(s[f"q_loaded{slot}"], 16 * j + 16)
                        pe.wait_ge(s["negated"], j * SLOTS + slot + 1)
                    for m in range(2):
                        keys = slice((2 * pair + m) * P, (2 * pair + m + 1) * P)
                        out = ps[:, 2 * (pair % 2) + m, :]
                        nc.tensor.matmul(out, k1[:, slot % 2, keys], q1[:, slot, :], start=True, stop=False)
                        mm = nc.tensor.matmul(out, k2[:, slot % 2, keys], q2[:, slot, :], start=False, stop=True)
                    mm.then_inc(s["scores_done"], 1)

                def values(j, slot, pair):
                    n = j * SLOTS + slot
                    pe.wait_ge(s["lo_done"], n * PAIRS + pair + 1 + 2)
                    if pair == 0:
                        pe.wait_ge(s["o_copied"], n)
                    kv, at = slot % 2, pair % SLOTS
                    for m in range(2):
                        tile = 2 * pair + m
                        for part_v, part_p in ((v_hi, p_hi), (v_hi, p_lo), (v_lo, p_hi)):
                            first = tile == 0 and part_v is v_hi and part_p is p_hi
                            mm = nc.tensor.matmul(ps[0:DH + 1, 6, :], part_v[:, kv, tile, :], part_p[:, at, m, :],
                                                  start=first, stop=(tile == NC - 1 and part_v is v_lo))
                    mm.then_inc(s["pv_done"], 1)

                def one_block(j, slot, before, after):
                    u = 0
                    for pair in range(PAIRS):
                        units = MAX_PLAN[pair] if after else 0
                        scores(j, slot, pair)
                        for _ in range((units + 1) // 2):
                            max_unit(*after, u)
                            u += 1
                        if pair >= LAG:
                            values(j, slot, pair - LAG)
                        elif before:
                            values(*before, PAIRS + pair - LAG)
                        if pair == MAX_DONE + 1 and after:
                            turn_max(*after)
                        for _ in range(units // 2):
                            max_unit(*after, u)
                            u += 1

                pe.sem_inc(s["exp_done"], 2)
                pe.wait_ge(s["k_first0"], 16)
                for u in range(N_UNITS):
                    max_unit(0, 0, u)
                turn_max(0, 0)
                pe.wait_ge(s["ones_set"], 2)
                for kv in range(KV_HEADS):
                    pe.wait_ge(s[f"k_first{kv}"], 16)
                    pe.wait_ge(s[f"k_loaded{kv}"], 32)
                pe.wait_ge(s["v_split"], 2)
                one_block(0, 0, None, (0, 1))
                for slot in range(1, SLOTS):
                    one_block(0, slot, (0, slot - 1), (slot // (SLOTS - 1), (slot + 1) % SLOTS))
                with pe.Fori(1, ROUNDS - 1) as j:
                    one_block(j, 0, (j - 1, SLOTS - 1), (j, 1))
                    for slot in range(1, SLOTS):
                        one_block(j, slot, (j, slot - 1), (j + slot // (SLOTS - 1), (slot + 1) % SLOTS))
                j = ROUNDS - 1
                one_block(j, 0, (j - 1, SLOTS - 1), (j, 1))
                for slot in range(1, SLOTS):
                    one_block(j, slot, (j, slot - 1), (j, slot + 1) if slot < SLOTS - 1 else None)
                for pair in range(PAIRS - LAG, PAIRS):
                    values(j, SLOTS - 1, pair)

            @block.scalar
            def _(act):
                with act.Fori(0, ROUNDS) as j:
                    for g in range(SLOTS * PAIRS):
                        n, pair = j * SLOTS + g // PAIRS, g % PAIRS
                        act.wait_ge(s["scores_done"], n * PAIRS + pair + 1)
                        act.wait_ge(s["lo_done"], n * PAIRS + pair + 1)
                        nc.scalar.activation(probs[:, pair % 2], ps[:, 2 * (pair % 2):2 * (pair % 2) + 2, :], ACT.Exp,
                                             scale=SCALE).then_inc(s["exp_done"], 1)
                        act.wait_ge(s["exp_done"], n * PAIRS + pair + 1 + 2)
                        act.wait_ge(s["pv_done"], n * PAIRS + pair + 1)
                        nc.scalar.activation(p_hi[:, pair % SLOTS], probs[:, pair % 2], ACT.Copy).then_inc(s["hi_done"], 1)

            @block.vector
            def _(dve):
                def read_units(n, units, u):
                    for w in range(u, u + units):
                        dve.wait_ge(s["unit_done"], n * N_UNITS + w + 1)
                        nc.vector.tensor_reduce(part[:, w // NQ, w % NQ:w % NQ + 1], ps[:, 4 + w % 2, :], AX.X, ALU.max) \
                            .then_inc(s["unit_read"], 1)

                def all_maxima(n):
                    dve.wait_ge(s["unit_read"], n * N_UNITS + N_UNITS + 2)
                    dve.wait_ge(s["turned"], n)
                    nc.vector.tensor_reduce(top[:], part[:], AX.X, ALU.max).then_inc(s["max_part"], 1)

                def minus_max(slot, n):
                    dve.wait_ge(s["turned"], n + 1)
                    turned = ps[0:NQ, 7, 0:P].unsqueeze(1).broadcast_to([NQ, NQ, P])
                    nc.vector.tensor_tensor(q2[DH:K_ROWS, slot, :].rearrange("r (t q) -> r t q", q=P), turned, quarter[:],
                                            ALU.mult).then_inc(s["negated"], 1)

                def low_part(n, pair):
                    dve.wait_ge(s["hi_done"], n * PAIRS + pair + 1)
                    dve.wait_ge(s["pv_done"], n * PAIRS + pair + 1)
                    nc.vector.tensor_tensor(p_lo[:, pair % SLOTS], probs[:, pair % 2], p_hi[:, pair % SLOTS].bitcast(F32),
                                            ALU.subtract).then_inc(s["lo_done"], 1)

                def output(n, kv, before):
                    dve.wait_ge(s["pv_done"], n * PAIRS + PAIRS + SLOTS)
                    dve.wait_ge(s[f"o_stored{kv}"], before)
                    nc.vector.tensor_copy(o[:, kv, :], ps[0:DH + 1, 6, :]).then_inc(s["o_copied"], 1)

                def one_block(n, slot, stored, after):
                    u = 0
                    for pair in range(PAIRS):
                        units = MAX_PLAN[pair] if after else 0
                        read_units(n + 1, (units + 1) // 2, u)
                        if pair > 0:
                            low_part(n, pair - 1)
                        elif stored is not None:
                            low_part(n - 1, PAIRS - 1)
                        read_units(n + 1, units // 2, u + (units + 1) // 2)
                        u += units
                        if pair == LAG - 1 and stored is not None:
                            output(n - 1, (slot + 1) % 2, stored)
                        if pair == MAX_DONE and after:
                            all_maxima(n + 1)
                        if pair == MAX_DONE + 1 and after:
                            minus_max((slot + 1) % SLOTS, n + 1)

                dve.sem_inc(s["unit_read"], 2)
                dve.sem_inc(s["lo_done"], 2)
                dve.sem_inc(s["pv_done"], SLOTS)
                nc.vector.memset(k2[DH:K_ROWS, :, :].bitcast(F32), 1.0).then_inc(s["ones_set"], 1)
                dve.wait_ge(s["const_loaded"], 16)
                read_units(0, N_UNITS, 0)
                all_maxima(0)
                minus_max(0, 0)
                dve.wait_ge(s["v_loaded"], 32)
                dve.wait_ge(s["ones_set"], 2)
                nc.vector.tensor_copy(v_hi[:], v[:]).then_inc(s["v_split"], 1)
                dve.wait_ge(s["v_split"], 1)
                nc.vector.tensor_tensor(v_lo[:], v[:], v_hi[:].bitcast(F32), ALU.subtract).then_inc(s["v_split"], 1)
                one_block(0, 0, None, True)
                for slot in range(1, SLOTS):
                    one_block(slot, slot, 16 * ((slot - 1) // 2), True)
                with dve.Fori(1, ROUNDS - 1) as j:
                    for slot in range(SLOTS):
                        one_block(j * SLOTS + slot, slot, j * (16 * SLOTS // 2) + 16 * ((slot - 1) // 2), True)
                for slot in range(SLOTS):
                    n = NB - SLOTS + slot
                    one_block(n, slot, 16 * ((n - 1) // 2), slot < SLOTS - 1)
                low_part(NB - 1, PAIRS - 1)
                output(NB - 1, 1, 16 * (NB // 2 - 1))


ORDER = [*range(DN_HEADS, KT), *range(DN_HEADS)]


def output_projection(nc, a, c, l):
    names = ("w_loaded0 w_loaded1 scaled gated y_hi y_lo w_hi w_lo proj_done psum_free squared summed "
             "xr_loaded0 xr_loaded1 x_stored0 x_stored1 small_loaded passed "
             "squares summed_dn mean root inv turned copied den_loaded den_done den_stored rows_stored "
             + " ".join(f"tile_loaded{k}" for k in range(KT)) + " "
             + " ".join(f"dn_loaded{k}" for k in range(DN_HEADS)))
    n_rows = DN_HEADS * NC
    with ExitStack() as stack, semaphores(nc, names) as s:
        b = Buffers(nc, stack, "out")
        y_hi = b.sbuf("y_hi", [P, KT, SEQ], F32R)
        y_lo = b.sbuf("y_lo", [P, KT, SEQ], F32R)
        w_raw = b.sbuf("w_raw", [P, 2, KT * P])
        w_hi = b.sbuf("w_hi", [P, 2, KT, P], F32R)
        w_lo = b.sbuf("w_lo", [P, 2, KT, P], F32R)
        norm = b.sbuf("norm", [P, 1])
        x = b.sbuf("x", [P, 3, SEQ])
        mean = b.sbuf("mean", [P, DN_HEADS, NC])
        inv = b.sbuf("inv", [P, DN_HEADS, NC])
        rows = b.sbuf("rows", [n_rows, P])
        den = b.sbuf("den", [P, P])
        den_inv = b.sbuf("den_inv", [P, P])
        acc = c.sq_acc
        squares = [acc[:], x[:, 2, :]]
        ps = b.banks()
        with nc.Block() as block:

            @block.sync
            def _(sp):
                sp.dma_start(norm[:], a.dn_norm_w[l]).then_inc(s["small_loaded"], 16)
                for h in range(ATT_HEADS):
                    sp.dma_start(den[h * NC:(h + 1) * NC, :], a.att_o[h, DH].rearrange("(c p) -> c p", p=P)) \
                        .then_inc(s["den_loaded"], 16)
                def load_gate(k):
                    sp.dma_start(y_lo[:, k, :].bitcast(F32), a.proj[T_Z + k]).then_inc(s[f"tile_loaded{k}"], 16)

                def load_denominators(k):
                    for half in range(2):
                        h = 2 * (k - DN_HEADS) + half
                        part = slice(half * DH, (half + 1) * DH)
                        sp.dma_start(y_hi[part, k, :].bitcast(F32), a.den_rows[h].partition_broadcast(DH)) \
                            .then_inc(s[f"tile_loaded{k}"], 16)

                def load_outputs(m, k):
                    for half in range(2):
                        h = 2 * (k - DN_HEADS) + half
                        sp.dma_start(x[half * DH:(half + 1) * DH, m % 3, :], a.att_o[h, 0:DH]).then_inc(s[f"tile_loaded{k}"], 16)

                load_gate(ORDER[0])
                load_outputs(0, ORDER[0])
                sp.wait_ge(s["den_done"], 1)
                sp.dma_start(a.den_rows.rearrange("h (c p) -> (h c) p", p=P), den_inv[:]).then_inc(s["den_stored"], 16)
                for u in range(2):
                    sp.dma_start(w_raw[:, u, :], a.w_out[l, u]).then_inc(s[f"w_loaded{u}"], 16)
                sp.wait_ge(s["den_stored"], 16)
                load_denominators(ORDER[0])
                for k in range(DN_HEADS):
                    sp.dma_start(y_hi[:, k, :].bitcast(F32), a.dn_o[k]).then_inc(s[f"dn_loaded{k}"], 16)
                for m, k in enumerate(ORDER[:DN_HEADS]):
                    if m >= 1:
                        load_denominators(k)
                        load_gate(k)
                    if m == 1:
                        load_outputs(m, k)
                for k in range(DN_HEADS):
                    load_gate(k)
                sp.wait_ge(s["summed_dn"], DN_HEADS)
                load_outputs(2, ORDER[2])
                sp.wait_ge(s["y_lo"], 1)
                load_outputs(3, ORDER[3])
                sp.wait_ge(s["copied"], 1)
                sp.dma_start(a.o_rows.rearrange("h (c p) -> (h c) p", p=P), rows[:]).then_inc(s["rows_stored"], 16)
                sp.wait_ge(s["rows_stored"], 16)
                for k in range(DN_HEADS):
                    m = DN_HEADS + k
                    sp.wait_ge(s["y_lo"], m - 2)
                    sp.dma_start(x[:, m % 3, :], a.o_rows[k].partition_broadcast(P)).then_inc(s[f"tile_loaded{k}"], 16)
                for u in range(2):
                    sp.wait_ge(s["w_lo"], u + 1)
                    sp.dma_start(w_raw[:, u, :], a.w_out[l, 2 + u]).then_inc(s[f"w_loaded{u}"], 16)
                sp.wait_ge(s["y_lo"], KT)
                with sp.Fori(0, KT // 2) as i:
                    for u in range(2):
                        wait_in_loop(sp, s, f"x_stored{u}", 16 * i)
                        wait_in_loop(sp, s, "squared", i * 2)
                        sp.dma_start(x[:, u, :], a.x_res[i * 2 + u]).then_inc(s[f"xr_loaded{u}"], 16)
                    for u in range(2):
                        wait_in_loop(sp, s, "psum_free", 2 * (i * 2 + u) + 6)
                        sp.dma_start(a.x_res[i * 2 + u], x[:, u, :]).then_inc(s[f"x_stored{u}"], 16)
                        wait_in_loop(sp, s, "w_lo", i * 2 + u + 3)
                        at = (i * 2 + u + 4) % KT
                        sp.dma_start(w_raw[:, u, :], a.w_out[l, at]).then_inc(s[f"w_loaded{u}"], 16)
                for u in range(2):
                    sp.wait_ge(s[f"x_stored{u}"], 16 * (KT // 2))
                    sp.wait_ge(s[f"w_loaded{u}"], 16 * (KT // 2 + 2))

            @block.tensor
            def _(pe):
                for k in range(DN_HEADS):
                    pe.wait_ge(s["squares"], k + 1)
                    for n in range(NC):
                        col = k * NC + n
                        mm = nc.tensor.matmul(ps[:, 7, col:col + 1], squares[k % 2][:, n * P:(n + 1) * P], c.ones[:, 0:1],
                                              start=True, stop=True)
                    mm.then_inc(s["summed_dn"], 1)
                pe.wait_ge(s["w_lo"], 2)
                for m, k in enumerate(ORDER):
                    pe.wait_ge(s["y_lo"], m + 1)
                    for u in range(2):
                        if m == 0 and u == 1:
                            pe.wait_ge(s["inv"], 1)
                            nc.tensor.transpose(ps[0:n_rows, 7, P:2 * P], mean[:].rearrange("p h c -> p (h c)"), c.ident[:]) \
                                .then_inc(s["turned"], 1)
                            pe.wait_ge(s["copied"], 1)
                        for w, y in ((w_hi, y_hi), (w_hi, y_lo), (w_lo, y_hi)):
                            for n in range(NQ):
                                mm = nc.tensor.matmul(ps[:, NQ * u + n, :], w[:, u, k, :], y[:, k, n * QB:(n + 1) * QB],
                                                      start=(m == 0 and w is w_hi and y is y_hi),
                                                      stop=(m == KT - 1 and w is w_lo))
                        if m == KT - 1:
                            mm.then_inc(s["proj_done"], 2)
                with pe.Fori(1, KT // 2) as i:
                    for u in range(2):
                        t = i * 2 + u
                        pe.wait_ge(s["w_lo"], t + 1)
                        for half in range(2):
                            pe.wait_ge(s["psum_free"], 2 * t + half + 1)
                            for k in range(KT):
                                for w, y in ((w_hi, y_hi), (w_hi, y_lo), (w_lo, y_hi)):
                                    for n in range(2):
                                        at = half * HALF + n * QB
                                        mm = nc.tensor.matmul(
                                            ps[:, NQ * u + 2 * half + n, :], w[:, u, k, :], y[:, k, at:at + QB],
                                            start=(k == 0 and w is w_hi and y is y_hi), stop=(k == KT - 1 and w is w_lo))
                            mm.then_inc(s["proj_done"], 1)

            @block.gpsimd
            def _(pool):
                pool.sem_inc(s["psum_free"], 4)

            @block.scalar
            def _(act):
                for k in range(DN_HEADS):
                    act.wait_ge(s[f"dn_loaded{k}"], 16)
                    if k >= 2:
                        act.wait_ge(s["summed_dn"], k - 1)
                    nc.scalar.activation(squares[k % 2], y_hi[:, k, :].bitcast(F32), ACT.Square) \
                        .then_inc(s["squares"], 1)
                for m, k in enumerate(ORDER):
                    act.wait_ge(s["gated"], m + 1)
                    nc.scalar.copy(y_hi[:, k, :], x[:, m % 3, :]).then_inc(s["y_hi"], 1)
                    if m == 0:
                        for u in range(2):
                            act.wait_ge(s[f"w_loaded{u}"], 16)
                            nc.scalar.copy(w_hi[:, u].rearrange("p k m -> p (k m)"), w_raw[:, u, :]).then_inc(s["w_hi"], 1)
                        act.wait_ge(s["mean"], 1)
                        nc.scalar.activation(inv[:], mean[:], ACT.Sqrt).then_inc(s["root"], 1)
                with act.Fori(0, KT // 2) as i:
                    for u in range(2):
                        t = i * 2 + u
                        act.wait_ge(s[f"w_loaded{u}"], 16 * i + 32)
                        act.wait_ge(s["proj_done"], 2 * t + 2)
                        nc.scalar.copy(w_hi[:, u].rearrange("p k m -> p (k m)"), w_raw[:, u, :]).then_inc(s["w_hi"], 1)
                        act.wait_ge(s["psum_free"], 2 * t + 6)
                        act.wait_ge(s["summed"], t + 1)
                        nc.scalar.activation(x[:, 2, :], x[:, u, :], ACT.Square).then_inc(s["squared"], 1)

            @block.vector
            def _(dve):
                dve.wait_ge(s["small_loaded"], 16)
                dve.wait_ge(s["den_loaded"], 16 * ATT_HEADS)
                nc.vector.reciprocal(den_inv[:], den[:]).then_inc(s["den_done"], 1)

                def split_y(m):
                    k = ORDER[m]
                    dve.wait_ge(s["y_hi"], m + 1)
                    nc.vector.tensor_tensor(y_lo[:, k, :], x[:, m % 3, :], y_hi[:, k, :].bitcast(F32),
                                            ALU.subtract).then_inc(s["y_lo"], 1)

                def split_w(u):
                    nc.vector.tensor_tensor(w_lo[:, u].rearrange("p k m -> p (k m)"), w_raw[:, u, :],
                                            w_hi[:, u].rearrange("p k m -> p (k m)").bitcast(F32),
                                            ALU.subtract).then_inc(s["w_lo"], 1)

                for m, k in enumerate(ORDER):
                    xs = x[:, m % 3, :]
                    dve.wait_ge(s[f"tile_loaded{k}"], 32 if k < DN_HEADS else 80)
                    if k < DN_HEADS:
                        nc.vector.scalar_tensor_tensor(out=xs, in0=xs, scalar=norm[:, 0:1], in1=y_hi[:, k, :].bitcast(F32),
                                                       op0=ALU.mult, op1=ALU.mult).then_inc(s["scaled"], 1)
                    else:
                        nc.vector.tensor_tensor(xs, xs, y_hi[:, k, :].bitcast(F32), ALU.mult).then_inc(s["scaled"], 1)
                    dve.wait_ge(s["scaled"], m + 1)
                    nc.vector.tensor_tensor(xs, xs, y_lo[:, k, :].bitcast(F32), ALU.mult).then_inc(s["gated"], 1)
                    if m > 1:
                        split_y(m - 1)
                    if m == 0:
                        split_y(0)
                        for u in range(2):
                            dve.wait_ge(s["w_hi"], u + 1)
                            split_w(u)
                        dve.wait_ge(s["summed_dn"], DN_HEADS)
                        nc.vector.scalar_tensor_tensor(out=mean[:].rearrange("p h c -> p (h c)"), in0=ps[:, 7, 0:n_rows],
                                                       scalar=1.0 / DN_D, in1=c.q_eps[:].rearrange("p h c -> p (h c)"),
                                                       op0=ALU.mult, op1=ALU.add).then_inc(s["mean"], 1)
                        dve.wait_ge(s["root"], 1)
                        nc.vector.reciprocal(mean[:], inv[:]).then_inc(s["inv"], 1)
                        dve.wait_ge(s["turned"], 1)
                        nc.vector.tensor_copy(rows[:], ps[0:n_rows, 7, P:2 * P]).then_inc(s["copied"], 1)
                split_y(KT - 1)
                dve.wait_ge(s["y_lo"], KT)
                nc.vector.memset(acc[:], 0.0).then_inc(s["summed"], 1)
                with dve.Fori(0, KT // 2) as i:
                    for u in range(2):
                        t = i * 2 + u
                        dve.wait_ge(s[f"xr_loaded{u}"], 16 * i + 16)
                        for half in range(2):
                            dve.wait_ge(s["proj_done"], 2 * t + half + 1)
                            xs = x[:, u, half * HALF:(half + 1) * HALF]
                            nc.vector.tensor_tensor(xs, ps[:, NQ * u + 2 * half:NQ * u + 2 * half + 2, :]
                                                    .rearrange("p b n -> p (b n)"), xs,
                                                    ALU.add).then_inc(s["psum_free"], 1)
                        dve.wait_ge(s["w_hi"], t + 3)
                        split_w(u)
                        dve.wait_ge(s["squared"], t + 1)
                        dve.wait_ge(s["summed"], t + 1)
                        nc.vector.tensor_tensor(acc[:], acc[:], x[:, 2, :], ALU.add).then_inc(s["summed"], 1)


def finish(nc, a, c):
    with ExitStack() as stack, semaphores(nc, "const_loaded x_loaded0 x_loaded1 normed stored0 stored1 passed") as s:
        b = Buffers(nc, stack, "fin")
        x = b.sbuf("x", [P, 2, SEQ])
        r = b.sbuf("r", [P, SEQ])
        w = b.sbuf("w", [P, KT])
        with nc.Block() as block:

            @block.sync
            def _(sp):
                sp.dma_start(w[:], a.norm_w[DEPTH]).then_inc(s["const_loaded"], 16)
                sp.dma_start(r[:], a.x_scale.partition_broadcast(P)).then_inc(s["const_loaded"], 16)
                for k in range(KT):
                    if k >= 2:
                        sp.wait_ge(s[f"stored{k % 2}"], 16 * (k // 2))
                    sp.dma_start(x[:, k % 2, :], a.x_res[k]).then_inc(s[f"x_loaded{k % 2}"], 16)

            @block.vector
            def _(dve):
                dve.wait_ge(s["const_loaded"], 32)
                for k in range(KT):
                    dve.wait_ge(s[f"x_loaded{k % 2}"], 16 * (k // 2 + 1))
                    nc.vector.scalar_tensor_tensor(out=x[:, k % 2, :], in0=x[:, k % 2, :], scalar=w[:, k:k + 1],
                                                   in1=r[:], op0=ALU.mult, op1=ALU.mult).then_inc(s["normed"], 1)

            @block.scalar
            def _(act):
                for k in range(KT):
                    act.wait_ge(s["normed"], k + 1)
                    act.dma_start(a.out[k], x[:, k % 2, :]).then_inc(s[f"stored{k % 2}"], 16)
                for u in range(2):
                    act.wait_ge(s[f"stored{u}"], 16 * (KT // 2))


class Arrays:
    pass


def constants():
    f = np.float32
    i = np.arange(P)
    j, t = i[:, None], i[None, :]
    masks = np.zeros((P, N_DIR, LEVELS + 1, P), f)
    for lv in range(LEVELS):
        s = 1 << lv
        upper = (j // (2 * s) == t // (2 * s)) & (j // s < t // s)
        masks[:, 0, lv] = upper
        masks[:, 1, lv] = upper.T
    masks[:, 0, LEVELS] = j <= t
    masks[:, 1, LEVELS] = j >= t
    masks[:, :, 0] *= -1
    ind = np.zeros((P, 2), f)
    ind[:DH, 0] = 1
    ind[DH:, 1] = 1
    half = DH // 2
    inv = (f(10000.0) ** (-np.arange(0, half, 2, dtype=f) / f(half))).astype(f)
    tok = np.arange(SEQ)
    ang = np.zeros((P, SEQ), f)
    sign = np.zeros((P, 1))
    for p in range(P):
        d = p % DH
        pos = (tok // DH if d < half else tok % DH).astype(f)
        ang[p] = pos * inv[d % (half // 2)]
        sign[p] = -1 if d % half < half // 2 else 1
    cos = np.cos(ang.astype(np.float64)).astype(f)
    sin = (sign * np.sin(ang.astype(np.float64))).astype(f)
    quarter = np.zeros((NQ, NQ, 1), f)
    quarter[np.arange(NQ), np.arange(NQ)] = -1
    partner = (i // (DH // 4) ^ 1) * (DH // 4) + i % (DH // 4)
    return {"swap": np.eye(P, dtype=f)[partner], "halves_t": np.ascontiguousarray(ind.T), "masks": masks,
            "ident": np.eye(P, dtype=f), "ones": np.ones((P, P), f), "halves": ind,
            "rope": np.stack([cos, sin]), "quarter": np.ascontiguousarray(np.broadcast_to(quarter, (NQ, NQ, P)))}


def build(nc, a):
    c = Arrays()
    dram = lambda n, shape, dt=F32: nc.dram_tensor(n, shape, dt, kind="Internal").ap()
    a.x_res = dram("x_res", (KT, P, SEQ))
    a.x_scale = dram("x_scale", (SEQ,))
    a.ba = dram("ba", (2 * W_BA, SEQ))
    a.proj = dram("proj", (N_TILES, P, SEQ))
    scratch(a, dram)
    with ExitStack() as stack:
        sb = lambda n, shape: stack.enter_context(nc.sbuf_tensor(n, shape, F32))
        c.ident = sb("c_ident", [P, P])
        c.ones = sb("c_ones", [P, P])
        c.eps = sb("c_eps", [P, 2])
        c.halves = sb("c_halves", [P, 2])
        c.sums = sb("c_sums", [P, T_Z - T_Q, NC, 2])
        c.tok = sb("c_tok", [P, NC, TABLES, ITEMS])
        c.v_scale = sb("c_v_scale", [P, NC, DN_HEADS])
        c.q_eps = sb("c_q_eps", [P, DN_HEADS, NC])
        with semaphores(nc, "loaded set_up") as s:
            with nc.Block() as block:
                @block.sync
                def _(sp):
                    sp.dma_start(c.ident[:], a.ident).then_inc(s["loaded"], 16)
                    sp.dma_start(c.ones[:], a.ones).then_inc(s["loaded"], 16)
                    sp.dma_start(c.halves[:], a.halves).then_inc(s["loaded"], 16)
                    sp.wait_ge(s["loaded"], 48)

                @block.vector
                def _(dve):
                    nc.vector.memset(c.eps[:], EPS).then_inc(s["set_up"], 1)
        with ExitStack() as inner:
            c.sq_acc = inner.enter_context(nc.sbuf_tensor("sq_acc_in", [P, SEQ], F32))
            load_input(nc, a, c)
            token_scales(nc, a, c, "input")
        with nc.Fori(0, DEPTH) as l:
            input_projection(nc, a, c, l)
            token_inputs(nc, a, c, l)
            delta_net(nc, a, c, l)
            attention(nc, a, c, l)
            with ExitStack() as inner:
                c.sq_acc = inner.enter_context(nc.sbuf_tensor("sq_acc", [P, SEQ], F32))
                output_projection(nc, a, c, l)
                token_scales(nc, a, c, "layer")
        finish(nc, a, c)


_SHAPES = ["x_in", "w_in", "w_ba", "norm_w", "decay", "dn_norm_w", "qk_norm_w", "w_out",
           "masks", "ident", "ones", "halves", "rope", "quarter", "swap", "halves_t"]


def lay_out(x, norm_w, w_in, conv_w, a_log, dt_bias, dn_norm_w, q_norm_w, k_norm_w, w_out, final_norm_w):
    depth = w_in.shape[0]
    g = {"x_in": np.asarray(x)[0].T.reshape(KT, P, SEQ)}
    w = np.asarray(w_in)
    conv = DN_HEADS * P
    at_z = 3 * conv
    at_ba = at_z + conv
    at_q = at_ba + W_BA
    at_v = at_q + ATT_HEADS * DH + KV_HEADS * DH
    at_gate = at_v + KV_HEADS * DH
    order = np.concatenate([np.arange(2 * conv, 3 * conv), np.arange(0, 2 * conv), np.arange(at_q, at_gate),
                            np.arange(at_z, at_ba), np.arange(at_gate, w.shape[2])])
    tiles = w[:, :, order].reshape(depth, KT, P, N_TILES, P).transpose(0, 3, 2, 1, 4).reshape(depth, N_TILES, P, KT * P)
    taps = np.zeros((depth, N_TILES, P, WCOLS - KT * P), w.dtype)
    conv_order = order[:CONV_TILES * P]
    taps[:, :CONV_TILES, :, :CONV_K] = np.asarray(conv_w)[:, :, conv_order].reshape(
        depth, CONV_K, CONV_TILES, P).transpose(0, 2, 3, 1)
    g["w_in"] = np.concatenate([tiles, taps], axis=3)
    g["w_ba"] = w[:, :, at_ba:at_q].reshape(depth, KT, P, W_BA).transpose(0, 2, 1, 3)
    norms = np.concatenate([np.asarray(norm_w), np.asarray(final_norm_w)[None]])
    g["norm_w"] = norms.reshape(depth + 1, KT, P).transpose(0, 2, 1)
    g["decay"] = np.stack([np.asarray(a_log).reshape(depth, ITEMS), np.asarray(dt_bias).reshape(depth, ITEMS)], axis=1)
    g["dn_norm_w"] = np.asarray(dn_norm_w)[:, :, None]
    swap = np.arange(DH).reshape(4, DH // 4)[[1, 0, 3, 2]].reshape(-1)
    q, k = np.asarray(q_norm_w), np.asarray(k_norm_w)
    g["qk_norm_w"] = np.stack([np.concatenate([v, v], axis=1) for v in (q, q[:, swap], k, k[:, swap])], axis=2)
    g["w_out"] = np.asarray(w_out).reshape(depth, KT, P, KT, P).transpose(0, 3, 2, 1, 4).reshape(depth, KT, P, KT * P)
    g.update(constants())
    return {n: np.ascontiguousarray(v) for n, v in g.items()}


def kernel(**inputs):
    import concourse.bacc as bacc
    from concourse.bass_utils import run_bass_kernel_spmd

    nc = bacc.Bacc("TRN2", target_bir_lowering=False, num_devices=1)
    g = lay_out(**inputs)
    a, arrays = Arrays(), {}
    a_dict = a.__dict__
    for name in _SHAPES:
        arrays[f"in_{name}"] = g[name]
        a_dict[name] = nc.dram_tensor(f"in_{name}", g[name].shape, mybir.dt.from_np(g[name].dtype),
                                      kind="ExternalInput").ap()
    a.out = nc.dram_tensor("out_T", (KT, P, SEQ), F32, kind="ExternalOutput").ap()
    build(nc, a)
    r = run_bass_kernel_spmd(nc, [arrays], core_ids=[0])
    out = r.results[0]["out_T"]
    return np.ascontiguousarray(out.reshape(D_MODEL, SEQ).T)[None]
```
